# Optimizing a Trainium2 kernel written in Bass

```python
import jax, jax.numpy as jnp
from jax import lax
import numpy as np

D_MODEL = 1024
BATCH = 1
SEQ = 512
DEPTH = 2

GRID_W = 64
CTX_LEN = 256
ROPE_BASE = 10000.0
ALPHA = (2 * DEPTH) ** 0.25
BETA = (8 * DEPTH) ** -0.25
N_EVEN = (DEPTH + 1) // 2
N_ODD = DEPTH // 2
Q_BLOCK = 128
EPS = 1e-5
NEG = -1e30

H_MLA = 8
MLA_NOPE = 64
MLA_ROPE = 32
MLA_V = 64
MLA_Q_LORA = 384
MLA_KV_LORA = 256

H_RET = 4
RET_DK = 128
RET_DV = 128
RET_CHUNK = 128

AB_IN = MLA_Q_LORA + MLA_KV_LORA + MLA_ROPE + 2 * H_RET * RET_DK + 2 * H_RET * RET_DV
AB_MIX = H_MLA * MLA_V + H_RET * RET_DV

H_M = 8
M_DK = 64
M_DV = 128
M_CHUNK = 64
CONV_W = 3
M_IN = 2 * H_M * M_DK + 2 * H_M * M_DV + 4 * H_M
M_MIX = H_M * M_DV

D_FF = -(-8 * D_MODEL // (3 * 256)) * 256

kernel_name = 'hybrid_mla_retention_mlstm_dit'

def _layer_norm(x, g, b):
    xf = x.astype(jnp.float32)
    mu = jnp.mean(xf, axis=-1, keepdims=True)
    var = jnp.mean(jnp.square(xf - mu), axis=-1, keepdims=True)
    return ((xf - mu) * lax.rsqrt(var + EPS) * g + b).astype(x.dtype)

def _head_norm(x):
    xf = x.astype(jnp.float32)
    mu = jnp.mean(xf, axis=-1, keepdims=True)
    var = jnp.mean(jnp.square(xf - mu), axis=-1, keepdims=True)
    return (xf - mu) * lax.rsqrt(var + EPS)

def _rms_norm(x, g):
    xf = x.astype(jnp.float32)
    return (xf * lax.rsqrt(jnp.mean(jnp.square(xf), axis=-1, keepdims=True) + EPS) * g).astype(x.dtype)

def _modulate(x, shift, scale):
    return x * (1.0 + scale) + shift

def _swiglu(h, w_in, w_out):
    up, gate = jnp.split(h @ w_in, 2, axis=-1)
    return (jax.nn.silu(gate) * up) @ w_out

def _axial_tables(n, d):
    rows = n // GRID_W
    row = jnp.repeat(jnp.arange(rows, dtype=jnp.float32), GRID_W)
    col = jnp.tile(jnp.arange(GRID_W, dtype=jnp.float32), rows)
    da = d // 2
    inv = ROPE_BASE ** (-jnp.arange(0, da, 2, dtype=jnp.float32) / da)
    ar = row[:, None] * inv
    ac = col[:, None] * inv
    return (jnp.cos(ar), jnp.sin(ar), jnp.cos(ac), jnp.sin(ac))

def _rot_half(x, cos, sin):
    x1, x2 = jnp.split(x, 2, axis=-1)
    cos = cos[:, None, :]
    sin = sin[:, None, :]
    return jnp.concatenate([x1 * cos - x2 * sin, x1 * sin + x2 * cos], axis=-1)

def _rope_2d(x, tabs):
    cos_r, sin_r, cos_c, sin_c = tabs
    xr, xc = jnp.split(x, 2, axis=-1)
    return jnp.concatenate([_rot_half(xr, cos_r, sin_r), _rot_half(xc, cos_c, sin_c)], axis=-1).astype(x.dtype)

def _to_heads(a, n_heads):
    b, s, _ = a.shape
    return a.reshape(b, s, n_heads, -1).transpose(0, 2, 1, 3).astype(jnp.float32)

def _seq_flip(a):
    return jnp.flip(a, axis=2)

def _block_attention(q, k, v):
    b, s, h, d = q.shape
    nb = s // Q_BLOCK
    scale = d ** -0.5
    qb = q.reshape(b, nb, Q_BLOCK, h, d).transpose(1, 0, 2, 3, 4)

    def one_block(qblk):
        logits = jnp.einsum('bqhd,bkhd->bhqk', qblk, k).astype(jnp.float32) * scale
        p = jax.nn.softmax(logits, axis=-1).astype(v.dtype)
        return jnp.einsum('bhqk,bkhd->bqhd', p, v)

    o = lax.map(one_block, qb)
    return o.transpose(1, 0, 2, 3, 4).reshape(b, s, h, v.shape[-1])

def _ret_update(r, k, v, lg):
    n = k.shape[2]
    pos = jnp.arange(n, dtype=jnp.float32)
    wk = jnp.exp(lg[:, None] * (n - 1 - pos))
    return r * jnp.exp(lg * n)[None, :, None, None] + jnp.einsum('bhjd,hj,bhjv->bhdv', k, wk, v)

def _ret_scan(q, k, v, lg, r0):
    b, h, s, _ = q.shape
    nc = s // RET_CHUNK

    def chunks(a):
        return jnp.moveaxis(a.reshape((b, h, nc, RET_CHUNK) + a.shape[3:]), 2, 0)

    pos = jnp.arange(RET_CHUNK, dtype=jnp.float32)
    rel = pos[:, None] - pos[None, :]
    d_intra = jnp.where(rel >= 0, jnp.exp(lg[:, None, None] * jnp.maximum(rel, 0.0)), 0.0)
    d_q = jnp.exp(lg[:, None] * (pos + 1.0))

    def step(r, inp):
        qc, kc, vc = inp
        sc = jnp.einsum('bhid,bhjd->bhij', qc, kc) * d_intra
        o = jnp.einsum('bhij,bhjv->bhiv', sc, vc) + jnp.einsum('bhid,hi,bhdv->bhiv', qc, d_q, r)
        return _ret_update(r, kc, vc, lg), o

    r_fin, o = lax.scan(step, r0, (chunks(q), chunks(k), chunks(v)))
    return jnp.moveaxis(o, 0, 2).reshape(b, h, s, -1), r_fin

def _mlstm_update(state, k, v, li, lf):
    c_mat, n_vec, m = state
    b_cum = jnp.cumsum(lf, axis=-1)
    b_end = b_cum[..., -1]
    lw = b_end[..., None] - b_cum + li
    m_new = jnp.maximum(b_end + m, jnp.max(lw, axis=-1))
    w = jnp.exp(lw - m_new[..., None])
    carry = jnp.exp(b_end + m - m_new)
    c_new = carry[..., None, None] * c_mat + jnp.einsum('bhs,bhsd,bhsv->bhdv', w, k, v)
    n_new = carry[..., None] * n_vec + jnp.einsum('bhs,bhsd->bhd', w, k)
    return (c_new, n_new, m_new)

def _mlstm_scan(q, k, v, li, lf, state0):
    b, h, s, _ = q.shape
    nc = s // M_CHUNK

    def chunks(a):
        return jnp.moveaxis(a.reshape((b, h, nc, M_CHUNK) + a.shape[3:]), 2, 0)

    tril = jnp.tril(jnp.ones((M_CHUNK, M_CHUNK), dtype=bool))

    def step(state, inp):
        c_mat, n_vec, m = state
        qc, kc, vc, ic, fc = inp
        b_cum = jnp.cumsum(fc, axis=-1)
        logd = jnp.where(tril, b_cum[..., :, None] - b_cum[..., None, :] + ic[..., None, :], NEG)
        inter = b_cum + m[..., None]
        m_t = jnp.maximum(inter, jnp.max(logd, axis=-1))
        sc = jnp.einsum('bhtd,bhsd->bhts', qc, kc) * jnp.exp(logd - m_t[..., None])
        w_inter = jnp.exp(inter - m_t)
        num = jnp.einsum('bhts,bhsv->bhtv', sc, vc) + w_inter[..., None] * jnp.einsum('bhtd,bhdv->bhtv', qc, c_mat)
        den = jnp.sum(sc, axis=-1) + w_inter * jnp.einsum('bhtd,bhd->bht', qc, n_vec)
        h_t = num / jnp.maximum(jnp.abs(den), jnp.exp(-m_t))[..., None]
        return _mlstm_update(state, kc, vc, ic, fc), h_t

    st, hs = lax.scan(step, state0, (chunks(q), chunks(k), chunks(v), chunks(li), chunks(lf)))
    return jnp.moveaxis(hs, 0, 2).reshape(b, h, s, -1), st

def _centred_conv(x, w, bias):
    ch = x.shape[-1]
    y = lax.conv_general_dilated(x, w[:, None, :], window_strides=(1,), padding='SAME',
                                 dimension_numbers=('NWC', 'WIO', 'NWC'), feature_group_count=ch)
    return y + bias

def _ab_project(h, w_in, q_norm, w_uq, kv_norm, w_ukv, tabs_mla, tabs_ret):
    b, s, _ = h.shape
    o1 = MLA_Q_LORA
    o2 = o1 + MLA_KV_LORA
    o3 = o2 + MLA_ROPE
    o4 = o3 + H_RET * RET_DK
    o5 = o4 + H_RET * RET_DK
    o6 = o5 + H_RET * RET_DV
    cq, ckv, kr, rq, rk, rv, rg = jnp.split(h @ w_in, [o1, o2, o3, o4, o5, o6], axis=-1)
    q = (_rms_norm(cq, q_norm) @ w_uq).reshape(b, s, H_MLA, MLA_NOPE + MLA_ROPE)
    kv = (_rms_norm(ckv, kv_norm) @ w_ukv).reshape(b, s, H_MLA, MLA_NOPE + MLA_V)
    q_nope, q_rope = jnp.split(q, [MLA_NOPE], axis=-1)
    k_nope, v = jnp.split(kv, [MLA_NOPE], axis=-1)
    k_rope = kr[:, :, None, :]
    rq = rq.reshape(b, s, H_RET, RET_DK)
    rk = rk.reshape(b, s, H_RET, RET_DK)
    if tabs_mla is not None:
        q_rope = _rope_2d(q_rope, tabs_mla)
        k_rope = _rope_2d(k_rope, tabs_mla)
        rq = _rope_2d(rq, tabs_ret)
        rk = _rope_2d(rk, tabs_ret)
    q = jnp.concatenate([q_nope, q_rope], axis=-1)
    k = jnp.concatenate([k_nope, jnp.broadcast_to(k_rope, (b, s, H_MLA, MLA_ROPE))], axis=-1)
    rq = rq.transpose(0, 2, 1, 3).astype(jnp.float32)
    rk = rk.transpose(0, 2, 1, 3).astype(jnp.float32) * RET_DK ** -0.5
    rv = _to_heads(rv, H_RET)
    return (q, k, v), (rq, rk, rv), rg

def _ab_merge(att, ret, rg, w_out):
    b, s = att.shape[:2]
    ret = _head_norm(ret.transpose(0, 2, 1, 3)).reshape(b, s, -1)
    ret = (jax.nn.silu(rg.astype(jnp.float32)) * ret).astype(rg.dtype)
    return jnp.concatenate([att.reshape(b, s, -1), ret], axis=-1) @ w_out

def _attn_ret_mixer(h_lat, h_ctx, w_in, q_norm, w_uq, kv_norm, w_ukv, log_decay, w_out,
                    tabs_mla, tabs_ret, need_ctx_out):
    (ql, kl, vl), (rql, rkl, rvl), rgl = _ab_project(h_lat, w_in, q_norm, w_uq, kv_norm, w_ukv, tabs_mla, tabs_ret)
    (qc, kc, vc), (rqc, rkc, rvc), rgc = _ab_project(h_ctx, w_in, q_norm, w_uq, kv_norm, w_ukv, None, None)
    lg_f = log_decay[0].astype(jnp.float32)
    lg_b = log_decay[1].astype(jnp.float32)
    r0 = jnp.zeros((h_lat.shape[0], H_RET, RET_DK, RET_DV), jnp.float32)
    fl = _seq_flip
    if need_ctx_out:
        ret_cf, r_f = _ret_scan(rqc, rkc, rvc, lg_f, r0)
        ret_cb, r_b = _ret_scan(fl(rqc), fl(rkc), fl(rvc), lg_b, r0)
        att_c = _block_attention(qc, kc, vc)
        y_ctx = _ab_merge(att_c, ret_cf + fl(ret_cb), rgc, w_out)
    else:
        r_f = _ret_update(r0, rkc, rvc, lg_f)
        r_b = _ret_update(r0, fl(rkc), fl(rvc), lg_b)
        y_ctx = None
    att_l = _block_attention(ql, jnp.concatenate([kl, kc], axis=1), jnp.concatenate([vl, vc], axis=1))
    ret_lf, _ = _ret_scan(rql, rkl, rvl, lg_f, r_f)
    ret_lb, _ = _ret_scan(fl(rql), fl(rkl), fl(rvl), lg_b, r_b)
    y_lat = _ab_merge(att_l, ret_lf + fl(ret_lb), rgl, w_out)
    return y_lat, y_ctx

def _mlstm_project(h, w_in, conv_w, conv_b, gate_b):
    b, s, _ = h.shape
    o1 = 2 * H_M * M_DK
    o2 = o1 + H_M * M_DV
    o3 = o2 + H_M * M_DV
    qk, v, og, g = jnp.split(h @ w_in, [o1, o2, o3], axis=-1)
    qk = jax.nn.silu(_centred_conv(qk, conv_w, conv_b))
    q, k = jnp.split(qk, 2, axis=-1)
    q = _to_heads(q, H_M)
    k = _to_heads(k, H_M) * M_DK ** -0.5
    v = _to_heads(v, H_M)
    g = (g.reshape(b, s, 4, H_M) + gate_b).astype(jnp.float32).transpose(2, 0, 3, 1)
    fwd = (g[0], jax.nn.log_sigmoid(g[1]))
    bwd = (g[2], jax.nn.log_sigmoid(g[3]))
    return q, k, v, og, fwd, bwd

def _mlstm_merge(h_sum, og, norm_g, w_out):
    b, s = og.shape[:2]
    hn = _head_norm(h_sum.transpose(0, 2, 1, 3)).reshape(b, s, -1) * norm_g
    return (jax.nn.sigmoid(og.astype(jnp.float32)) * hn).astype(og.dtype) @ w_out

def _mlstm_mixer(h_lat, h_ctx, w_in, conv_w, conv_b, gate_b, norm_g, w_out, need_ctx_out):
    ql, kl, vl, ogl, gfl, gbl = _mlstm_project(h_lat, w_in, conv_w, conv_b, gate_b)
    qc, kc, vc, ogc, gfc, gbc = _mlstm_project(h_ctx, w_in, conv_w, conv_b, gate_b)
    b = h_lat.shape[0]
    zero = (jnp.zeros((b, H_M, M_DK, M_DV), jnp.float32), jnp.zeros((b, H_M, M_DK), jnp.float32),
            jnp.zeros((b, H_M), jnp.float32))
    fl = _seq_flip
    if need_ctx_out:
        hcf, st_f = _mlstm_scan(qc, kc, vc, gfc[0], gfc[1], zero)
        hcb, st_b = _mlstm_scan(fl(qc), fl(kc), fl(vc), fl(gbc[0]), fl(gbc[1]), zero)
        y_ctx = _mlstm_merge(hcf + fl(hcb), ogc, norm_g, w_out)
    else:
        st_f = _mlstm_update(zero, kc, vc, gfc[0], gfc[1])
        st_b = _mlstm_update(zero, fl(kc), fl(vc), fl(gbc[0]), fl(gbc[1]))
        y_ctx = None
    hlf, _ = _mlstm_scan(ql, kl, vl, gfl[0], gfl[1], st_f)
    hlb, _ = _mlstm_scan(fl(ql), fl(kl), fl(vl), fl(gbl[0]), fl(gbl[1]), st_b)
    y_lat = _mlstm_merge(hlf + fl(hlb), ogl, norm_g, w_out)
    return y_lat, y_ctx

def setup_inputs(seed: int = 0) -> dict:
    key = jax.random.key(seed)
    ks = jax.random.split(key, 24)
    f32 = jnp.float32
    D = D_MODEL

    def nrm(k, shape, s):
        return s * jax.random.normal(k, shape, f32)

    ret_base = jnp.log1p(-(2.0 ** (-5.0 - jnp.arange(H_RET, dtype=f32))))
    f_lin = jnp.linspace(3.0, 6.0, H_M, dtype=f32)
    zeros_h = jnp.zeros((H_M,), f32)
    gate_base = jnp.stack([zeros_h, f_lin, zeros_h, f_lin])
    return {
        'x': nrm(ks[0], (BATCH, SEQ, D), 1.0),
        'c': nrm(ks[1], (BATCH, D), 1.0),
        'ctx': nrm(ks[2], (BATCH, CTX_LEN, D), 1.0),
        'c_ctx': nrm(ks[3], (D,), 1.0),
        'mod_w': nrm(ks[4], (DEPTH, D, 6 * D), 0.5 * D ** -0.5),
        'mod_b': nrm(ks[5], (DEPTH, 6 * D), 0.02),
        'ln_g': 1.0 + nrm(ks[6], (DEPTH, 2, D), 0.02),
        'ln_b': nrm(ks[7], (DEPTH, 2, D), 0.02),
        'ffn_w_in': nrm(ks[8], (DEPTH, D, 2 * D_FF), D ** -0.5),
        'ffn_w_out': nrm(ks[9], (DEPTH, D_FF, D), BETA * D_FF ** -0.5),
        'ab_w_in': nrm(ks[10], (N_EVEN, D, AB_IN), D ** -0.5),
        'mla_q_norm': 1.0 + nrm(ks[11], (N_EVEN, MLA_Q_LORA), 0.02),
        'mla_w_uq': nrm(ks[12], (N_EVEN, MLA_Q_LORA, H_MLA * (MLA_NOPE + MLA_ROPE)), MLA_Q_LORA ** -0.5),
        'mla_kv_norm': 1.0 + nrm(ks[13], (N_EVEN, MLA_KV_LORA), 0.02),
        'mla_w_ukv': nrm(ks[14], (N_EVEN, MLA_KV_LORA, H_MLA * (MLA_NOPE + MLA_V)), MLA_KV_LORA ** -0.5),
        'ret_log_decay': ret_base * (1.0 + nrm(ks[15], (N_EVEN, 2, H_RET), 0.05)),
        'ab_w_out': nrm(ks[16], (N_EVEN, AB_MIX, D), BETA * AB_MIX ** -0.5),
        'm_w_in': nrm(ks[17], (N_ODD, D, M_IN), D ** -0.5),
        'm_conv_w': nrm(ks[18], (N_ODD, CONV_W, 2 * H_M * M_DK), CONV_W ** -0.5),
        'm_conv_b': nrm(ks[19], (N_ODD, 2 * H_M * M_DK), 0.02),
        'm_gate_b': gate_base[None] + nrm(ks[20], (N_ODD, 4, H_M), 0.1),
        'm_norm_g': 1.0 + nrm(ks[21], (N_ODD, M_MIX), 0.02),
        'm_w_out': nrm(ks[22], (N_ODD, M_MIX, D), BETA * M_MIX ** -0.5),
    }

def reference(x, c, ctx, c_ctx, mod_w, mod_b, ln_g, ln_b, ffn_w_in, ffn_w_out,
              ab_w_in, mla_q_norm, mla_w_uq, mla_kv_norm, mla_w_ukv, ret_log_decay, ab_w_out,
              m_w_in, m_conv_w, m_conv_b, m_gate_b, m_norm_g, m_w_out):
    n_lat = x.shape[1]
    tabs_mla = _axial_tables(n_lat, MLA_ROPE)
    tabs_ret = _axial_tables(n_lat, RET_DK)
    sc = jax.nn.silu(c)
    sc_ctx = jax.nn.silu(c_ctx)
    for l in range(DEPTH):
        last = l == DEPTH - 1
        ml = [m[:, None, :] for m in jnp.split(sc @ mod_w[l] + mod_b[l], 6, axis=-1)]
        mc = jnp.split(sc_ctx @ mod_w[l] + mod_b[l], 6, axis=-1)
        h_lat = _modulate(x, ml[0], ml[1])
        h_ctx = _modulate(ctx, mc[0], mc[1])
        j = l // 2
        if l % 2 == 0:
            y_lat, y_ctx = _attn_ret_mixer(h_lat, h_ctx, ab_w_in[j], mla_q_norm[j], mla_w_uq[j], mla_kv_norm[j],
                                           mla_w_ukv[j], ret_log_decay[j], ab_w_out[j], tabs_mla, tabs_ret,
                                           not last)
        else:
            y_lat, y_ctx = _mlstm_mixer(h_lat, h_ctx, m_w_in[j], m_conv_w[j], m_conv_b[j], m_gate_b[j],
                                        m_norm_g[j], m_w_out[j], not last)
        x = _layer_norm(ALPHA * x + ml[2] * y_lat, ln_g[l, 0], ln_b[l, 0])
        x = _layer_norm(ALPHA * x + ml[5] * _swiglu(_modulate(x, ml[3], ml[4]), ffn_w_in[l], ffn_w_out[l]),
                        ln_g[l, 1], ln_b[l, 1])
        if not last:
            ctx = _layer_norm(ALPHA * ctx + mc[2] * y_ctx, ln_g[l, 0], ln_b[l, 0])
            ctx = _layer_norm(ALPHA * ctx + mc[5] * _swiglu(_modulate(ctx, mc[3], mc[4]), ffn_w_in[l], ffn_w_out[l]),
                              ln_g[l, 1], ln_b[l, 1])
    return x


_drawn_inputs = setup_inputs


def setup_inputs(seed=0):
    import zlib

    import numpy as np

    out = dict(_drawn_inputs(seed))
    spreads = {}
    factors = {'ctx': 3.534,
     'c_ctx': 2.898,
     'mod_b': 4.931,
     'mla_q_norm': 8.0,
     'mla_w_uq': 8.0,
     'mla_kv_norm': 8.0,
     'mla_w_ukv': 3.29,
     'ret_log_decay': 3.245,
     'm_conv_b': 8.0,
     'm_norm_g': 8.0}
    for name, (base, spread) in spreads.items():
        noise = np.random.default_rng([zlib.crc32(name.encode()), seed]).standard_normal(out[name].shape)
        drawn = base * np.exp(spread * noise) if base else spread * noise
        out[name] = __import__('jax').numpy.asarray(drawn.astype(out[name].dtype))
    for name, factor in factors.items():
        out[name] = (out[name] * factor).astype(out[name].dtype)
    return out
```

```python
from contextlib import ExitStack

import numpy as np

import concourse.bass as bass
from concourse import mybir

F32 = mybir.dt.float32
F32R = mybir.dt.float32r
ALU = mybir.AluOpType
ACT = mybir.ActivationFunctionType
AX = mybir.AxisListType

P = 128
D = 1024
KD = D // P
LAT, CTX = 512, 256
T = LAT + CTX
TT = T // P
LT = LAT // P
GRID_W = 64
ROPE_BASE = 10000.0
DEPTH = 2
ALPHA = (2 * DEPTH) ** 0.25
EPS = 1e-5

H_MLA, NOPE, ROPE, MLA_V = 8, 64, 32, 64
DQ = NOPE + ROPE
Q_LORA, KV_LORA = 384, 256
KQ, KKV = Q_LORA // P, KV_LORA // P
H_RET, RET_D = 4, 128
H_M, M_DK, M_DV = 8, 64, 128
D_FF = -(-8 * D // (3 * 256)) * 256
FC = D_FF // P
THIRDS = ((0, 8), (8, 8), (16, FC - 16))

RING = 4
UNIT = 1024

C_KR = Q_LORA + KV_LORA
C_RQ = C_KR + ROPE
C_RK = C_RQ + H_RET * RET_D
C_RV = C_RK + H_RET * RET_D
C_RG = C_RV + H_RET * RET_D
C_MK = H_M * M_DK
C_MV = 2 * H_M * M_DK
C_MO = C_MV + H_M * M_DV
C_MG = C_MO + H_M * M_DV

V_C, V_CC, V_LG, V_LB = 0, 8, 16, 48
V_QN, V_KVN, V_CW, V_CB, V_NG = 80, 83, 85, 109, 117
V_ROWS = 125

REL_W = 896
K_ID, K_ONE, K_RR, K_RM = 0, 128, 256, 384
K_BASE = 512
K_COSR, K_SINR = 512, 1024
K_COSM, K_SINM = 1536, 2048
K_REL = 2560
K_SEL = K_REL + REL_W
K_ALL = K_SEL + H_M * P


def shape_constants():
    k = np.zeros((P, K_ALL), np.float32)
    p = np.arange(P)
    k[p, K_ID + p] = 1.0
    k[:, K_ONE:K_ONE + P] = 1.0

    def rotation(base, first, width, half):
        for b in range(first, first + width, 2 * half):
            for c in range(half):
                k[b + half + c, base + b + c] = -1.0
                k[b + c, base + b + half + c] = 1.0

    rotation(K_RR, 0, P, RET_D // 4)
    rotation(K_RM, NOPE, ROPE, ROPE // 4)
    t = np.arange(LAT)
    pos = np.stack([t // GRID_W, t % GRID_W]).astype(np.float32)

    def table(width, first, cos_at, sin_at):
        da = width // 2
        inv = (np.float32(ROPE_BASE) ** (-np.arange(0, da, 2, dtype=np.float32) / np.float32(da))).astype(np.float32)
        for i in range(width):
            a = pos[i // da] * inv[i % (da // 2)]
            k[first + i, cos_at:cos_at + LAT] = np.cos(a)
            k[first + i, sin_at:sin_at + LAT] = np.sin(a)

    table(RET_D, 0, K_COSR, K_SINR)
    table(ROPE, NOPE, K_COSM, K_SINM)
    k[:, K_REL:K_REL + REL_W] = np.arange(REL_W)[None, :] - p[:, None]
    for h in range(H_M):
        k[h, K_SEL + h * P:K_SEL + (h + 1) * P] = 1.0
    return k


def build(nc, x, c, ctx, c_ctx, mod_w, mod_b, ln_g, ln_b, ffn_w_in, ffn_w_out, ab_w_in, mla_q_norm, mla_w_uq,
          mla_kv_norm, mla_w_ukv, ret_log_decay, ab_w_out, m_w_in, m_conv_w, m_conv_b, m_gate_b, m_norm_g,
          m_w_out, consts, out):
    es = ExitStack()

    def sb(name, shape, dt=F32, at=None):
        return (at or es).enter_context(nc.sbuf_tensor(name, shape, dt))

    def sem(name):
        return es.enter_context(nc.semaphore(name))

    kc = sb("kc", [P, K_BASE])
    ident, ones = kc[:, K_ID:K_ID + P], kc[:, K_ONE:K_ONE + P]
    rot_ret, rot_mla = kc[:, K_RR:K_RR + P], kc[:, K_RM:K_RM + P]
    xT = sb("xT", [P, KD, T])
    ring = sb("ring", [P, RING, UNIT])
    vcol = sb("vcol", [P, P])
    scol = sb("scol", [P, 16])
    modb = sb("modb", [P, DEPTH * 48])
    modc = sb("modc", [P, DEPTH, 6, KD, 2])
    epsc = sb("epsc", [P, 1])
    onec = sb("onec", [P, 1])
    lnbuf = sb("lnbuf", [P, 6, T])
    lnm, lnr, s1, s2 = (lnbuf[:, i, :] for i in range(4))
    sq = lnbuf[:, 4:6, :]

    def phase():
        return ExitStack()

    ph = phase()
    xin = sb("xin", [P, TT, D], at=ph)
    vrow = sb("vrow", [P, P], at=ph)
    brow = sb("brow", [96, P], at=ph)
    ph.close()
    m0 = phase()
    hT0 = sb("hT0", [P, KD, T], at=m0)
    hT0f = hT0[:, :, :].rearrange("p k t -> p (k t)")
    W_KV = KKV * H_MLA * (NOPE + MLA_V)
    wukv = hT0f[:, 0:W_KV].rearrange("p (k n) -> p k n", k=KKV)
    va = hT0f[:, W_KV:W_KV + TT * H_MLA * MLA_V].rearrange("p (t d) -> p t d", t=TT)
    cqkv = sb("cqkv", [P, KQ + KKV, T], at=m0)
    krope = sb("krope", [P, T], at=m0)
    wuq = sb("wuq", [P, KQ, H_MLA * DQ], at=m0)
    rg = sb("rg", [P, TT, H_RET * RET_D], at=m0)
    cosM = sb("cosM", [P, 2, LAT], at=m0)
    ph = phase()
    rq = sb("rq", [P, H_RET, T], at=ph)
    rk = sb("rk", [P, H_RET, T], at=ph)
    rv = sb("rv", [P, TT, H_RET * RET_D], at=ph)
    cosR = sb("cosR", [P, 2, LAT], at=ph)
    rel = sb("rel", [P, REL_W], at=ph)
    PT_W = TT * LAT + 2 * CTX
    pt = sb("pt", [P, 2, PT_W], at=ph)
    sqb = pt[:, 0, :][:, 0:4 * T].rearrange("p (c t) -> p c t", t=T)
    sqb4 = pt[:, 1, 0:T]
    rms = pt[:, 1, T:3 * T].rearrange("p (c t) -> p c t", t=T)
    lnf = lnbuf[:, :, :].rearrange("p a t -> p (a t)")
    S2_W = LAT + P
    strip = lnf[:, 0:2 * (REL_W + S2_W)].rearrange("p (b n) -> p b n", b=2)
    stripb = lnf[:, 2 * (REL_W + S2_W):2 * (REL_W + S2_W) + REL_W]
    lgc = sb("lgc", [P, 4, 2 * H_RET], at=ph)
    rtmp = sb("rtmp", [P, LAT], at=ph)
    rst = sb("rst", [P, TT, 6], at=ph)
    rmv = sb("rmv", [P, TT, 2], at=ph)
    rrs = sb("rrs", [P, TT], at=ph)
    rnm = sb("rnm", [P, 2, RET_D], at=ph)
    ph.close()
    ph = phase()
    qh = sb("qh", [P, H_MLA, T], at=ph)
    kh = sb("kh", [P, H_MLA, T], at=ph)
    att = sb("att", [P, TT, H_MLA * MLA_V], at=ph)
    pa = sb("pa", [P, 2, T], at=ph)
    paT = sb("paT", [P, 2, T], at=ph)
    mtmp = sb("mtmp", [P, LAT], at=ph)
    NI = H_MLA * TT
    nmx = sb("nmx", [P, 2, NI], at=ph)
    den = sb("den", [P, 2, NI], at=ph)
    ph.close()
    m0.close()
    m1 = phase()
    hT1 = sb("hT1", [P, KD, T], at=m1)
    mq = sb("mq", [P, H_M // 2, LAT], at=m1)
    mk = sb("mk", [P, H_M // 2, T], at=m1)
    mv = sb("mv", [P, TT, H_M, M_DV + 1], at=m1)
    mo = sb("mo", [P, LT, H_M * M_DV], at=m1)
    selr = sb("selr", [P, H_M * P], at=m1)
    acol = sb("acol", [P, 2, TT, H_M], at=m1)
    fcol = sb("fcol", [P, 2, LT, H_M], at=m1)
    ee = sb("ee", [P, 4, LAT], at=m1)
    negm = sb("negm", [P, 2, LAT], at=m1)
    FW = 2 * LAT + sum(LAT - P * j for j in range(LT))
    ph = phase()
    wgr = sb("wgr", [P, KD, 4 * H_M], at=ph)
    wg = sb("wg", [P, KD, P], at=ph)
    gb = sb("gb", [P, 1], at=ph)
    cpad = sb("cpad", [P, 2, T + 4], at=ph)
    cacc = sb("cacc", [P, 2, T + 2], at=ph)
    li = sb("li", [P, 2, T], at=ph)
    lf = sb("lf", [P, 2, T], at=ph)
    gt = sb("gt", [P, 2, T], at=ph)
    gbc = sb("gbc", [P, 2, T], at=ph)
    ph.close()
    ph = phase()
    pp = sb("pp", [P, 2, 2, FW], at=ph)
    dab = sb("dab", [P, 2, LT, 2], at=ph)
    mst = sb("mst", [P, LT * H_M, 6], at=ph)
    mmv = sb("mmv", [P, LT * H_M, 2], at=ph)
    mrs = sb("mrs", [P, LT * H_M], at=ph)
    hf = sb("hfwd", [P, 2, M_DV], at=ph)
    ph.close()
    hb = hT1[:, :, :].rearrange("p k t -> p (k t)")[:, 0:LT * D].rearrange("p (t d) -> p t d", t=LT)
    m1.close()
    ph = phase()
    hhi = sb("hhi", [P, KD, T], F32R, at=ph)
    hlo = sb("hlo", [P, KD, T], F32R, at=ph)
    uhi = sb("uhi", [P, 8, T], F32R, at=ph)
    ulo = sb("ulo", [P, 8, T], F32R, at=ph)
    whi = sb("whi", [P, RING, UNIT], F32R, at=ph)
    wlo = sb("wlo", [P, RING, UNIT], F32R, at=ph)
    sg = sb("sg", [P, 2, T], at=ph)
    hu = sb("hu", [P, 2, T], at=ph)
    ph.close()
    ph = phase()
    orow = sb("orow", [P, LT, D], at=ph)
    ph.close()

    PS = [es.enter_context(nc.psum_tensor(f"ps{i}", [P, 1024], F32)) for i in range(4)]

    def half(i):
        return PS[i // 2][:, 512 * (i % 2):512 * (i % 2) + 512]


    N_MOD, N_IN0, N_OUT, N_FFN, N_IN1 = 6 * KD, 22, KD, sum(2 * nj + KD for _, nj in THIRDS), 24
    NB = {}
    UB = {}
    n = u = 0
    for stage, count, direct in (("mod0", N_MOD, 1), ("in0", N_IN0, 1), ("out0", N_OUT, 1), ("mod1", N_MOD, 1),
                                 ("ffn0", N_FFN, 0), ("in1", N_IN1, 1), ("out1", N_OUT, 1), ("ffn1", N_FFN, 0)):
        NB[stage], UB[stage] = n, u
        n += count
        u += count if direct else 0
    FB = (0, N_FFN)
    JB = (0, FC)
    ZB = (0, KD + 3 * KD)
    NT = (T, LAT)
    SEGS = (((0, LAT, 0), (LAT, T, 1)), ((0, LAT, 0),))
    ALL_SEGS = SEGS[0]
    MOD_CREDIT = 2
    H_CREDIT = 2
    TILE_CREDIT = 2

    def view(slot, k):
        return ring[:, slot, :].rearrange("p (k n) -> p k n", k=k)

    landed = [sem(f"landed{i}") for i in range(RING)]
    consts_in, tabs_in, x_in, wq_in, wkv_in, gate_in = (sem(s) for s in ("consts_in", "tabs_in", "x_in", "wq_in", "wkv_in", "gate_in"))
    unit_done = sem("unit_done")
    vec_T, vec_ev, scol_ok, xT_mm, xT_ev = (sem(s) for s in ("vec_T", "vec_ev", "scol_ok", "xT_mm", "xT_ev"))
    mod_ev = sem("mod_ev")
    hmod, xa_done, fh_hi, fh_lo = (sem(s) for s in ("hmod", "xa_done", "fh_hi", "fh_lo"))
    ip_ev, sq_made, rms_mm, rms_ln, rms_ready, cq_norm = (sem(s) for s in ("ip_ev", "sq_made", "rms_mm", "rms_ln", "rms_ready", "cq_norm"))
    rope_mm, rope_ev, rope_done, rg_ready = (sem(s) for s in ("rope_mm", "rope_ev", "rope_done", "rg_ready"))
    strip_in, strip_exp = sem("strip_in"), sem("strip_exp")
    ret_s, ret_p, ret_o, ret_var, ret_rstd, ret_nrm = (sem(s) for s in ("ret_s", "ret_p", "ret_o", "ret_var", "ret_rstd", "ret_nrm"))
    mp_mm, mp_ev, mrope_mm, mrope_ev, mrope_done, kr_cp = (sem(s) for s in ("mp_mm", "mp_ev", "mrope_mm", "mrope_ev", "mrope_done", "kr_cp"))
    att_s, att_nmx, att_exp, att_t, att_tA, att_tB, att_o, att_n = (sem(s) for s in ("att_s", "att_nmx", "att_exp", "att_t", "att_tA", "att_tB", "att_o", "att_n"))
    oT_mm, oT_ev, z_ev = sem("oT_mm"), sem("oT_ev"), sem("z_ev")
    ln_sq, ln_sum1, ln_sum2, ln_mm, ln_mean, ln_var, ln_rstd, ln_norm, x_new = (sem(s) for s in ("ln_sq", "ln_sum1", "ln_sum2", "ln_mm", "ln_mean", "ln_var", "ln_rstd", "ln_norm", "x_new"))
    hi_made, lo_made, ffn_tile, silu_done, h_done, uhi_done, ulo_done = (sem(s) for s in ("hi_made", "lo_made", "ffn_tile", "silu_done", "h_done", "uhi_done", "ulo_done"))
    gate_w, gate_mm, gate_ev, f_ev, conv_done, silu_ev, vg_ev, pad_ok = (sem(s) for s in ("gate_w", "gate_mm", "gate_ev", "f_ev", "conv_done", "silu_ev", "vg_ev", "pad_ok"))
    ls_in, ls_ln, rows_ok, floor_in, floor_ok, tr_mm, tr_ev = (sem(s) for s in ("ls_in", "ls_ln", "rows_ok", "floor_in", "floor_ok", "tr_mm", "tr_ev"))
    nm_mm, ms_mm, mexp, msel, mp_done, mo_mm, mh_ev, mvar, mrstd, mn_done = (sem(s) for s in ("nm_mm", "ms_mm", "mexp", "msel", "mp_done", "mo_mm", "mh_ev", "mvar", "mrstd", "mn_done"))
    eps_ok, ones_ok = sem("eps_ok"), sem("ones_ok")
    out_mm, out_ev, out_st = sem("out_mm"), sem("out_ev"), sem("out_st")
    dve_step, act_step, pool_step = sem("dve_step"), sem("act_step"), sem("pool_step")

    F_COLS = [0, P, 2 * P, 3 * P, 4 * P, C_KR] + [C_RQ + P * i for i in range(4)] + [C_RK + P * i for i in range(4)]
    NF = len(F_COLS)
    RET_TILES = [(j, 0) for j in range(TT)] + [(j, 1) for j in range(LT, TT)]

    def ret_off(j, seg):
        return j * LAT if seg == 0 else TT * LAT + (j - LT) * CTX

    def m_range(j, d):
        if j >= LT:
            return 0, LAT
        return (P * j, LAT) if d == 0 else (0, P * (j + 1))

    M_OFF = [[], []]
    for d in range(2):
        at = 0
        for j in range(TT):
            M_OFF[d].append(at)
            at += m_range(j, d)[1] - m_range(j, d)[0]
    assert at == FW
    M_SCALE, R_SCALE, A_SCALE = M_DK ** -0.5, RET_D ** -0.5, DQ ** -0.5
    N_ATT = H_MLA * TT

    def lat_items(it):
        return (it // TT) * LT + min(it % TT + 1, LT)

    block = es.enter_context(nc.Block())

    @block.sync
    def _(sp):
        def unit(n, dst, src):
            sp.dma_start(dst, src).then_inc(landed[n % RING], 16)

        def mod_unit(l, g, k, n_static):
            src = mod_w[l, k * P:(k + 1) * P, :]
            cols = bass.ds(g * D, D) if not isinstance(g, int) else slice(g * D, (g + 1) * D)
            unit(n_static, ring[:, n_static % RING, :], src[:, cols])

        for k in range(KD):
            if k >= RING:
                sp.wait_ge(unit_done, k - RING + 1)
            mod_unit(0, 0, k, k)
        with sp.Fori(1, 6) as g:
            for k in range(KD):
                sp.wait_ge(unit_done, g * KD + (k - RING + 1))
                mod_unit(0, g, k, k)
        w_in = ab_w_in[0].rearrange("(k p) n -> p k n", p=P)
        for f, c0 in enumerate(F_COLS):
            n, w = NB["in0"] + f, ROPE if c0 == C_KR else P
            sp.wait_ge(unit_done, n - RING + 1)
            unit(n, view(n % RING, KD)[:, :, 0:w], w_in[:, :, c0:c0 + w])
        for i in range(8):
            n, c0 = NB["in0"] + NF + i, (C_RV, C_RG)[i // 4]
            sp.wait_ge(unit_done, n - RING + 1)
            unit(n, view(n % RING, 2), w_in[:, 2 * (i % 4):2 * (i % 4) + 2, c0:c0 + 512])
        sp.wait_ge(unit_done, UB["out0"])
        sp.dma_start(wukv, mla_w_ukv[0].rearrange("(k p) n -> p k n", p=P)).then_inc(wkv_in, 16)
        w_out = ab_w_out[0].rearrange("(k p) n -> p k n", p=P)
        for m in range(KD):
            n = NB["out0"] + m
            sp.wait_ge(unit_done, n - RING + 1)
            unit(n, view(n % RING, KD), w_out[:, :, m * P:(m + 1) * P])
        with sp.Fori(0, 6) as g:
            for k in range(KD):
                sp.wait_ge(unit_done, g * KD + (NB["mod1"] + k - RING + 1))
                mod_unit(1, g, k, NB["mod1"] + k)

        def ffn_units(l):
            first = NB[f"ffn{l}"]
            w_up = ffn_w_in[l].rearrange("(k p) n -> p k n", p=P)
            w_dn = ffn_w_out[l].rearrange("(k p) n -> p k n", p=P)

            def in_four(j0, it):
                for s in range(4):
                    c0 = (it * 2 + (j0 + s // 2)) * P + (s % 2) * D_FF
                    cols = slice(c0, c0 + P) if isinstance(it, int) else bass.ds(c0, P)
                    n = (first + s) % RING
                    unit(n, view(n, KD), w_up[:, :, cols])

            U = FB[l]
            for third, (j0, nj) in enumerate(THIRDS):
                start = 0
                if third == 0:
                    for s in range(4):
                        sp.wait_ge(unit_done, UB[f"in1"] - RING + 1 + s if l == 0 else UB["out1"] + KD - RING + 1 + s)
                        c0 = (j0 + s // 2) * P + (s % 2) * D_FF
                        n = (first + s) % RING
                        unit(n, view(n, KD), w_up[:, :, c0:c0 + P])
                    start = 1
                with sp.Fori(start, nj // 2) as it:
                    for s in range(4):
                        sp.wait_ge(lo_made, it * 4 + (U + s - RING + 1))
                        n = (first + s) % RING
                        unit(n, view(n, KD), w_up[:, :, bass.ds(it * (2 * P) + ((j0 + s // 2) * P + (s % 2) * D_FF), P)])
                U += 2 * nj
                with sp.Fori(0, 2) as it:
                    for s in range(4):
                        sp.wait_ge(lo_made, it * 4 + (U + s - RING + 1))
                        n = (first + s) % RING
                        dst = ring[:, n, 0:nj * P].rearrange("p (k n) -> p k n", k=nj)
                        unit(n, dst, w_dn[:, j0:j0 + nj, bass.ds(it * (4 * P) + s * P, P)])
                U += KD

        ffn_units(0)
        w_in = m_w_in[0].rearrange("(k p) n -> p k n", p=P)
        for i in range(N_IN1):
            n = NB["in1"] + i
            if i < RING:
                sp.wait_ge(lo_made, FB[1] - RING + 1 + i)
            else:
                sp.wait_ge(unit_done, UB["in1"] + i - RING + 1)
            if i < 8:
                unit(n, view(n % RING, KD), w_in[:, :, i * P:(i + 1) * P])
            else:
                g, q = (i - 8) // 4, (i - 8) % 4
                unit(n, view(n % RING, 2), w_in[:, 2 * q:2 * q + 2, C_MV + g * 512:C_MV + (g + 1) * 512])
        w_out = m_w_out[0].rearrange("(k p) n -> p k n", p=P)
        for m in range(KD):
            n = NB["out1"] + m
            sp.wait_ge(unit_done, UB["out1"] + m - RING + 1)
            unit(n, view(n % RING, KD), w_out[:, :, m * P:(m + 1) * P])
        ffn_units(1)
        for t in range(LT):
            sp.wait_ge(out_ev, t + 1)
            sp.dma_start(out[0, t * P:(t + 1) * P, :], orow[:, t, :]).then_inc(out_st, 16)
        sp.wait_ge(out_st, 16 * LT)

    @block.tensor
    def _(pe):
        pe.sem_inc(ffn_tile, TILE_CREDIT)

        def loaded(n):
            pe.wait_ge(landed[n % RING], 16 * (n // RING + 1))

        pe.wait_ge(consts_in, 16 * 13)
        pe.transpose(half(0)[:, 0:96], brow[0:96, :], ident[0:96, 0:96])
        pe.transpose(half(1)[:, 0:V_ROWS], vrow[0:V_ROWS, :], ident[0:V_ROWS, 0:V_ROWS]).then_inc(vec_T, 1)
        pe.wait_ge(x_in, 16 * 2)
        for k in range(KD):
            b = 1 + k % 2
            if k >= 2:
                pe.wait_ge(xT_ev, k - 1)
            for t in range(TT):
                mm = pe.transpose(PS[b][:, t * P:(t + 1) * P], xin[:, t, k * P:(k + 1) * P], ident)
            mm.then_inc(xT_mm, 1)

        s_kv = scol[:, :].rearrange("p (v k) -> p k v", v=2)

        def modulation(l):
            n0, u0 = NB[f"mod{l}"], UB[f"mod{l}"]
            if l == 0:
                pe.wait_ge(scol_ok, 1)
            with pe.Fori(0, 3) as gp:
                for g2 in range(2):
                    bank = half(6 + g2)
                    pe.wait_ge(mod_ev, gp * 2 + (6 * l + g2 - 1 + MOD_CREDIT))
                    for k in range(KD):
                        s = g2 * KD + k
                        pe.wait_ge(landed[(n0 + s) % RING], gp * (16 * 4) + 16 * ((n0 + s) // RING + 1))
                        for b in range(KD):
                            mm = pe.matmul(bank[:, 2 * b:2 * b + 2], ring[:, (n0 + s) % RING, b * P:(b + 1) * P],
                                           s_kv[:, k, :], start=(k == 0 and b == 0), stop=(k == KD - 1),
                                           skip_group_check=True)
                        mm.then_inc(unit_done, 1)

        modulation(0)

        n = NB["in0"]

        def rotate(r, bank, mat, src, lo, hi, done, evac):
            if r >= 2:
                pe.wait_ge(evac, r - 1)
            pe.matmul(bank[lo:hi, :], mat[lo:hi, lo:hi], src, start=True, stop=True).then_inc(done, 1)

        def rms_sums(first, count):
            for c in range(first, first + count):
                for a, b, _ in ALL_SEGS:
                    src = sqb[:, c, a:b] if c < 4 else sqb4[:, a:b]
                    mm = pe.matmul(PS[3][:, a:b], ones, src, start=(c == first), stop=(c == first + count - 1))
            mm.then_inc(rms_mm, 1)

        def rot_source(f):
            if f == 5:
                return krope[NOPE:DQ, 0:LAT]
            return rq[:, f - 6, 0:LAT] if f < 10 else rk[:, f - 10, 0:LAT]

        for f in range(NF):
            pair, lo, hi = PS[f % 3], 0, P
            if f == 5:
                lo, hi = NOPE, DQ
            if f >= 3:
                pe.wait_ge(ip_ev, f - 2)
            loaded(n)
            for k in range(KD):
                if f == 0:
                    pe.wait_ge(hmod, k + 1)
                for a, b, _ in ALL_SEGS:
                    mm = pe.matmul(pair[lo:hi, a:b], view(n % RING, KD)[:, k, 0:hi - lo], hT0[:, k, a:b],
                                   start=(k == 0), stop=(k == KD - 1))
            mm.then_inc(unit_done, 1)
            n += 1
            if f == 3:
                pe.wait_ge(mod_ev, MOD_CREDIT + 6)
                pe.wait_ge(sq_made, 3)
                rms_sums(0, KQ)
            if f == 5:
                pe.wait_ge(sq_made, 5)
                pe.wait_ge(rms_ln, 1)
                rms_sums(KQ, KKV)
            if f == 6:
                pe.wait_ge(rms_ln, 2)
                pe.wait_ge(ip_ev, 6)
                pe.wait_ge(tabs_in, 16 * 4)
                rotate(0, half(6), rot_mla, rot_source(5), NOPE, DQ, rope_mm, rope_ev)
            if f >= 7:
                pe.wait_ge(ip_ev, f)
                rotate(f - 6, half(6 + (f - 6) % 2), rot_ret, rot_source(f - 1), 0, P, rope_mm, rope_ev)

        def token_major(banks, hT, ready):
            nonlocal n
            for q in range(4):
                loaded(n)
                for k in (2 * q, 2 * q + 1):
                    for t, b in banks:
                        if k == 0:
                            ready(b)
                        mm = pe.matmul(half(b), hT[:, k, t * P:(t + 1) * P], view(n % RING, 2)[:, k % 2, :],
                                       start=(k == 0), stop=(k == KD - 1))
                mm.then_inc(unit_done, 1)
                n += 1

        token_major([(0, 0), (1, 1), (4, 4), (5, 5), (2, 2), (3, 3)], hT0,
                    lambda b: pe.wait_ge(ip_ev, NF if b in (2, 3) else NF - 1))
        rotate(8, half(6), rot_ret, rot_source(13), 0, P, rope_mm, rope_ev)

        def rg_ready_for(b):
            if b < 4:
                pe.wait_ge(ip_ev, NF + 1 + b // 2)
            else:
                pe.wait_ge(rope_ev, 9)

        token_major([(0, 0), (1, 1), (2, 2), (3, 3), (4, 6), (5, 7)], hT0, rg_ready_for)

        def ret_scores(h):
            pe.wait_ge(rope_done, 6 + h)
            for i, (j, seg) in enumerate(RET_TILES):
                s = 8 * h + i
                if s >= 4:
                    pe.wait_ge(ret_p, s - 3)
                else:
                    pe.wait_ge(rg_ready, 2)
                a, b, _ = ALL_SEGS[seg]
                pe.matmul(half(s % 4)[:, 0:b - a], rk[:, h, j * P:(j + 1) * P], rq[:, h, a:b],
                          start=True, stop=True).then_inc(ret_s, 1)

        def ret_values(h):
            pe.wait_ge(ret_p, 8 * h + 8)
            if h >= 2:
                pe.wait_ge(ret_nrm, h - 1)
            else:
                pe.wait_ge(rg_ready, 3)
            for t in range(TT):
                seg = 0 if t < LT else 1
                bank = half(4 + 2 * (h % 2) + seg)
                js = [j for j, s in RET_TILES if s == seg]
                tq = (t - LT * seg) * P
                for j in js:
                    mm = pe.matmul(bank[:, tq:tq + P], pt[:, h % 2, ret_off(j, seg) + tq:ret_off(j, seg) + tq + P],
                                   rv[:, j, h * P:(h + 1) * P], start=(j == js[0]), stop=(j == js[-1]))
            mm.then_inc(ret_o, 1)

        ret_scores(0)
        for h in range(1, H_RET):
            ret_scores(h)
            ret_values(h - 1)
        ret_values(H_RET - 1)

        pe.wait_ge(ret_p, 8 * H_RET)
        pe.wait_ge(ret_nrm, 3)
        pe.wait_ge(wq_in, 16)
        pe.wait_ge(cq_norm, 5)
        for m in range(19):
            pair = PS[m % 3]
            if m >= 3:
                pe.wait_ge(mp_ev, m - 2)
            if m < 8:
                for k in range(KQ):
                    for a, b, _ in ALL_SEGS:
                        mm = pe.matmul(pair[0:DQ, a:b], wuq[:, k, m * DQ:(m + 1) * DQ], cqkv[:, k, a:b],
                                       start=(k == 0), stop=(k == KQ - 1))
            elif m < 16:
                h = m - 8
                if h == 0:
                    pe.wait_ge(wkv_in, 16)
                for k in range(KKV):
                    for a, b, _ in ALL_SEGS:
                        mm = pe.matmul(pair[0:NOPE, a:b], wukv[:, k, h * P:h * P + NOPE], cqkv[:, KQ + k, a:b],
                                       start=(k == 0), stop=(k == KKV - 1))
            else:
                for i in range(2):
                    t = 2 * (m - 16) + i
                    dst = pair[:, 512 * i:512 * i + 512].rearrange("p (h d) -> p h d", h=H_MLA)
                    for k in range(KKV):
                        w = wukv[:, k, :].rearrange("p (h d) -> p h d", h=H_MLA)[:, :, NOPE:NOPE + MLA_V]
                        mm = pe.matmul(dst, cqkv[:, KQ + k, t * P:(t + 1) * P], w, start=(k == 0), stop=(k == KKV - 1))
            mm.then_inc(mp_mm, 1)
            if 1 <= m <= 8:
                h = m - 1
                pe.wait_ge(mp_ev, h + 1)
                if h == 0:
                    pe.wait_ge(ret_nrm, 4)
                rotate(h, half(6 + h % 2), rot_mla, qh[NOPE:DQ, h, 0:LAT], NOPE, DQ, mrope_mm, mrope_ev)

        def att_scores(it):
            h, t = divmod(it, TT)
            if it >= 2:
                pe.wait_ge(att_exp, it - 1)
            else:
                pe.wait_ge(mp_ev, 19)
            if t == 0:
                pe.wait_ge(mrope_done, h + 1)
                pe.wait_ge(kr_cp, h + 1)
            for a, b, _ in (ALL_SEGS if t < LT else ALL_SEGS[1:]):
                mm = pe.matmul(PS[it % 2][:, a:b], qh[0:DQ, h, t * P:(t + 1) * P], kh[0:DQ, h, a:b], start=True, stop=True)
            mm.then_inc(att_s, 1)

        def att_transpose(it):
            t = it % TT
            pe.wait_ge(att_exp, it + 1)
            if it >= 1:
                pe.wait_ge(att_tA, lat_items(it - 1))
                pe.wait_ge(att_tB, it)
            for j in range(0 if t < LT else LT, TT):
                mm = pe.transpose(PS[2][:, j * P:(j + 1) * P], pa[:, it % 2, j * P:(j + 1) * P], ident)
            mm.then_inc(att_t, 1)

        def att_values(it):
            h, t = divmod(it, TT)
            pe.wait_ge(att_tA, lat_items(it))
            pe.wait_ge(att_tB, it + 1)
            if it >= 2:
                pe.wait_ge(att_n, it - 1)
            j0 = 0 if t < LT else LT
            for j in range(j0, TT):
                mm = pe.matmul(half(6 + it % 2)[:, 0:MLA_V], paT[:, it % 2, j * P:(j + 1) * P],
                               va[:, j, h * MLA_V:(h + 1) * MLA_V], start=(j == j0), stop=(j == TT - 1))
            mm.then_inc(att_o, 1)

        for i in range(N_ATT + 2):
            if i < N_ATT:
                att_scores(i)
            if 1 <= i <= N_ATT:
                att_transpose(i - 1)
            if i >= 2:
                att_values(i - 2)

        def out_projection(l, source, hT):
            nonlocal n
            for c in range(KD):
                if c >= 4:
                    pe.wait_ge(oT_ev, KD * l + c - 3)
                for t in range(NT[l] // P):
                    mm = pe.transpose(PS[c % 4][:, t * P:(t + 1) * P], source(c, t), ident)
                mm.then_inc(oT_mm, 1)
            for m in range(KD):
                if m < 4:
                    pe.wait_ge(oT_ev, KD * l + 5 + m)
                else:
                    pe.wait_ge(z_ev, ZB[l] + m - 3)
                loaded(n)
                for k in range(KD):
                    if m == 0:
                        pe.wait_ge(oT_ev, KD * l + k + 1)
                    for a, b, _ in SEGS[l]:
                        mm = pe.matmul(PS[m % 4][:, a:b], view(n % RING, KD)[:, k, :], hT[:, k, a:b],
                                       start=(k == 0), stop=(k == KD - 1))
                mm.then_inc(unit_done, 1)
                n += 1

        def ln_sums(i):
            l = i // 2
            for q, (src, ready, count) in enumerate(((s1, ln_sum1, i + 1), (s2, ln_sum2, KD * (i + 1)))):
                pe.wait_ge(ready, count)
                for a, b, _ in SEGS[l]:
                    mm = pe.matmul(PS[q][:, a:b], ones, src[:, a:b], start=True, stop=True)
                mm.then_inc(ln_mm, 1)

        def ffn(l):
            U, J = FB[l], JB[l]
            z0 = ZB[l] + KD
            for third, (j0, nj) in enumerate(THIRDS):
                def three(dst, s, k, hi, lo, first, last, w):
                    a3 = [(whi, hi, first, False), (whi, lo, False, False), (wlo, hi, False, last)]
                    for wt, h, st, sp_ in a3:
                        for a, b, _ in SEGS[l]:
                            mm = pe.matmul(dst[:, a:b], wt[:, s, k * P:(k + 1) * P], h[:, a:b], start=st, stop=sp_)
                    return mm

                with pe.Fori(0, nj // 2) as it:
                    for s in range(4):
                        if s % 2 == 0:
                            if third:
                                pe.wait_ge(z_ev, z0 + KD * third - 2 + s)
                            pe.wait_ge(h_done, it * 2 + (J + s // 2 - 1 + H_CREDIT))
                        pe.wait_ge(lo_made, it * 4 + (U + s + 1))
                        for k in range(KD):
                            if third == 0 and s == 0:
                                pe.wait_ge(fh_lo, KD * l + k + 1)
                            mm = three(PS[s], s, k, hhi[:, k, :], hlo[:, k, :], k == 0, k == KD - 1, P)
                        mm.then_inc(ffn_tile, 1)
                U += 2 * nj
                with pe.Fori(0, 2) as it:
                    for s in range(4):
                        if s < 2:
                            pe.wait_ge(h_done, J + nj - 1 + s + H_CREDIT)
                        pe.wait_ge(z_ev, it * 4 + (z0 + KD * third + s - 3))
                        pe.wait_ge(lo_made, it * 4 + (U + s + 1))
                        for k in range(nj):
                            if s == 0:
                                pe.wait_ge(ulo_done, J + k + 1)
                            mm = three(PS[s], s, k, uhi[:, k, :], ulo[:, k, :], k == 0, k == nj - 1, P)
                        mm.then_inc(ffn_tile, 1)
                U += KD
                J += nj

        pe.wait_ge(att_n, N_ATT)
        n = NB["out0"]
        out_projection(0, lambda c, t: att[:, t, c * P:(c + 1) * P] if c < 4 else rg[:, t, (c - 4) * P:(c - 3) * P], hT0)
        ln_sums(0)
        modulation(1)
        pe.wait_ge(mod_ev, MOD_CREDIT + 12)
        ffn(0)
        ln_sums(1)

        n = NB["in1"]
        pe.wait_ge(gate_w, 4)
        for k in range(KD):
            pe.wait_ge(hmod, KD + k + 1)
            for a, b, _ in ALL_SEGS:
                mm = pe.matmul(PS[3][:, a:b], wg[:, k, :], hT1[:, k, a:b], start=(k == 0), stop=(k == KD - 1))
        mm.then_inc(gate_mm, 1)
        for f in range(8):
            if f >= 3:
                pe.wait_ge(f_ev, f - 2)
            loaded(n)
            for k in range(KD):
                for a, b, _ in (ALL_SEGS if f >= 4 else ALL_SEGS[:1]):
                    mm = pe.matmul(PS[f % 3][:, a:b], view(n % RING, KD)[:, k, :], hT1[:, k, a:b],
                                   start=(k == 0), stop=(k == KD - 1))
            mm.then_inc(unit_done, 1)
            n += 1
        token_major([(t, t) for t in (4, 5, 0, 1, 2, 3)], hT1, lambda b: pe.wait_ge(f_ev, (7, 8, 6)[b // 2]))
        v1 = {3: lambda: pe.wait_ge(gate_ev, 4), 0: lambda: pe.wait_ge(vg_ev, 1), 1: lambda: pe.wait_ge(vg_ev, 2)}
        token_major([(0, 6), (1, 7), (2, 0), (3, 1), (4, 2), (5, 3)], hT1, lambda b: v1[b // 2]())
        token_major([(0, 4), (1, 5), (2, 6), (3, 7)], hT1, lambda b: pe.wait_ge(vg_ev, 3 if b < 6 else 4))
        token_major([(0, 0), (1, 1), (2, 2), (3, 3)], hT1, lambda b: pe.wait_ge(vg_ev, 5 if b < 2 else 6))

        pe.wait_ge(vg_ev, 8)
        pe.wait_ge(rows_ok, 1)
        for d in range(2):
            for t in range(TT):
                at = (d * TT + t) * H_M
                pe.transpose(half(6)[:, at:at + H_M], li[0:H_M, d, t * P:(t + 1) * P], ident[0:H_M, 0:H_M])
        pe.wait_ge(floor_ok, 1)
        for d in range(2):
            for t in range(LT):
                at = (2 * TT + d * LT + t) * H_M
                mm = pe.transpose(half(6)[:, at:at + H_M], gbc[0:H_M, d, t * P:(t + 1) * P], ident[0:H_M, 0:H_M])
        mm.then_inc(tr_mm, 1)

        def m_scores(h):
            if h == 0:
                pe.wait_ge(vg_ev, 10)
                pe.wait_ge(silu_ev, 8)
            else:
                pe.wait_ge(mexp, 12 * h)
            for d in range(2):
                mm = pe.matmul(half(d), selr[0:H_M, h * P:(h + 1) * P], negm[0:H_M, d, :], start=True, stop=True)
            mm.then_inc(nm_mm, 1)
            b = M_DK * (h % 2)
            for j in range(TT):
                s = TT * h + j
                if s >= 4:
                    pe.wait_ge(mp_done, 2 * (s - 3))
                pe.matmul(half(2 + s % 4), mk[b:b + M_DK, h // 2, j * P:(j + 1) * P], mq[b:b + M_DK, h // 2, :],
                          start=True, stop=True).then_inc(ms_mm, 1)

        def m_values(h):
            pe.wait_ge(mp_done, 12 * (h + 1))
            for t in range(LT):
                i = LT * h + t
                if i >= 2:
                    pe.wait_ge(mh_ev, i - 1)
                else:
                    pe.wait_ge(tr_ev, 2)
                for d in range(2):
                    js = [j for j in range(TT) if j >= LT or (j <= t if d == 0 else j >= t)]
                    for j in js:
                        at = M_OFF[d][j] + t * P - m_range(j, d)[0]
                        mm = pe.matmul(half(6 + i % 2)[:, d * (M_DV + 1):(d + 1) * (M_DV + 1)],
                                       pp[:, h % 2, d, at:at + P], mv[:, j, h, :], start=(j == js[0]), stop=(j == js[-1]))
                mm.then_inc(mo_mm, 1)

        m_scores(0)
        for h in range(1, H_M):
            m_scores(h)
            m_values(h - 1)
        m_values(H_M - 1)
        pe.wait_ge(mn_done, 1)
        out_projection(1, lambda c, t: mo[:, t, c * P:(c + 1) * P], hT1)
        ln_sums(2)
        ffn(1)
        ln_sums(3)
        pe.wait_ge(ln_rstd, 4)
        for t in range(LT):
            for k in range(KD):
                if t == 0:
                    pe.wait_ge(x_new, 3 * KD + k + 1)
                mm = pe.transpose(PS[t][:, k * P:(k + 1) * P], xT[:, k, t * P:(t + 1) * P], ident)
            mm.then_inc(out_mm, 1)

    @block.scalar
    def _(act):
        steps = 0

        def step(ins):
            nonlocal steps
            steps += 1
            ins.then_inc(act_step, 1)
            act.wait_ge(act_step, steps)

        rows = [(c[0], V_C, 8), (c_ctx, V_CC, 8), (ln_g.rearrange("l s n -> (l s n)"), V_LG, 32),
                (ln_b.rearrange("l s n -> (l s n)"), V_LB, 32), (mla_q_norm[0], V_QN, KQ), (mla_kv_norm[0], V_KVN, KKV),
                (m_conv_w[0].rearrange("w n -> (w n)"), V_CW, 24), (m_conv_b[0], V_CB, 8), (m_norm_g[0], V_NG, 8)]
        act.dma_start(kc[:, :], consts[:, 0:K_BASE]).then_inc(consts_in, 16)
        for src, at, nr in rows:
            act.dma_start(vrow[at:at + nr, :], src.rearrange("(r n) -> r n", n=P)).then_inc(consts_in, 16)
        for l in range(DEPTH):
            act.dma_start(brow[48 * l:48 * l + 48, :], mod_b[l].rearrange("(r n) -> r n", n=P)).then_inc(consts_in, 16)
        act.dma_start(vrow[V_ROWS:P, :], consts[V_ROWS:P, 0:P]).then_inc(consts_in, 16)
        act.dma_start(xin[:, 0:LT, :], x[0].rearrange("(t p) n -> p t n", p=P)).then_inc(x_in, 16)
        act.dma_start(xin[:, LT:TT, :], ctx[0].rearrange("(t p) n -> p t n", p=P)).then_inc(x_in, 16)
        act.wait_ge(vec_ev, 1)
        act.activation(scol[:, :], vcol[:, V_C:V_C + 16], ACT.Silu).then_inc(scol_ok, 1)
        act.wait_ge(xT_mm, KD)
        act.dma_start(cosR[:, :, :], consts[:, K_COSR:K_COSR + 2 * LAT].rearrange("p (a t) -> p a t", a=2)).then_inc(tabs_in, 16)
        act.dma_start(cosM[:, :, :], consts[:, K_COSM:K_COSM + 2 * LAT].rearrange("p (a t) -> p a t", a=2)).then_inc(tabs_in, 16)
        act.dma_start(rel[:, :], consts[:, K_REL:K_REL + REL_W]).then_inc(tabs_in, 16)
        act.dma_start(lgc[:, 0, :], ret_log_decay[0].rearrange("a h -> (a h)").partition_broadcast(P)).then_inc(tabs_in, 16)
        act.dma_start(wuq[:, :, :], mla_w_uq[0].rearrange("(k p) n -> p k n", p=P)).then_inc(wq_in, 16)

        def modulate(l, hT, x_sem, x0):
            act.wait_ge(mod_ev, MOD_CREDIT + 6 * l + 2)
            for k in range(KD):
                act.wait_ge(x_sem, x0 + k + 1)
                for a, b, v in ALL_SEGS:
                    ins = act.activation(hT[:, k, a:b], xT[:, k, a:b], ACT.Identity, bias=modc[:, l, 0, k, v:v + 1],
                                         scale=modc[:, l, 1, k, v:v + 1])
                ins.then_inc(hmod, 1)

        modulate(0, hT0, xT_ev, 0)

        def strips(h):
            b, lgf, lgb = h % 2, h, H_RET + h
            act.wait_ge(strip_in, 2 * h + 1)
            act.activation(strip[:, b, 0:REL_W], strip[:, b, 0:REL_W], ACT.Exp, scale=lgc[:, 0, lgf:lgf + 1])
            act.activation(strip[:, b, REL_W:], rel[:, 0:S2_W], ACT.Exp, scale=lgc[:, 0, lgf:lgf + 1], bias=lgc[:, 2, lgf:lgf + 1])
            act.activation(stripb, stripb, ACT.Exp, scale=lgc[:, 1, lgb:lgb + 1]).then_inc(strip_exp, 1)
            act.wait_ge(strip_in, 2 * h + 2)
            act.activation(stripb[:, 0:S2_W], rel[:, 0:S2_W], ACT.Exp, scale=lgc[:, 1, lgb:lgb + 1],
                           bias=lgc[:, 3, lgb:lgb + 1]).then_inc(strip_exp, 1)

        def inverse_rms(i, k):
            act.wait_ge(rms_mm, i + 1)
            act.activation(rms[:, i, :], PS[3][:, 0:T], ACT.Ln, scale=1.0 / (k * P), bias=epsc[:, :]).then_inc(rms_ln, 1)
            act.wait_ge(rms_ln, i + 1)
            act.activation(rms[:, i, :], rms[:, i, :], ACT.Exp, scale=-0.5).then_inc(rms_ready, 1)

        act.wait_ge(eps_ok, 1)
        for f in range(NF):
            act.wait_ge(unit_done, UB["in0"] + f + 1)
            src = PS[f % 3][:, 0:T]
            if f < 5:
                act.activation(sqb[:, f, :] if f < 4 else sqb4, src, ACT.Square).then_inc(sq_made, 1)
                dst = cqkv[:, f, :]
            elif f == 5:
                src, dst = PS[f % 3][NOPE:DQ, 0:T], krope[NOPE:DQ, :]
            else:
                dst = rq[:, f - 6, :] if f < 10 else rk[:, f - 10, :]
            act.activation(dst, src, ACT.Copy).then_inc(ip_ev, 1)
            if f == 3:
                inverse_rms(0, KQ)
            if f == 5:
                inverse_rms(1, KKV)
        strips(0)
        strips(1)
        act.wait_ge(unit_done, UB["in0"] + NF + 4)
        for i in range(3):
            act.activation(rv[:, 2 * i:2 * i + 2, :], PS[i][:, :].rearrange("p (t d) -> p t d", t=2), ACT.Copy).then_inc(ip_ev, 1)
        act.wait_ge(unit_done, UB["in0"] + NF + 8)
        for i, b in enumerate((0, 1, 3)):
            act.activation(rg[:, 2 * i:2 * i + 2, :], PS[b][:, :].rearrange("p (t d) -> p t d", t=2), ACT.Silu).then_inc(rg_ready, 1)

        def ret_inverse_std(h):
            act.wait_ge(ret_var, h + 1)
            step(act.activation(rrs[:, :], rmv[:, :, 1], ACT.Ln, bias=epsc[:, :]))
            act.activation(rrs[:, :], rrs[:, :], ACT.Exp, scale=-0.5).then_inc(ret_rstd, 1)

        strips(2)
        ret_inverse_std(0)
        strips(3)
        for h in range(1, H_RET):
            ret_inverse_std(h)

        act.wait_ge(ret_nrm, H_RET)
        for m in range(19):
            act.wait_ge(mp_mm, m + 1)
            pair = PS[m % 3]
            if m < 8:
                ins = act.activation(qh[0:DQ, m, :], pair[0:DQ, 0:T], ACT.Copy)
            elif m < 16:
                ins = act.activation(kh[0:NOPE, m - 8, :], pair[0:NOPE, 0:T], ACT.Copy)
            else:
                i = m - 16
                ins = act.activation(va[:, 2 * i:2 * i + 2, :], pair[:, :].rearrange("p (t d) -> p t d", t=2), ACT.Copy)
            ins.then_inc(mp_ev, 1)

        def att_exponent(it):
            act.wait_ge(att_nmx, it + 1)
            if it >= 2:
                act.wait_ge(att_t, it - 1)
            a = 0 if it % TT < LT else LAT
            act.activation(pa[:, it % 2, a:T], PS[it % 2][:, a:T], ACT.Exp, bias=nmx[:, 0, it:it + 1], scale=A_SCALE,
                           accum_out=den[:, 0, it:it + 1]).then_inc(att_exp, 1)

        def att_copy(it):
            act.wait_ge(att_t, it + 1)
            if it >= 2:
                act.wait_ge(att_o, it - 1)
            act.activation(paT[:, it % 2, 0:LAT], PS[2][:, 0:LAT], ACT.Copy).then_inc(att_tA, 1)

        for i in range(N_ATT + 1):
            if i < N_ATT:
                att_exponent(i)
            if i >= 1 and (i - 1) % TT < LT:
                att_copy(i - 1)

        def ln_square(i, m):
            l = i // 2
            done = ZB[l] + (KD if i % 2 == 0 else 4 * KD) - KD + m + 1
            act.wait_ge(z_ev, done)
            if KD * i + m >= 2:
                act.wait_ge(ln_sum2, KD * i + m - 1)
            act.activation(sq[:, m % 2, 0:NT[l]], xT[:, m, 0:NT[l]], ACT.Square).then_inc(ln_sq, 1)

        def layer_norm(i):
            l, nt = i // 2, NT[i // 2]
            act.wait_ge(ln_mm, 2 * i + 1)
            act.activation(lnm[:, 0:nt], PS[0][:, 0:nt], ACT.Copy, scale=1.0 / D)
            act.activation(s1[:, 0:nt], PS[0][:, 0:nt], ACT.Square, scale=1.0 / D).then_inc(ln_mean, 1)
            act.wait_ge(ln_var, i + 1)
            step(act.activation(lnr[:, 0:nt], s2[:, 0:nt], ACT.Ln))
            act.activation(lnr[:, 0:nt], lnr[:, 0:nt], ACT.Exp, scale=-0.5).then_inc(ln_rstd, 1)
            for k in range(KD):
                act.wait_ge(ln_norm, KD * i + k + 1)
                g, b = V_LG + KD * i + k, V_LB + KD * i + k
                act.activation(xT[:, k, 0:nt], xT[:, k, 0:nt], ACT.Identity, bias=vcol[:, b:b + 1],
                               scale=vcol[:, g:g + 1]).then_inc(x_new, 1)

        def out_projection(l, hT):
            nt = NT[l]
            for c in range(KD):
                act.wait_ge(oT_mm, KD * l + c + 1)
                if l == 0:
                    ins = act.activation(hT[:, c, 0:nt], PS[c % 4][:, 0:nt], ACT.Copy)
                else:
                    ins = act.activation(hT[:, c, 0:nt], PS[c % 4][:, 0:nt], ACT.Copy, scale=vcol[:, V_NG + c:V_NG + c + 1])
                ins.then_inc(oT_ev, 1)
            for m in range(KD):
                ln_square(2 * l, m)
            layer_norm(2 * l)

        def ffn(l):
            nt, first = NT[l], NB[f"ffn{l}"]
            for k in range(KD):
                act.wait_ge(x_new, KD * 2 * l + k + 1)
                for a, b, v in SEGS[l]:
                    ins = act.activation(hhi[:, k, a:b], xT[:, k, a:b], ACT.Identity, bias=modc[:, l, 3, k, v:v + 1],
                                         scale=modc[:, l, 4, k, v:v + 1])
                ins.then_inc(fh_hi, 1)

            def split(u, s, width, n_of):
                act.wait_ge(landed[(first + s) % RING], n_of)
                if not isinstance(u, int) or u - 3 + TILE_CREDIT > 0:
                    act.wait_ge(ffn_tile, u + (TILE_CREDIT - 3))
                act.activation(whi[:, s, 0:width], ring[:, (first + s) % RING, 0:width], ACT.Copy).then_inc(hi_made, 1)

            def split_static(v, width):
                split(FB[l] + v, v % 4, width, 16 * ((first + v) // RING + 1))

            split_static(0, UNIT)
            split_static(1, UNIT)
            V, J = 0, JB[l]
            for third, (j0, nj) in enumerate(THIRDS):
                def silu(it, jj):
                    act.wait_ge(ffn_tile, it * 4 + (FB[l] + V + 2 * jj + 2 + TILE_CREDIT))
                    act.wait_ge(h_done, it * 2 + (J + jj - 1 + H_CREDIT))
                    act.activation(sg[:, jj, 0:nt], PS[2 * jj + 1][:, 0:nt], ACT.Silu).then_inc(silu_done, 1)

                def high(it, jj):
                    act.wait_ge(h_done, it * 2 + (J + jj + 1 + H_CREDIT))
                    j = it * 2 + jj
                    dst = uhi[:, j, 0:nt] if isinstance(it, int) else uhi[:, bass.ds(j, 1), 0:nt].rearrange("p a t -> p (a t)")
                    act.activation(dst, hu[:, jj, 0:nt], ACT.Copy).then_inc(uhi_done, 1)

                with act.Fori(0, nj // 2 - 1) as it:
                    for jj in range(2):
                        for q in range(2):
                            s = 2 * jj + q + 2
                            split(it * 4 + (FB[l] + V + s), s % 4, UNIT, it * 16 + 16 * ((first + V + s) // RING + 1))
                        silu(it, jj)
                        high(it, jj)
                last = nj // 2 - 1
                for jj in range(2):
                    for q in range(2):
                        v = V + 4 * last + 2 * jj + q + 2
                        split_static(v, UNIT if jj == 0 else nj * P)
                    silu(last, jj)
                    high(last, jj)
                V += 2 * nj
                for m in range(KD):
                    if m + 2 < KD:
                        split_static(V + m + 2, nj * P)
                    elif third < 2:
                        split_static(V + m + 2, UNIT)
                    if third == 2:
                        ln_square(2 * l + 1, m)
                V += KD
                J += nj
            layer_norm(2 * l + 1)

        out_projection(0, hT0)
        ffn(0)

        act.wait_ge(lo_made, FB[1])
        act.wait_ge(ln_norm, KD * 2)
        act.dma_start(wgr[:, :, :], m_w_in[0].rearrange("(k p) n -> p k n", p=P)[:, :, C_MG:C_MG + 4 * H_M]).then_inc(gate_in, 16)
        for g in range(4):
            act.dma_start(gb[32 * g:32 * g + H_M, :], m_gate_b[0, g].unsqueeze(1)).then_inc(gate_in, 16)
        act.dma_start(selr[:, :], consts[:, K_SEL:K_SEL + H_M * P]).then_inc(gate_in, 16)
        modulate(1, hT1, x_new, KD)
        act.wait_ge(gate_in, 16 * 6)
        act.wait_ge(gate_mm, 1)
        for g, dst in enumerate((li, gt, li, gt)):
            act.activation(dst[0:H_M, g // 2, :], PS[3][32 * g:32 * g + H_M, 0:T], ACT.Identity,
                           bias=gb[32 * g:32 * g + H_M, :]).then_inc(gate_ev, 1)

        def conv_in(f):
            act.wait_ge(unit_done, UB["in1"] + f + 1)
            if f < 2:
                act.wait_ge(pad_ok, 4)
            else:
                act.wait_ge(conv_done, f - 1)
            ins = act.activation(cpad[:, f % 2, 1:1 + LAT], PS[f % 3][:, 0:LAT], ACT.Copy)
            if f >= 4:
                ins = act.activation(cpad[:, f % 2, LAT + 3:T + 3], PS[f % 3][:, LAT:T], ACT.Copy)
            ins.then_inc(f_ev, 1)

        def conv_out(f):
            act.wait_ge(conv_done, f + 1)
            bias = vcol[:, V_CB + f:V_CB + f + 1]
            if f < 4:
                act.activation(mq[:, f, :], cacc[:, f % 2, 0:LAT], ACT.Silu, bias=bias).then_inc(silu_ev, 1)
            else:
                act.activation(mk[:, f - 4, 0:LAT], cacc[:, f % 2, 0:LAT], ACT.Silu, bias=bias)
                act.activation(mk[:, f - 4, LAT:T], cacc[:, f % 2, LAT + 2:T + 2], ACT.Silu, bias=bias).then_inc(silu_ev, 1)

        conv_in(0)
        act.wait_ge(ls_in, 1)
        step(act.activation(lf[0:H_M, :, :], gbc[0:H_M, :, :], ACT.Exp))
        act.activation(lf[0:H_M, :, :], lf[0:H_M, :, :], ACT.Ln, bias=onec[0:H_M, :]).then_inc(ls_ln, 1)
        for f in range(1, 8):
            conv_in(f)
            conv_out(f - 1)
        conv_out(7)
        act.wait_ge(floor_in, 1)
        act.activation(gbc[0:H_M, :, 0:LAT], gbc[0:H_M, :, 0:LAT], ACT.Exp, scale=-1.0).then_inc(floor_ok, 1)
        pairs = ((0, 1, 2), (3, 0, 1))
        for g in range(2):
            act.wait_ge(unit_done, UB["in1"] + 8 + 4 * (g + 1))
            for i, b in enumerate(pairs[g]):
                for q in range(2):
                    ins = act.activation(mv[:, 2 * i + q, 4 * g:4 * g + 4, 0:M_DV],
                                         half(2 * b + q).rearrange("p (h d) -> p h d", h=4), ACT.Copy)
                ins.then_inc(vg_ev, 1)
        for g in range(2):
            act.wait_ge(unit_done, UB["in1"] + 16 + 4 * (g + 1))
            for i, b in enumerate(((2, 3), (0, 1))[g]):
                act.activation(mo[:, 2 * i:2 * i + 2, 512 * g:512 * (g + 1)], PS[b][:, :].rearrange("p (t d) -> p t d", t=2),
                               ACT.Sigmoid).then_inc(vg_ev, 1)
        act.wait_ge(tr_ev, 1)
        for h in range(H_M):
            act.wait_ge(nm_mm, h + 1)
            for j in range(TT):
                for d in range(2):
                    e = 2 * (TT * h + j) + d
                    if e >= 4:
                        act.wait_ge(mp_done, e - 3)
                    a, b = m_range(j, d)
                    act.activation(ee[:, e % 4, a:b], half(d)[:, a:b], ACT.Exp, bias=acol[:, d, j, h:h + 1]).then_inc(mexp, 1)
        act.wait_ge(mvar, 1)
        step(act.activation(mrs[:, :], mmv[:, :, 1], ACT.Ln, bias=epsc[:, :]))
        act.activation(mrs[:, :], mrs[:, :], ACT.Exp, scale=-0.5).then_inc(mrstd, 1)
        out_projection(1, hT1)
        ffn(1)
        for t in range(LT):
            act.wait_ge(out_mm, t + 1)
            act.activation(orow[:, t, :], PS[t][:, :], ACT.Copy).then_inc(out_ev, 1)

    @block.vector
    def _(dve):
        steps = 0

        def step(ins):
            nonlocal steps
            steps += 1
            ins.then_inc(dve_step, 1)
            dve.wait_ge(dve_step, steps)

        dve.sem_inc(mod_ev, MOD_CREDIT)
        dve.sem_inc(h_done, H_CREDIT)
        dve.memset(onec[:, :], 1.0)
        dve.memset(epsc[:, :], EPS).then_inc(eps_ok, 1)
        dve.wait_ge(vec_T, 1)
        dve.tensor_copy(vcol[:, 0:V_ROWS], half(1)[:, 0:V_ROWS]).then_inc(vec_ev, 1)
        dve.tensor_copy(modb[:, :], half(0)[:, 0:96])
        for k in range(KD):
            dve.wait_ge(xT_mm, k + 1)
            dve.tensor_copy(xT[:, k, :], PS[1 + k % 2][:, 0:T]).then_inc(xT_ev, 1)

        def modulation(l):
            for g in range(6):
                dve.wait_ge(unit_done, UB[f"mod{l}"] + KD * (g + 1))
                src = half(6 + g % 2)[:, 0:16].rearrange("p (b v) -> p v b", v=2)
                at = 48 * l + KD * g
                for v in range(2):
                    dst = modc[:, l, g, :, :].rearrange("p b v -> p v b")[:, v, :]
                    if g in (1, 4):
                        ins = dve.scalar_tensor_tensor(dst, src[:, v, :], 1.0, modb[:, at:at + KD], ALU.add, ALU.add)
                    else:
                        ins = dve.tensor_tensor(dst, src[:, v, :], modb[:, at:at + KD], ALU.add)
                ins.then_inc(mod_ev, 1)

        modulation(0)
        dve.wait_ge(tabs_in, 16 * 4)
        for i, f in ((1, -1.0), (2, float(P)), (3, 640.0)):
            ins = dve.tensor_scalar(lgc[:, i, :], lgc[:, 0, :], f, None, ALU.mult)
        step(ins)
        for c in range(KQ + KKV):
            i = 0 if c < KQ else 1
            dve.wait_ge(rms_ready, i + 1)
            dve.scalar_tensor_tensor(cqkv[:, c, :], cqkv[:, c, :], vcol[:, V_QN + c:V_QN + c + 1], rms[:, i, :],
                                     ALU.mult, ALU.mult).then_inc(cq_norm, 1)

        def rope(r, bank, X, tab, tmp, lo, hi, mm, ev, done):
            dve.wait_ge(mm, r + 1)
            dve.tensor_tensor(tmp[lo:hi, :], bank[lo:hi, :], tab[lo:hi, 1, :], ALU.mult).then_inc(ev, 1)
            step(dve.tensor_tensor(X, X, tab[lo:hi, 0, :], ALU.mult))
            dve.tensor_tensor(X, X, tmp[lo:hi, :], ALU.add).then_inc(done, 1)

        rope(0, half(6), krope[NOPE:DQ, 0:LAT], cosM, rtmp, NOPE, DQ, rope_mm, rope_ev, rope_done)

        def rope_ret(r):
            X = rq[:, r - 1, 0:LAT] if r <= H_RET else rk[:, r - 1 - H_RET, 0:LAT]
            dve.wait_ge(rope_done, r)
            rope(r, half(6 + r % 2), X, cosR, rtmp, 0, P, rope_mm, rope_ev, rope_done)

        for r in range(1, 8):
            rope_ret(r)

        def strips(h):
            a = strip[:, h % 2, 0:REL_W]
            far = float(LAT - P)
            dve.tensor_scalar(a, rel[:, :], -far, 0.0, ALU.add, ALU.max)
            dve.tensor_scalar(stripb, rel[:, :], -far, 0.0, ALU.add, ALU.min).then_inc(strip_in, 1)
            dve.wait_ge(strip_exp, 2 * h + 1)
            dve.scalar_tensor_tensor(a, rel[:, :], far, a, ALU.is_ge, ALU.mult)
            step(dve.scalar_tensor_tensor(stripb, rel[:, :], far, stripb, ALU.is_le, ALU.mult))
            dve.tensor_tensor(a, a, stripb, ALU.add).then_inc(strip_in, 1)
            dve.wait_ge(strip_exp, 2 * h + 2)
            step(dve.tensor_tensor(strip[:, h % 2, REL_W:], strip[:, h % 2, REL_W:], stripb[:, 0:S2_W], ALU.add))

        strips(0)
        strips(1)
        rope_ret(8)

        def ret_weigh(h):
            if h >= 2:
                dve.wait_ge(ret_o, h - 1)
            for i, (j, seg) in enumerate(RET_TILES):
                s = 8 * h + i
                dve.wait_ge(ret_s, s + 1)
                a, b, _ = ALL_SEGS[seg]
                w = b - a
                if seg == 0 and j >= LT:
                    c0 = REL_W + P * (TT - 1 - j)
                else:
                    c0 = (LAT - P) - P * (j - LT * seg)
                dve.scalar_tensor_tensor(pt[:, h % 2, ret_off(j, seg):ret_off(j, seg) + w], half(s % 4)[:, 0:w], R_SCALE,
                                         strip[:, h % 2, c0:c0 + w], ALU.mult, ALU.mult).then_inc(ret_p, 1)

        def ret_norm(h):
            dve.wait_ge(ret_o, h + 1)

            def o(t):
                seg = 0 if t < LT else 1
                return half(4 + 2 * (h % 2) + seg)[:, (t - LT * seg) * P:(t - LT * seg + 1) * P]

            for t in range(TT):
                ins = dve.bn_stats(rst[:, t, :], o(t))
            step(ins)
            for t in range(TT):
                ins = dve.bn_aggr(rmv[:, t, :], rst[:, t, :])
            ins.then_inc(ret_var, 1)
            dve.wait_ge(ret_rstd, h + 1)
            for t in range(TT):
                step(dve.tensor_scalar(rnm[:, t % 2, :], o(t), rmv[:, t, 0:1], rrs[:, t:t + 1], ALU.subtract, ALU.mult))
                dst = rg[:, t, h * P:(h + 1) * P]
                ins = dve.tensor_tensor(dst, dst, rnm[:, t % 2, :], ALU.mult)
            ins.then_inc(ret_nrm, 1)

        dve.wait_ge(rg_ready, 3)
        ret_weigh(0)
        ret_weigh(1)
        strips(2)
        ret_norm(0)
        ret_weigh(2)
        strips(3)
        ret_norm(1)
        ret_weigh(3)
        ret_norm(2)
        ret_norm(3)

        for h in range(H_MLA):
            rope(h, half(6 + h % 2), qh[NOPE:DQ, h, 0:LAT], cosM, mtmp, NOPE, DQ, mrope_mm, mrope_ev, mrope_done)
            dve.wait_ge(mrope_done, h + 1)

        def att_max(it):
            dve.wait_ge(att_s, it + 1)
            a = 0 if it % TT < LT else LAT
            step(dve.tensor_reduce(nmx[:, 1, it:it + 1], PS[it % 2][:, a:T], AX.X, ALU.max))
            dve.tensor_scalar(nmx[:, 0, it:it + 1], nmx[:, 1, it:it + 1], -A_SCALE, None, ALU.mult).then_inc(att_nmx, 1)

        def att_copy(it):
            dve.wait_ge(att_t, it + 1)
            if it >= 2:
                dve.wait_ge(att_o, it - 1)
            dve.tensor_copy(paT[:, it % 2, LAT:T], PS[2][:, LAT:T]).then_inc(att_tB, 1)

        def att_norm(it):
            h, t = divmod(it, TT)
            dve.wait_ge(att_o, it + 1)
            step(dve.reciprocal(den[:, 1, it:it + 1], den[:, 0, it:it + 1]))
            dve.tensor_scalar(att[:, t, h * MLA_V:(h + 1) * MLA_V], half(6 + it % 2)[:, 0:MLA_V], den[:, 1, it:it + 1],
                              None, ALU.mult).then_inc(att_n, 1)

        for i in range(N_ATT + 2):
            if i < N_ATT:
                att_max(i)
            if 1 <= i <= N_ATT:
                att_copy(i - 1)
            if i >= 2:
                att_norm(i - 2)

        def z_update(l, g, m, pair, z):
            for a, b, v in SEGS[l]:
                ins = dve.scalar_tensor_tensor(xT[:, m, a:b], pair[:, a:b], modc[:, l, g, m, v:v + 1], xT[:, m, a:b],
                                               ALU.mult, ALU.add)
            ins.then_inc(z_ev, 1)

        def ln_sum(i, m, z):
            nt = NT[i // 2]
            dve.wait_ge(z_ev, z)
            if m == 0:
                ins = dve.tensor_copy(s1[:, 0:nt], xT[:, m, 0:nt])
            else:
                ins = dve.tensor_tensor(s1[:, 0:nt], s1[:, 0:nt], xT[:, m, 0:nt], ALU.add)
            if m == KD - 1:
                ins.then_inc(ln_sum1, 1)
            else:
                step(ins)

        def layer_norm(i):
            nt = NT[i // 2]
            dve.wait_ge(ln_mm, 2 * i + 2)
            dve.wait_ge(ln_mean, i + 1)
            step(dve.scalar_tensor_tensor(s2[:, 0:nt], PS[1][:, 0:nt], 1.0 / D, s1[:, 0:nt], ALU.mult, ALU.subtract))
            dve.tensor_scalar(s2[:, 0:nt], s2[:, 0:nt], 0.0, EPS, ALU.max, ALU.add).then_inc(ln_var, 1)
            dve.wait_ge(ln_rstd, i + 1)
            for k in range(KD):
                z = xT[:, k, 0:nt]
                step(dve.tensor_tensor(z, z, lnm[:, 0:nt], ALU.subtract))
                dve.tensor_tensor(z, z, lnr[:, 0:nt], ALU.mult).then_inc(ln_norm, 1)

        def out_projection(l):
            for m in range(KD):
                dve.wait_ge(unit_done, UB[f"out{l}"] + m + 1)
                dve.wait_ge(xa_done, KD * 2 * l + m + 1)
                z_update(l, 2, m, PS[m % 4], 0)
                if m >= 1:
                    ln_sum(2 * l, m - 1, ZB[l] + m)
            ln_sum(2 * l, KD - 1, ZB[l] + KD)
            layer_norm(2 * l)

        def ffn(l):
            nt = NT[l]
            for k in range(KD):
                dve.wait_ge(x_new, KD * 2 * l + k + 1)
                for a, b, v in SEGS[l]:
                    ins = dve.tensor_scalar(hu[:, k % 2, a:b], xT[:, k, a:b], modc[:, l, 4, k, v:v + 1],
                                            modc[:, l, 3, k, v:v + 1], ALU.mult, ALU.add)
                step(ins)
                dve.wait_ge(fh_hi, KD * l + k + 1)
                dve.tensor_tensor(hlo[:, k, 0:nt], hu[:, k % 2, 0:nt], hhi[:, k, 0:nt].bitcast(F32), ALU.subtract).then_inc(fh_lo, 1)
            V, J, z0 = 0, JB[l], ZB[l] + KD
            for third, (j0, nj) in enumerate(THIRDS):
                with dve.Fori(0, nj // 2) as it:
                    for jj in range(2):
                        dve.wait_ge(silu_done, it * 2 + (J + jj + 1))
                        dve.wait_ge(uhi_done, it * 2 + (J + jj + 1 - 2) if J or third else it * 2 + jj)
                        dve.tensor_tensor(hu[:, jj, 0:nt], sg[:, jj, 0:nt], PS[2 * jj][:, 0:nt], ALU.mult).then_inc(h_done, 1)
                        dve.wait_ge(uhi_done, it * 2 + (J + jj + 1))
                        j = it * 2 + jj
                        hi = uhi[:, bass.ds(j, 1), 0:nt].rearrange("p a t -> p (a t)")
                        lo = ulo[:, bass.ds(j, 1), 0:nt].rearrange("p a t -> p (a t)")
                        dve.tensor_tensor(lo, hu[:, jj, 0:nt], hi.bitcast(F32), ALU.subtract).then_inc(ulo_done, 1)
                V += 2 * nj
                for m in range(KD):
                    dve.wait_ge(ffn_tile, FB[l] + V + m + 1 + TILE_CREDIT)
                    if third == 0:
                        dve.wait_ge(xa_done, KD * (2 * l + 1) + m + 1)
                    else:
                        dve.wait_ge(z_ev, z0 + KD * (third - 1) + m + 1)
                    z_update(l, 5, m, PS[m % 4], 0)
                    if third == 2 and m >= 1:
                        ln_sum(2 * l + 1, m - 1, z0 + 2 * KD + m)
                V += KD
                J += nj
            ln_sum(2 * l + 1, KD - 1, z0 + 3 * KD)
            layer_norm(2 * l + 1)

        out_projection(0)
        modulation(1)
        ffn(0)

        dve.wait_ge(gate_ev, 4)
        z_, g_, b_ = gt[0:H_M, :, :], gbc[0:H_M, :, :], lf[0:H_M, :, :]
        dve.scalar_tensor_tensor(g_, z_, -1.0, z_, ALU.mult, ALU.min).then_inc(ls_in, 1)

        def conv(f):
            w = LAT if f < 4 else T + 2
            dve.wait_ge(f_ev, f + 1)
            if f >= 2:
                dve.wait_ge(silu_ev, f - 1)
            y = cacc[:, f % 2, 0:w]

            def tap(i):
                return vcol[:, V_CW + 8 * i + f:V_CW + 8 * i + f + 1]

            step(dve.tensor_scalar(y, cpad[:, f % 2, 1:1 + w], tap(1), None, ALU.mult))
            step(dve.scalar_tensor_tensor(y, cpad[:, f % 2, 0:w], tap(0), y, ALU.mult, ALU.add))
            dve.scalar_tensor_tensor(y, cpad[:, f % 2, 2:2 + w], tap(2), y, ALU.mult, ALU.add).then_inc(conv_done, 1)

        dve.wait_ge(ls_ln, 1)
        step(dve.scalar_tensor_tensor(b_, z_, 0.0, b_, ALU.min, ALU.subtract))

        def scan(dst, src, d, op, init):
            for a, b in ((LAT, T), (0, LAT)):
                sl = slice(a, b) if d == 0 else slice(b - 1, a - 1 if a else None, -1)
                step(dve.tensor_tensor_scan(dst[0:H_M, d, sl], src[0:H_M, d, sl], src[0:H_M, d, sl], init, op, ALU.bypass))
                last = T - 1 if d == 0 else LAT
                init = dst[0:H_M, d, last:last + 1]

        conv(0)
        for d in range(2):
            scan(gbc, lf, d, ALU.add, 0.0)
        conv(1)
        step(dve.tensor_tensor(li[0:H_M, :, :], li[0:H_M, :, :], g_, ALU.subtract))
        for d in range(2):
            scan(gt, li, d, ALU.max, 0.0)
        conv(2)
        dve.tensor_scalar(negm[0:H_M, :, :], gt[0:H_M, :, 0:LAT], -1.0, None, ALU.mult).then_inc(rows_ok, 1)
        dve.tensor_tensor(gbc[0:H_M, :, 0:LAT], gbc[0:H_M, :, 0:LAT], gt[0:H_M, :, 0:LAT], ALU.add).then_inc(floor_in, 1)
        for f in range(3, 8):
            conv(f)
        dve.wait_ge(tr_mm, 1)
        dve.tensor_copy(acol[:, :, :, :], half(6)[:, 0:2 * TT * H_M].rearrange("p (d t h) -> p d t h", d=2, t=TT)).then_inc(tr_ev, 1)
        dve.tensor_copy(fcol[:, :, :, :], half(6)[:, 2 * TT * H_M:2 * (TT + LT) * H_M].rearrange("p (d t h) -> p d t h", d=2, t=LT)).then_inc(tr_ev, 1)

        def m_weigh(h):
            if h >= 2:
                dve.wait_ge(mo_mm, LT * (h - 1))
            for j in range(TT):
                for d in range(2):
                    s = TT * h + j
                    e = 2 * s + d
                    dve.wait_ge(ms_mm, s + 1)
                    if j < LT:
                        dve.wait_ge(msel, 2 * LT * h + 2 * j + d + 1)
                    else:
                        dve.wait_ge(mexp, e + 1)
                    a, b = m_range(j, d)
                    at = M_OFF[d][j]
                    dve.scalar_tensor_tensor(pp[:, h % 2, d, at:at + b - a], half(2 + s % 4)[:, a:b], M_SCALE,
                                             ee[:, e % 4, a:b], ALU.mult, ALU.mult).then_inc(mp_done, 1)

        def m_divide(h):
            for t in range(LT):
                i = LT * h + t
                dve.wait_ge(mo_mm, i + 1)
                o = half(6 + i % 2)[:, 0:2 * (M_DV + 1)].rearrange("p (d v) -> p d v", d=2)
                dd = dab[:, i % 2, t, :]
                step(dve.tensor_scalar(dd, o[:, :, M_DV], -1.0, None, ALU.mult))
                step(dve.tensor_tensor(dd, dd, o[:, :, M_DV], ALU.max))
                step(dve.tensor_tensor(dd, dd, fcol[:, :, t, h], ALU.max))
                step(dve.reciprocal(dd, dd))
                step(dve.tensor_scalar(hf[:, i % 2, :], o[:, 0, 0:M_DV], dd[:, 0:1], None, ALU.mult))
                dst = hb[:, t, h * M_DV:(h + 1) * M_DV]
                dve.scalar_tensor_tensor(dst, o[:, 1, 0:M_DV], dd[:, 1:2], hf[:, i % 2, :], ALU.mult, ALU.add).then_inc(mh_ev, 1)
            dve.wait_ge(mh_ev, LT * (h + 1))
            for t in range(LT):
                ins = dve.bn_stats(mst[:, h * LT + t, :], hb[:, t, h * M_DV:(h + 1) * M_DV])
            step(ins)
            for t in range(LT):
                ins = dve.bn_aggr(mmv[:, h * LT + t, :], mst[:, h * LT + t, :])
            if h == H_M - 1:
                ins.then_inc(mvar, 1)

        dve.wait_ge(vg_ev, 10)
        m_weigh(0)
        for h in range(1, H_M):
            m_weigh(h)
            m_divide(h - 1)
        m_divide(H_M - 1)
        dve.wait_ge(mrstd, 1)
        for h in range(H_M):
            for t in range(LT):
                i = h * LT + t
                dst = hb[:, t, h * M_DV:(h + 1) * M_DV]
                ins = dve.tensor_scalar(dst, dst, mmv[:, i, 0:1], mrs[:, i:i + 1], ALU.subtract, ALU.mult)
        step(ins)
        for t in range(LT):
            ins = dve.tensor_tensor(mo[:, t, :], mo[:, t, :], hb[:, t, :], ALU.mult)
        ins.then_inc(mn_done, 1)
        out_projection(1)
        ffn(1)

    @block.gpsimd
    def _(pool):
        def scale_residual(i, ready, first):
            nt = NT[i // 2]
            for k in range(KD):
                pool.wait_ge(ready, first + k + 1)
                pool.tensor_scalar(xT[:, k, 0:nt], xT[:, k, 0:nt], ALPHA, None, ALU.mult).then_inc(xa_done, 1)

        def ln_sum(i, m):
            nt = NT[i // 2]
            pool.wait_ge(ln_sq, KD * i + m + 1)
            if m == 0:
                pool.tensor_copy(s2[:, 0:nt], sq[:, 0, 0:nt]).then_inc(ln_sum2, 1)
            else:
                pool.wait_ge(ln_sum2, KD * i + m)
                pool.tensor_tensor(s2[:, 0:nt], s2[:, 0:nt], sq[:, m % 2, 0:nt], ALU.add).then_inc(ln_sum2, 1)

        def ffn(l):
            def low(u, s, width):
                pool.wait_ge(hi_made, u)
                pool.tensor_tensor(wlo[:, s, 0:width], ring[:, (NB[f"ffn{l}"] + s) % RING, 0:width],
                                   whi[:, s, 0:width].bitcast(F32), ALU.subtract).then_inc(lo_made, 1)

            full = sum(2 * nj + KD for _, nj in THIRDS[:2]) + 2 * THIRDS[2][1]
            with pool.Fori(0, full // 4) as it:
                for s in range(4):
                    low(it * 4 + (FB[l] + s + 1), s, UNIT)
            w = THIRDS[2][1] * P
            low(FB[l] + full + 1, 0, w)
            low(FB[l] + full + 2, 1, w)
            for m in range(KD):
                if m + 2 < KD:
                    low(FB[l] + full + m + 3, (m + 2) % 4, w)
                ln_sum(2 * l + 1, m)

        scale_residual(0, hmod, 0)
        pool.wait_ge(xa_done, KD)
        pool.wait_ge(rope_done, 1)
        pool.wait_ge(ret_nrm, H_RET)
        for h in range(H_MLA):
            pool.tensor_copy(kh[NOPE:DQ, h, :], krope[NOPE:DQ, :]).then_inc(kr_cp, 1)
        for m in range(KD):
            ln_sum(0, m)
        scale_residual(1, fh_lo, 0)
        ffn(0)
        pool.wait_ge(gate_in, 16 * 6)
        pool.memset(wg[:, :, :], 0.0).then_inc(pool_step, 1)
        pool.wait_ge(pool_step, 1)
        for g in range(4):
            pool.tensor_copy(wg[:, :, 32 * g:32 * g + H_M], wgr[:, :, H_M * g:H_M * (g + 1)]).then_inc(gate_w, 1)
        for s in range(2):
            pool.memset(cpad[:, s, 0:1], 0.0)
            pool.memset(cpad[:, s, LAT + 1:LAT + 3], 0.0).then_inc(pad_ok, 1)
            pool.memset(cpad[:, s, T + 3:T + 4], 0.0).then_inc(pad_ok, 1)
        pool.memset(mv[:, :, :, M_DV:M_DV + 1], 1.0).then_inc(ones_ok, 1)
        scale_residual(2, hmod, KD)
        for h in range(H_M):
            for j in range(LT):
                for d in range(2):
                    e = 2 * (TT * h + j) + d
                    pool.wait_ge(mexp, e + 1)
                    blk = ee[:, e % 4, j * P:(j + 1) * P]
                    sign = 1 if d == 0 else -1
                    pool.affine_select(out=blk, in_=blk, pattern=[[sign, P]], compare_op=ALU.is_ge, fill=0.0, base=0,
                                       channel_multiplier=-sign).then_inc(msel, 1)
        for m in range(KD):
            ln_sum(2, m)
        scale_residual(3, fh_lo, KD)
        ffn(1)

    es.close()


_INS = ['x', 'c', 'ctx', 'c_ctx', 'mod_w', 'mod_b', 'ln_g', 'ln_b', 'ffn_w_in', 'ffn_w_out', 'ab_w_in', 'mla_q_norm',
        'mla_w_uq', 'mla_kv_norm', 'mla_w_ukv', 'ret_log_decay', 'ab_w_out', 'm_w_in', 'm_conv_w', 'm_conv_b',
        'm_gate_b', 'm_norm_g', 'm_w_out']


def kernel(**inputs):
    import concourse.bacc as _bacc
    from concourse.bass_utils import run_bass_kernel_spmd as _run

    nc = _bacc.Bacc("TRN2", target_bir_lowering=False, num_devices=1)
    arrays, args = {}, []
    for name in _INS:
        a = np.ascontiguousarray(inputs[name])
        arrays[f"in_{name}"] = a
        args.append(nc.dram_tensor(f"in_{name}", a.shape, mybir.dt.from_np(a.dtype), kind="ExternalInput").ap())
    k = shape_constants()
    arrays["in_consts"] = k
    args.append(nc.dram_tensor("in_consts", k.shape, F32, kind="ExternalInput").ap())
    args.append(nc.dram_tensor("out", (1, LAT, D), F32, kind="ExternalOutput").ap())
    build(nc, *args)
    r = _run(nc, [arrays], core_ids=[0])
    return r.results[0]["out"]
```

```python
from contextlib import ExitStack

import numpy as np

import concourse.bass as bass
from concourse import mybir

F32 = mybir.dt.float32
F32R = mybir.dt.float32r
ALU = mybir.AluOpType
ACT = mybir.ActivationFunctionType
AX = mybir.AxisListType

P = 128
D = 1024
KD = D // P
LAT, CTX = 512, 256
T = LAT + CTX
TT = T // P
LT = LAT // P
GRID_W = 64
ROPE_BASE = 10000.0
DEPTH = 2
ALPHA = (2 * DEPTH) ** 0.25
EPS = 1e-5

H_MLA, NOPE, ROPE, MLA_V = 8, 64, 32, 64
DQ = NOPE + ROPE
Q_LORA, KV_LORA = 384, 256
KQ, KKV = Q_LORA // P, KV_LORA // P
H_RET, RET_D = 4, 128
H_M, M_DK, M_DV = 8, 64, 128
D_FF = -(-8 * D // (3 * 256)) * 256
FC = D_FF // P
THIRDS = ((0, 8), (8, 8), (16, FC - 16))

RING = 4
UNIT = 1024

C_KR = Q_LORA + KV_LORA
C_RQ = C_KR + ROPE
C_RK = C_RQ + H_RET * RET_D
C_RV = C_RK + H_RET * RET_D
C_RG = C_RV + H_RET * RET_D
C_MK = H_M * M_DK
C_MV = 2 * H_M * M_DK
C_MO = C_MV + H_M * M_DV
C_MG = C_MO + H_M * M_DV

V_C, V_CC, V_LG, V_LB = 0, 8, 16, 48
V_QN, V_KVN, V_CW, V_CB, V_NG = 80, 83, 85, 109, 117
V_ROWS = 125

REL_W = 896
K_ID, K_ONE, K_RR, K_RM = 0, 128, 256, 384
K_BASE = 512
K_COSR, K_SINR = 512, 1024
K_COSM, K_SINM = 1536, 2048
K_REL = 2560
K_SEL = K_REL + REL_W
K_ALL = K_SEL + H_M * P


def shape_constants():
    k = np.zeros((P, K_ALL), np.float32)
    p = np.arange(P)
    k[p, K_ID + p] = 1.0
    k[:, K_ONE:K_ONE + P] = 1.0

    def rotation(base, first, width, half):
        for b in range(first, first + width, 2 * half):
            for c in range(half):
                k[b + half + c, base + b + c] = -1.0
                k[b + c, base + b + half + c] = 1.0

    rotation(K_RR, 0, P, RET_D // 4)
    rotation(K_RM, NOPE, ROPE, ROPE // 4)
    t = np.arange(LAT)
    pos = np.stack([t // GRID_W, t % GRID_W]).astype(np.float32)

    def table(width, first, cos_at, sin_at):
        da = width // 2
        inv = (np.float32(ROPE_BASE) ** (-np.arange(0, da, 2, dtype=np.float32) / np.float32(da))).astype(np.float32)
        for i in range(width):
            a = pos[i // da] * inv[i % (da // 2)]
            k[first + i, cos_at:cos_at + LAT] = np.cos(a)
            k[first + i, sin_at:sin_at + LAT] = np.sin(a)

    table(RET_D, 0, K_COSR, K_SINR)
    table(ROPE, NOPE, K_COSM, K_SINM)
    k[:, K_REL:K_REL + REL_W] = np.arange(REL_W)[None, :] - p[:, None]
    for h in range(H_M):
        k[h, K_SEL + h * P:K_SEL + (h + 1) * P] = 1.0
    return k


def build(nc, x, c, ctx, c_ctx, mod_w, mod_b, ln_g, ln_b, ffn_w_in, ffn_w_out, ab_w_in, mla_q_norm, mla_w_uq,
          mla_kv_norm, mla_w_ukv, ret_log_decay, ab_w_out, m_w_in, m_conv_w, m_conv_b, m_gate_b, m_norm_g,
          m_w_out, consts, out):
    es = ExitStack()

    def sb(name, shape, dt=F32, at=None):
        return (at or es).enter_context(nc.sbuf_tensor(name, shape, dt))

    def under(*specs):
        st = ExitStack()
        r = [sb(name, shape, dt, at=st) for name, shape, dt in specs]
        st.close()
        return r if len(r) > 1 else r[0]

    def sem(name):
        return es.enter_context(nc.semaphore(name))

    kc = sb("kc", [P, K_BASE])
    ident, ones = kc[:, K_ID:K_ID + P], kc[:, K_ONE:K_ONE + P]
    rot_ret, rot_mla = kc[:, K_RR:K_RR + P], kc[:, K_RM:K_RM + P]
    xT = sb("xT", [P, KD, T])
    ring = sb("ring", [P, RING, UNIT])
    vcol = sb("vcol", [P, P])
    scol = sb("scol", [P, 16])
    modb = sb("modb", [P, DEPTH * 48])
    modc = sb("modc", [P, DEPTH, 6, KD, 2])
    mrow = sb("mrow", [2, D])
    epsc = sb("epsc", [P, 1])
    onec = sb("onec", [P, 1])
    _, whi1 = under(("whi1_pad", [P, 4 * T - UNIT], F32), ("whi1", [P, 2, UNIT], F32R))
    lnbuf = sb("lnbuf", [P, 6, T])
    lnm, lnr, s1, s2 = (lnbuf[:, i, :] for i in range(4))
    sq = lnbuf[:, 4:6, :]

    def phase():
        return ExitStack()

    ph = phase()
    xin = sb("xin", [P, TT, D], at=ph)
    vrow = sb("vrow", [P, P], at=ph)
    brow = sb("brow", [96, P], at=ph)
    ph.close()
    m0 = phase()
    hx = under(("hx", [P, 2, KD, T], F32R))
    hx_raw = under(("hx_raw", [P, 2, KD, T], F32))
    W_KV = H_MLA * (NOPE + MLA_V)
    wukv = sb("wukv", [P, KKV, W_KV], at=m0)
    va = sb("va", [P, TT, H_MLA * MLA_V], at=m0)
    kh, mtmp = under(("kh", [P, H_MLA, T], F32), ("mtmp", [P, LAT], F32))
    PT_W = TT * LAT + 2 * CTX
    pt = sb("pt", [P, 2, PT_W], at=m0)
    assert KKV * W_KV + TT * H_MLA * MLA_V + 2 * PT_W >= 2 * KD * T
    cqkv = sb("cqkv", [P, KQ + KKV, T], at=m0)
    krope = sb("krope", [P, T], at=m0)
    wuq = sb("wuq", [P, KQ, H_MLA * DQ], at=m0)
    wsp_in0 = under(("wsp_in0", [P, 2, 2, UNIT], F32R))
    rg = sb("rg", [P, TT, H_RET * RET_D], at=m0)
    sb("wsp_in0_rest", [P, 4 * UNIT - TT * H_RET * RET_D], at=m0)
    cosM = sb("cosM", [P, 2, LAT], at=m0)
    ph = phase()
    rq = sb("rq", [P, H_RET, T], at=ph)
    rk = sb("rk", [P, H_RET, T], at=ph)
    rv = sb("rv", [P, TT, H_RET * RET_D], at=ph)
    cosR = sb("cosR", [P, 2, LAT], at=ph)
    rel = sb("rel", [P, REL_W], at=ph)
    lnf = lnbuf[:, :, :].rearrange("p a t -> p (a t)")
    sqb, rms = lnbuf[:, 0:3, :], lnbuf[:, 3:5, :]
    S2_W = LAT + P
    strip = lnf[:, 0:2 * (REL_W + S2_W)].rearrange("p (b n) -> p b n", b=2)
    stripb = lnf[:, 2 * (REL_W + S2_W):2 * (REL_W + S2_W) + REL_W]
    lgc = sb("lgc", [P, 4, 2 * H_RET], at=ph)
    rtmp = sb("rtmp", [P, LAT], at=ph)
    rst = sb("rst", [P, TT, 6], at=ph)
    rmv = sb("rmv", [P, TT, 2], at=ph)
    rrs = sb("rrs", [P, TT], at=ph)
    rnm = sb("rnm", [P, 2, RET_D], at=ph)
    ph.close()
    ph = phase()
    wsp_out0 = under(("wsp_out0", [P, 2, 2, UNIT], F32R))
    qh = sb("qh", [P, H_MLA, T], at=ph)
    att = sb("att", [P, TT, H_MLA * MLA_V], at=ph)
    pa = lnbuf[:, 0:2, :]
    paT = sb("paT", [P, 2, T], at=ph)
    NI = H_MLA * TT
    nmx = sb("nmx", [P, 2, NI], at=ph)
    den = sb("den", [P, 2, NI], at=ph)
    ph.close()
    m0.close()
    m1 = phase()
    hb = under(("hb", [P, LT, D], F32))
    hT1 = sb("hT1", [P, KD, T], F32R, at=m1)
    mq = sb("mq", [P, H_M // 2, LAT], at=m1)
    mk = sb("mk", [P, H_M // 2, T], at=m1)
    wgr, wgf, wg = under(("wgr", [P, KD, 4 * H_M], F32), ("wgf", [P, KD, P], F32), ("wg", [P, 2, KD, P], F32R))
    mv = sb("mv", [P, TT, H_M, M_DV + 1], at=m1)
    hlo1 = under(("hlo1", [P, KD, T], F32R))
    hlo1_raw = under(("hlo1_raw", [P, KD, T], F32))
    mo = sb("mo", [P, LT, H_M * M_DV], at=m1)
    ee = sb("ee", [P, 4, LAT], at=m1)
    selr = sb("selr", [P, H_M * P], at=m1)
    acol = sb("acol", [P, 2, TT, H_M], at=m1)
    fcol = sb("fcol", [P, 2, LT, H_M], at=m1)
    negm = lnbuf[:, :, :].rearrange("p a t -> p (a t)")[:, 0:2 * LAT].rearrange("p (d t) -> p d t", d=2)
    FW = 2 * LAT + sum(LAT - P * j for j in range(LT))
    ph = phase()
    wlo1 = sb("wlo1", [P, 2, UNIT], F32R, at=ph)
    gb = sb("gb", [P, 1], at=ph)
    cpad = sb("cpad", [P, 2, T + 4], at=ph)
    cacc = sb("cacc", [P, 2, T + 2], at=ph)
    li = sb("li", [P, 2, T], at=ph)
    lf = sb("lf", [P, 2, T], at=ph)
    gt = sb("gt", [P, 2, T], at=ph)
    gbc = sb("gbc", [P, 2, T], at=ph)
    ph.close()
    ph = phase()
    hlo_out1, wsp_out1 = under(("hlo_out1", [P, KD, LAT], F32R), ("wsp_out1", [P, 2, 2, UNIT], F32R))
    pp = sb("pp", [P, 2, 2, FW], at=ph)
    dab = sb("dab", [P, 2, LT, 2], at=ph)
    mst = sb("mst", [P, LT * H_M, 6], at=ph)
    mmv = sb("mmv", [P, LT * H_M, 2], at=ph)
    mrs = sb("mrs", [P, LT * H_M], at=ph)
    hf = sb("hfwd", [P, 2, M_DV], at=ph)
    ph.close()
    m1.close()
    ph = phase()
    hhi = sb("hhi", [P, KD, T], F32R, at=ph)
    hlo = sb("hlo", [P, KD, T], F32R, at=ph)
    uhi = sb("uhi", [P, 8, T], F32R, at=ph)
    ulo = sb("ulo", [P, 8, T], F32R, at=ph)
    whi = sb("whi", [P, RING, UNIT], F32R, at=ph)
    wlo = sb("wlo", [P, RING, UNIT], F32R, at=ph)
    sg = sb("sg", [P, 2, T], at=ph)
    hu = sb("hu", [P, 2, T], at=ph)
    ph.close()
    ph = phase()
    orow = sb("orow", [P, LT, D], at=ph)
    ph.close()

    PS = [es.enter_context(nc.psum_tensor(f"ps{i}", [P, 1024], F32)) for i in range(4)]

    def half(i):
        return PS[i // 2][:, 512 * (i % 2):512 * (i % 2) + 512]


    N_IN0, N_OUT, N_FFN, N_IN1 = 22, KD, sum(2 * nj + KD for _, nj in THIRDS), 24
    STAGES = (("mod00", KD), ("mod01", KD), ("mod02", KD), ("in0", N_IN0), ("mod03", KD), ("mod10", KD), ("out0", N_OUT),
              ("mod04", KD), ("mod05", KD), ("ffn0", N_FFN), ("mod11", KD), ("mod12", KD), ("in1", N_IN1), ("mod13", KD),
              ("out1", N_OUT), ("mod14", KD), ("mod15", KD), ("ffn1", N_FFN))
    NB = {}
    UB = {}
    SB = {}
    freed_by = []
    u = v = 0
    for stage, count in STAGES:
        NB[stage], UB[stage], SB[stage] = len(freed_by), u, v
        for _ in range(count):
            if stage.startswith("mod"):
                freed_by.append((True, u))
            else:
                freed_by.append((False, v))
                v += 1
            if not stage.startswith("ffn"):
                u += 1
    MOD_AT = {}
    for stage, _ in STAGES:
        if stage.startswith("mod"):
            MOD_AT[int(stage[3]), int(stage[4])] = len(MOD_AT) + 1
    FB = (SB["ffn0"], SB["ffn1"])
    FT = (0, N_FFN)
    JB = (0, FC)
    ZB = (0, KD + 3 * KD)
    NT = (T, LAT)
    SEGS = (((0, LAT, 0), (LAT, T, 1)), ((0, LAT, 0),))
    ALL_SEGS = SEGS[0]
    H_CREDIT = 2
    TILE_CREDIT = 2

    def view(slot, k):
        return ring[:, slot, :].rearrange("p (k n) -> p k n", k=k)

    landed = [sem(f"landed{i}") for i in range(RING)]
    consts_in, tabs_in, x_in, wq_in, wkv_in, gate_in = (sem(s) for s in ("consts_in", "tabs_in", "x_in", "wq_in", "wkv_in", "gate_in"))
    unit_done = sem("unit_done")
    vec_T, vec_ev, scol_ok, xT_mm, xT_ev = (sem(s) for s in ("vec_T", "vec_ev", "scol_ok", "xT_mm", "xT_ev"))
    mod_row, mod_T = sem("mod_row"), sem("mod_T")
    mod_ev = sem("mod_ev")
    hmod, hmod_lo, xa_done, fh_hi, fh_lo = (sem(s) for s in ("hmod", "hmod_lo", "xa_done", "fh_hi", "fh_lo"))
    ip_ev, sq_made, rms_mm, rms_ln, rms_ready, cq_norm = (sem(s) for s in ("ip_ev", "sq_made", "rms_mm", "rms_ln", "rms_ready", "cq_norm"))
    rope_mm, rope_ev, rope_done, rg_ready = (sem(s) for s in ("rope_mm", "rope_ev", "rope_done", "rg_ready"))
    strip_in, strip_exp = sem("strip_in"), sem("strip_exp")
    ret_s, ret_p, ret_o, ret_var, ret_rstd, ret_nrm = (sem(s) for s in ("ret_s", "ret_p", "ret_o", "ret_var", "ret_rstd", "ret_nrm"))
    mp_mm, mp_ev, mrope_mm, mrope_ev, mrope_done, kr_cp = (sem(s) for s in ("mp_mm", "mp_ev", "mrope_mm", "mrope_ev", "mrope_done", "kr_cp"))
    att_s, att_nmx, att_exp, att_t, att_tA, att_tB, att_o, att_n = (sem(s) for s in ("att_s", "att_nmx", "att_exp", "att_t", "att_tA", "att_tB", "att_o", "att_n"))
    oT_mm, oT_hi, oT_ev, z_ev = sem("oT_mm"), sem("oT_hi"), sem("oT_ev"), sem("z_ev")
    ln_sq, ln_sum1, ln_sum2, ln_mm, ln_mean, ln_var, ln_rstd, ln_norm, x_new = (sem(s) for s in ("ln_sq", "ln_sum1", "ln_sum2", "ln_mm", "ln_mean", "ln_var", "ln_rstd", "ln_norm", "x_new"))
    hi_made, lo_made, ffn_tile, silu_done, h_done, uhi_done, ulo_done = (sem(s) for s in ("hi_made", "lo_made", "ffn_tile", "silu_done", "h_done", "uhi_done", "ulo_done"))
    gate_w, gate_mm, gate_ev, f_ev, conv_done, silu_ev, vg_ev, pad_ok = (sem(s) for s in ("gate_w", "gate_mm", "gate_ev", "f_ev", "conv_done", "silu_ev", "vg_ev", "pad_ok"))
    ls_in, ls_ln, rows_ok, floor_in, floor_ok, tr_mm, tr_ev = (sem(s) for s in ("ls_in", "ls_ln", "rows_ok", "floor_in", "floor_ok", "tr_mm", "tr_ev"))
    nm_mm, ms_mm, mexp, msel, mp_done, mo_mm, mh_ev, mvar, mrstd, mn_done = (sem(s) for s in ("nm_mm", "ms_mm", "mexp", "msel", "mp_done", "mo_mm", "mh_ev", "mvar", "mrstd", "mn_done"))
    eps_ok, ones_ok = sem("eps_ok"), sem("ones_ok")
    out_mm, out_ev, out_st = sem("out_mm"), sem("out_ev"), sem("out_st")
    dve_step, act_step, pool_step = sem("dve_step"), sem("act_step"), sem("pool_step")

    F_COLS = [0, P, 2 * P, 3 * P, 4 * P, C_KR] + [C_RQ + P * i for i in range(4)] + [C_RK + P * i for i in range(4)]
    NF = len(F_COLS)
    RET_TILES = [(j, 0) for j in range(TT)] + [(j, 1) for j in range(LT, TT)]

    def ret_off(j, seg):
        return j * LAT if seg == 0 else TT * LAT + (j - LT) * CTX

    def m_range(j, d):
        if j >= LT:
            return 0, LAT
        return (P * j, LAT) if d == 0 else (0, P * (j + 1))

    M_OFF = [[], []]
    for d in range(2):
        at = 0
        for j in range(TT):
            M_OFF[d].append(at)
            at += m_range(j, d)[1] - m_range(j, d)[0]
    assert at == FW
    M_SCALE, R_SCALE, A_SCALE = M_DK ** -0.5, RET_D ** -0.5, DQ ** -0.5
    N_ATT = H_MLA * TT

    def op_pair(i):
        return PS[(i + 1) % 4]

    def lat_items(it):
        return (it // TT) * LT + min(it % TT + 1, LT)

    block = es.enter_context(nc.Block())

    @block.sync
    def _(sp):
        def unit(n, dst, src):
            sp.dma_start(dst, src).then_inc(landed[n % RING], 16)

        def slot_free(n):
            if n >= RING:
                direct, i = freed_by[n - RING]
                sp.wait_ge(unit_done if direct else lo_made, i + 1)

        def mod_units(l, g):
            for k in range(KD):
                n = NB[f"mod{l}{g}"] + k
                slot_free(n)
                unit(n, ring[:, n % RING, :], mod_w[l, k * P:(k + 1) * P, g * D:(g + 1) * D])

        for g in range(3):
            mod_units(0, g)
        w_in = ab_w_in[0].rearrange("(k p) n -> p k n", p=P)
        for f, c0 in enumerate(F_COLS):
            n, w = NB["in0"] + f, P
            if c0 == C_KR:
                c0, w = C_KR - NOPE, DQ
            slot_free(n)
            unit(n, view(n % RING, KD)[:, :, 0:w], w_in[:, :, c0:c0 + w])
        for i in range(8):
            n, c0 = NB["in0"] + NF + i, (C_RV, C_RG)[i // 4]
            slot_free(n)
            unit(n, view(n % RING, 2), w_in[:, 2 * (i % 4):2 * (i % 4) + 2, c0:c0 + 512])
        sp.wait_ge(unit_done, UB["in0"] + N_IN0)
        sp.dma_start(wukv[:, :, :], mla_w_ukv[0].rearrange("(k p) n -> p k n", p=P)).then_inc(wkv_in, 16)
        mod_units(0, 3)
        mod_units(1, 0)
        w_out = ab_w_out[0].rearrange("(k p) n -> p k n", p=P)
        for m in range(KD):
            n = NB["out0"] + m
            slot_free(n)
            unit(n, view(n % RING, KD), w_out[:, :, m * P:(m + 1) * P])
        mod_units(0, 4)
        mod_units(0, 5)

        def ffn_units(l):
            first = NB[f"ffn{l}"]
            w_up = ffn_w_in[l].rearrange("(k p) n -> p k n", p=P)
            w_dn = ffn_w_out[l].rearrange("(k p) n -> p k n", p=P)

            U = FB[l]
            for third, (j0, nj) in enumerate(THIRDS):
                start = 0
                if third == 0:
                    for s in range(4):
                        slot_free(first + s)
                        c0 = (j0 + s // 2) * P + (s % 2) * D_FF
                        n = (first + s) % RING
                        unit(n, view(n, KD), w_up[:, :, c0:c0 + P])
                    start = 1
                with sp.Fori(start, nj // 2) as it:
                    for s in range(4):
                        sp.wait_ge(lo_made, it * 4 + (U + s - RING + 1))
                        n = (first + s) % RING
                        unit(n, view(n, KD), w_up[:, :, bass.ds(it * (2 * P) + ((j0 + s // 2) * P + (s % 2) * D_FF), P)])
                U += 2 * nj
                with sp.Fori(0, 2) as it:
                    for s in range(4):
                        sp.wait_ge(lo_made, it * 4 + (U + s - RING + 1))
                        n = (first + s) % RING
                        dst = ring[:, n, 0:nj * P].rearrange("p (k n) -> p k n", k=nj)
                        unit(n, dst, w_dn[:, j0:j0 + nj, bass.ds(it * (4 * P) + s * P, P)])
                U += KD

        ffn_units(0)
        mod_units(1, 1)
        mod_units(1, 2)
        w_in = m_w_in[0].rearrange("(k p) n -> p k n", p=P)
        for i in range(N_IN1):
            n = NB["in1"] + i
            slot_free(n)
            if i < 8:
                unit(n, view(n % RING, KD), w_in[:, :, i * P:(i + 1) * P])
            elif i >= 16:
                unit(n, ring[:, n % RING, :], w_in[:, i - 16, C_MO:C_MO + H_M * M_DV])
            else:
                g, q = (i - 8) // 4, (i - 8) % 4
                unit(n, view(n % RING, 2), w_in[:, 2 * q:2 * q + 2, C_MV + g * 512:C_MV + (g + 1) * 512])
        mod_units(1, 3)
        w_out = m_w_out[0].rearrange("(k p) n -> p k n", p=P)
        for m in range(KD):
            n = NB["out1"] + m
            slot_free(n)
            unit(n, view(n % RING, KD), w_out[:, :, m * P:(m + 1) * P])
        mod_units(1, 4)
        mod_units(1, 5)
        ffn_units(1)
        for t in range(LT):
            sp.wait_ge(out_ev, t + 1)
            sp.dma_start(out[0, t * P:(t + 1) * P, :], orow[:, t, :]).then_inc(out_st, 16)
        sp.wait_ge(out_st, 16 * LT)

    @block.tensor
    def _(pe):
        pe.sem_inc(ffn_tile, TILE_CREDIT)

        def loaded(n):
            pe.wait_ge(landed[n % RING], 16 * (n // RING + 1))

        pe.wait_ge(consts_in, 16 * 13)
        pe.transpose(half(0)[:, 0:96], brow[0:96, :], ident[0:96, 0:96])
        pe.transpose(half(1)[:, 0:V_ROWS], vrow[0:V_ROWS, :], ident[0:V_ROWS, 0:V_ROWS]).then_inc(vec_T, 1)
        pe.wait_ge(x_in, 16 * 2)
        for k in range(KD):
            b = 1 + k % 2
            if k >= 2:
                pe.wait_ge(xT_ev, k - 1)
            for t in range(TT):
                mm = pe.transpose(PS[b][:, t * P:(t + 1) * P], xin[:, t, k * P:(k + 1) * P], ident)
            mm.then_inc(xT_mm, 1)

        s_kv = scol[:, :].rearrange("p (v k) -> p k v", v=2)

        def mod_rows(l, g, pair, first=0, end=KD):
            for k in range(first, end):
                n = NB[f"mod{l}{g}"] + k
                loaded(n)
                for b in range(2):
                    mm = pe.matmul(pair[0:2, 512 * b:512 * (b + 1)], s_kv[:, k, :], ring[:, n % RING, 512 * b:512 * (b + 1)],
                                   start=(k == 0), stop=(k == KD - 1))
                mm.then_inc(unit_done, 1)

        def mod_columns(l, g, pair):
            pe.wait_ge(mod_row, MOD_AT[l, g])
            for b in range(KD):
                mm = pe.transpose(pair[:, 2 * b:2 * b + 2], mrow[0:2, b * P:(b + 1) * P], ident[0:2, 0:2])
            mm.then_inc(mod_T, 1)

        pe.wait_ge(scol_ok, 1)
        mod_rows(0, 0, PS[3])
        pe.wait_ge(xT_ev, 1)
        mod_rows(0, 1, PS[0], 0, 4)
        mod_columns(0, 0, PS[3])
        mod_rows(0, 1, PS[0], 4, KD)
        pe.wait_ge(mod_ev, 1)
        mod_rows(0, 2, PS[3], 0, 1)
        mod_columns(0, 1, PS[0])
        mod_rows(0, 2, PS[3], 1, KD)

        def three(dst, hi_lo_pairs, first, last):
            (s_hi, m_hi), (s_lo, m_lo) = hi_lo_pairs
            pe.matmul(dst, s_hi, m_hi, start=first, stop=False)
            pe.matmul(dst, s_hi, m_lo, start=False, stop=False)
            return pe.matmul(dst, s_lo, m_hi, start=False, stop=last)

        def split_unit(stage, i):
            pe.wait_ge(lo_made, SB[stage] + i + 1)

        def project(dst, w_hi, w_lo, h_hi, h_lo, first, last, segs):
            for w, h, st, sp_ in ((w_hi, h_hi, first, False), (w_hi, h_lo, False, False), (w_lo, h_hi, False, last)):
                for a, b, _ in segs:
                    mm = pe.matmul(dst[:, a:b], w, h[:, a:b], start=st, stop=sp_)
            return mm

        def rotate(r, bank, mat, src, lo, hi, done, evac):
            if r >= 2:
                pe.wait_ge(evac, r - 1)
            pe.matmul(bank[lo:hi, :], mat[lo:hi, lo:hi], src, start=True, stop=True).then_inc(done, 1)

        def rms_sums(first, count):
            for c in range(first, first + count):
                for a, b, _ in ALL_SEGS:
                    mm = pe.matmul(PS[3][:, a:b], ones, sqb[:, c % 3, a:b], start=(c == first), stop=(c == first + count - 1))
            mm.then_inc(rms_mm, 1)

        def rot_source(f):
            if f == 5:
                return krope[NOPE:DQ, 0:LAT]
            return rq[:, f - 6, 0:LAT] if f < 10 else rk[:, f - 10, 0:LAT]

        def feature_chunk(f, ks):
            hi = DQ if f == 5 else P
            split_unit("in0", f)
            for k in ks:
                if f < 2:
                    pe.wait_ge(hmod_lo, k + 1)
                w_hi, w_lo = (wsp_in0[:, a, f % 2, k * P:k * P + hi] for a in range(2))
                mm = project(PS[f % 3][0:hi, :], w_hi, w_lo, hx[:, 0, k, :], hx[:, 1, k, :], k == 0, k == KD - 1, ALL_SEGS)
            if k == KD - 1:
                mm.then_inc(unit_done, 1)

        for f in range(NF):
            if f >= 3:
                pe.wait_ge(ip_ev, f - 2)
            if f == 0:
                for k in range(KD):
                    feature_chunk(0, (k,))
                    feature_chunk(1, (k,))
            elif f >= 2:
                feature_chunk(f, range(KD))
            if f == 3:
                mod_columns(0, 2, PS[3])
                pe.wait_ge(mod_ev, MOD_AT[0, 2])
                pe.wait_ge(sq_made, 3)
                rms_sums(0, KQ)
            if f == 5:
                pe.wait_ge(sq_made, 5)
                pe.wait_ge(rms_ln, 1)
                rms_sums(KQ, KKV)
            if f == 6:
                pe.wait_ge(rms_ln, 2)
                pe.wait_ge(ip_ev, 6)
                pe.wait_ge(tabs_in, 16 * 4)
                rotate(0, half(6), rot_mla, rot_source(5), NOPE, DQ, rope_mm, rope_ev)
            if f >= 7:
                pe.wait_ge(ip_ev, f)
                rotate(f - 6, half(6 + (f - 6) % 2), rot_ret, rot_source(f - 1), 0, P, rope_mm, rope_ev)

        def token_major(stage, i0, banks, wsp, h_hi, h_lo, ready):
            for q in range(4):
                i = i0 + q
                split_unit(stage, i)
                for k in (2 * q, 2 * q + 1):
                    w_hi, w_lo = (wsp[a][:, i % 2, 512 * (k % 2):512 * (k % 2) + 512] for a in range(2))
                    for t, b in banks:
                        if k == 0:
                            ready(b)
                        cols = slice(t * P, (t + 1) * P)
                        mm = three(half(b), ((h_hi[:, k, cols], w_hi), (h_lo[:, k, cols], w_lo)), k == 0, k == KD - 1)
                mm.then_inc(unit_done, 1)

        in0_parts = ((wsp_in0[:, 0], wsp_in0[:, 1]), hx[:, 0], hx[:, 1])
        token_major("in0", NF, [(0, 0), (1, 1), (4, 4), (5, 5), (2, 2), (3, 3)], *in0_parts,
                    lambda b: pe.wait_ge(ip_ev, NF if b in (2, 3) else NF - 1))
        rotate(8, half(6), rot_ret, rot_source(13), 0, P, rope_mm, rope_ev)

        def rg_ready_for(b):
            if b < 4:
                pe.wait_ge(ip_ev, NF + 1 + b // 2)
            else:
                pe.wait_ge(rope_ev, 9)

        token_major("in0", NF + 4, [(0, 0), (1, 1), (2, 2), (3, 3), (4, 6), (5, 7)], *in0_parts, rg_ready_for)

        def ret_scores(h):
            pe.wait_ge(rope_done, 6 + h)
            for i, (j, seg) in enumerate(RET_TILES):
                s = 8 * h + i
                if s >= 4:
                    pe.wait_ge(ret_p, s - 3)
                else:
                    pe.wait_ge(rg_ready, 2)
                a, b, _ = ALL_SEGS[seg]
                pe.matmul(half(s % 4)[:, 0:b - a], rk[:, h, j * P:(j + 1) * P], rq[:, h, a:b],
                          start=True, stop=True).then_inc(ret_s, 1)

        def ret_values(h):
            pe.wait_ge(ret_p, 8 * h + 8)
            if h >= 2:
                pe.wait_ge(ret_nrm, h - 1)
            else:
                pe.wait_ge(rg_ready, 3)
                pe.wait_ge(mod_ev, MOD_AT[0, 3])
            for t in range(TT):
                seg = 0 if t < LT else 1
                bank = half(4 + 2 * (h % 2) + seg)
                js = [j for j, s in RET_TILES if s == seg]
                tq = (t - LT * seg) * P
                for j in js:
                    mm = pe.matmul(bank[:, tq:tq + P], pt[:, h % 2, ret_off(j, seg) + tq:ret_off(j, seg) + tq + P],
                                   rv[:, j, h * P:(h + 1) * P], start=(j == js[0]), stop=(j == js[-1]))
            mm.then_inc(ret_o, 1)

        pe.wait_ge(ip_ev, NF + 3)
        mod_rows(0, 3, PS[2])
        ret_scores(0)
        mod_columns(0, 3, PS[2])
        for h in range(1, H_RET):
            ret_scores(h)
            ret_values(h - 1)
        ret_values(H_RET - 1)

        pe.wait_ge(ret_p, 8 * H_RET)
        pe.wait_ge(ret_nrm, 3)
        pe.wait_ge(wq_in, 16)
        pe.wait_ge(cq_norm, 5)
        for m in range(19):
            pair = PS[m % 3]
            if m >= 3:
                pe.wait_ge(mp_ev, m - 2)
            if m < 8:
                for k in range(KQ):
                    for a, b, _ in ALL_SEGS:
                        mm = pe.matmul(pair[0:DQ, a:b], wuq[:, k, m * DQ:(m + 1) * DQ], cqkv[:, k, a:b],
                                       start=(k == 0), stop=(k == KQ - 1))
            elif m < 16:
                h = m - 8
                if h == 0:
                    pe.wait_ge(wkv_in, 16)
                for k in range(KKV):
                    for a, b, _ in ALL_SEGS:
                        mm = pe.matmul(pair[0:NOPE, a:b], wukv[:, k, h * P:h * P + NOPE], cqkv[:, KQ + k, a:b],
                                       start=(k == 0), stop=(k == KKV - 1))
            else:
                for i in range(2):
                    t = 2 * (m - 16) + i
                    dst = pair[:, 512 * i:512 * i + 512].rearrange("p (h d) -> p h d", h=H_MLA)
                    for k in range(KKV):
                        w = wukv[:, k, :].rearrange("p (h d) -> p h d", h=H_MLA)[:, :, NOPE:NOPE + MLA_V]
                        mm = pe.matmul(dst, cqkv[:, KQ + k, t * P:(t + 1) * P], w, start=(k == 0), stop=(k == KKV - 1))
            mm.then_inc(mp_mm, 1)
            if 1 <= m <= 8:
                h = m - 1
                pe.wait_ge(mp_ev, h + 1)
                if h == 0:
                    pe.wait_ge(ret_nrm, 4)
                rotate(h, half(6 + h % 2), rot_mla, qh[NOPE:DQ, h, 0:LAT], NOPE, DQ, mrope_mm, mrope_ev)

        def att_scores(it):
            h, t = divmod(it, TT)
            if it >= 2:
                pe.wait_ge(att_exp, it - 1)
            else:
                pe.wait_ge(mp_ev, 19)
            if t == 0:
                pe.wait_ge(mrope_done, h + 1)
                pe.wait_ge(kr_cp, h + 1)
            for a, b, _ in (ALL_SEGS if t < LT else ALL_SEGS[1:]):
                mm = pe.matmul(PS[it % 2][:, a:b], qh[0:DQ, h, t * P:(t + 1) * P], kh[0:DQ, h, a:b], start=True, stop=True)
            mm.then_inc(att_s, 1)

        def att_transpose(it):
            t = it % TT
            pe.wait_ge(att_exp, it + 1)
            if it >= 1:
                pe.wait_ge(att_tA, lat_items(it - 1))
                pe.wait_ge(att_tB, it)
            for j in range(0 if t < LT else LT, TT):
                mm = pe.transpose(PS[2][:, j * P:(j + 1) * P], pa[:, it % 2, j * P:(j + 1) * P], ident)
            mm.then_inc(att_t, 1)

        def att_values(it):
            h, t = divmod(it, TT)
            pe.wait_ge(att_tA, lat_items(it))
            pe.wait_ge(att_tB, it + 1)
            if it >= 2:
                pe.wait_ge(att_n, it - 1)
            j0 = 0 if t < LT else LT
            for j in range(j0, TT):
                mm = pe.matmul(half(6 + it % 2)[:, 0:MLA_V], paT[:, it % 2, j * P:(j + 1) * P],
                               va[:, j, h * MLA_V:(h + 1) * MLA_V], start=(j == j0), stop=(j == TT - 1))
            mm.then_inc(att_o, 1)

        for i in range(N_ATT + 2):
            if i < N_ATT:
                att_scores(i)
            if 1 <= i <= N_ATT:
                att_transpose(i - 1)
            if i >= N_ATT:
                q = (i - N_ATT) * 4
                mod_rows(1, 0, PS[0], q, q + 4)
            if i >= 2:
                att_values(i - 2)

        def out_projection(l, source, h_hi, h_lo, wsp):
            for c in range(KD):
                if c >= 4:
                    pe.wait_ge(oT_ev, KD * l + c - 3)
                elif c == 1 and l == 0:
                    mod_columns(1, 0, PS[0])
                    pe.wait_ge(mod_ev, MOD_AT[1, 0])
                for t in range(NT[l] // P):
                    mm = pe.transpose(op_pair(c)[:, t * P:(t + 1) * P], source(c, t), ident)
                mm.then_inc(oT_mm, 1)
            for m in range(KD):
                if m < 4:
                    pe.wait_ge(oT_ev, KD * l + 5 + m)
                else:
                    pe.wait_ge(z_ev, ZB[l] + m - 3)
                split_unit(f"out{l}", m)
                for k in range(KD):
                    if m == 0:
                        pe.wait_ge(oT_ev, KD * l + k + 1)
                    w_hi, w_lo = (wsp[:, a, m % 2, k * P:(k + 1) * P] for a in range(2))
                    mm = project(op_pair(m), w_hi, w_lo, h_hi[:, k, :], h_lo[:, k, :], k == 0, k == KD - 1, SEGS[l])
                mm.then_inc(unit_done, 1)

        def ln_with_mod(i, z, la, ga, lb, gb_):
            pe.wait_ge(z_ev, z - 1)
            mod_rows(la, ga, PS[2], 0, 3)
            ln_sums(i)
            mod_rows(la, ga, PS[2], 3, KD)
            pe.wait_ge(z_ev, z)
            mod_rows(lb, gb_, PS[3], 0, 3)
            mod_columns(la, ga, PS[2])
            mod_rows(lb, gb_, PS[3], 3, KD)
            mod_columns(lb, gb_, PS[3])
            pe.wait_ge(mod_ev, MOD_AT[lb, gb_])

        def ln_sums(i):
            l = i // 2
            for q, (src, ready, count) in enumerate(((s1, ln_sum1, i + 1), (s2, ln_sum2, KD * (i + 1)))):
                pe.wait_ge(ready, count)
                for a, b, _ in SEGS[l]:
                    mm = pe.matmul(PS[q][:, a:b], ones, src[:, a:b], start=True, stop=True)
                mm.then_inc(ln_mm, 1)

        def ffn(l):
            U, J = FB[l], JB[l]
            z0 = ZB[l] + KD
            for third, (j0, nj) in enumerate(THIRDS):
                def tile(s, k, hi, lo, last):
                    return project(PS[s], whi[:, s, k * P:(k + 1) * P], wlo[:, s, k * P:(k + 1) * P], hi, lo, k == 0, last, SEGS[l])

                with pe.Fori(0, nj // 2) as it:
                    for s in range(4):
                        if s % 2 == 0:
                            if third:
                                pe.wait_ge(z_ev, z0 + KD * third - 2 + s)
                            pe.wait_ge(h_done, it * 2 + (J + s // 2 - 1 + H_CREDIT))
                        pe.wait_ge(lo_made, it * 4 + (U + s + 1))
                        for k in range(KD):
                            if third == 0 and s == 0:
                                pe.wait_ge(fh_lo, KD * l + k + 1)
                            mm = tile(s, k, hhi[:, k, :], hlo[:, k, :], k == KD - 1)
                        mm.then_inc(ffn_tile, 1)
                U += 2 * nj
                with pe.Fori(0, 2) as it:
                    for s in range(4):
                        if s < 2:
                            pe.wait_ge(h_done, J + nj - 1 + s + H_CREDIT)
                        pe.wait_ge(z_ev, it * 4 + (z0 + KD * third + s - 3))
                        pe.wait_ge(lo_made, it * 4 + (U + s + 1))
                        for k in range(nj):
                            if s == 0:
                                pe.wait_ge(ulo_done, J + k + 1)
                            mm = tile(s, k, uhi[:, k, :], ulo[:, k, :], k == nj - 1)
                        mm.then_inc(ffn_tile, 1)
                U += KD
                J += nj

        pe.wait_ge(att_n, N_ATT)
        out_projection(0, lambda c, t: att[:, t, c * P:(c + 1) * P] if c < 4 else rg[:, t, (c - 4) * P:(c - 3) * P],
                       hx[:, 0], hx[:, 1], wsp_out0)
        ln_with_mod(0, KD, 0, 4, 0, 5)
        ffn(0)
        ln_with_mod(1, ZB[1], 1, 1, 1, 2)

        def m_chunk(f, k):
            w_hi, w_lo = (w[:, f % 2, k * P:(k + 1) * P] for w in (whi1, wlo1))
            return project(PS[f % 3], w_hi, w_lo, hT1[:, k, :], hlo1[:, k, :], k == 0, k == KD - 1,
                           ALL_SEGS if f >= 4 else ALL_SEGS[:1])

        pe.wait_ge(gate_w, 6)
        for k in range(KD):
            pe.wait_ge(hmod_lo, KD + k + 1)
            mm = project(PS[3], wg[:, 0, k, :], wg[:, 1, k, :], hT1[:, k, :], hlo1[:, k, :], k == 0, k == KD - 1, ALL_SEGS)
            if k == KD - 1:
                mm.then_inc(gate_mm, 1)
            for f in range(2):
                if k == 0:
                    split_unit("in1", f)
                mm = m_chunk(f, k)
                if k == KD - 1:
                    mm.then_inc(unit_done, 1)
        for f in range(2, 8):
            if f >= 3:
                pe.wait_ge(f_ev, f - 2)
            split_unit("in1", f)
            for k in range(KD):
                mm = m_chunk(f, k)
            mm.then_inc(unit_done, 1)
        in1_parts = ((whi1, wlo1), hT1, hlo1)
        token_major("in1", 8, [(t, t) for t in (4, 5, 0, 1, 2, 3)], *in1_parts, lambda b: pe.wait_ge(f_ev, (7, 8, 6)[b // 2]))
        v1 = {3: lambda: pe.wait_ge(gate_ev, 4), 0: lambda: pe.wait_ge(vg_ev, 1), 1: lambda: pe.wait_ge(vg_ev, 2)}
        token_major("in1", 12, [(0, 6), (1, 7), (2, 0), (3, 1), (4, 2), (5, 3)], *in1_parts, lambda b: v1[b // 2]())
        for k in range(KD):
            split_unit("in1", 16 + k)
            for b in (4, 5, 6, 7, 0, 1, 2, 3):
                if k == 0:
                    pe.wait_ge(vg_ev, {2: 3, 3: 4, 0: 5, 1: 6}[b // 2])
                cols, c0 = slice((b // 2) * P, (b // 2 + 1) * P), 512 * (b % 2)
                mm = three(half(b), ((hT1[:, k, cols], whi1[:, k % 2, c0:c0 + 512]), (hlo1[:, k, cols], wlo1[:, k % 2, c0:c0 + 512])),
                           k == 0, k == KD - 1)
            mm.then_inc(unit_done, 1)

        pe.wait_ge(vg_ev, 7)
        mod_rows(1, 3, PS[2])
        pe.wait_ge(vg_ev, 8)
        pe.wait_ge(rows_ok, 1)
        for d in range(2):
            for t in range(TT):
                at = (d * TT + t) * H_M
                pe.transpose(half(6)[:, at:at + H_M], li[0:H_M, d, t * P:(t + 1) * P], ident[0:H_M, 0:H_M])
        pe.wait_ge(floor_ok, 1)
        for d in range(2):
            for t in range(LT):
                at = (2 * TT + d * LT + t) * H_M
                mm = pe.transpose(half(6)[:, at:at + H_M], gbc[0:H_M, d, t * P:(t + 1) * P], ident[0:H_M, 0:H_M])
        mm.then_inc(tr_mm, 1)

        def m_scores(h):
            if h == 0:
                pe.wait_ge(vg_ev, 10)
                pe.wait_ge(silu_ev, 8)
            else:
                pe.wait_ge(mexp, 12 * h)
            for d in range(2):
                mm = pe.matmul(half(d), selr[0:H_M, h * P:(h + 1) * P], negm[0:H_M, d, :], start=True, stop=True)
            mm.then_inc(nm_mm, 1)
            b = M_DK * (h % 2)
            for j in range(TT):
                s = TT * h + j
                if s >= 4:
                    pe.wait_ge(mp_done, 2 * (s - 3))
                pe.matmul(half(2 + s % 4), mk[b:b + M_DK, h // 2, j * P:(j + 1) * P], mq[b:b + M_DK, h // 2, :],
                          start=True, stop=True).then_inc(ms_mm, 1)

        def m_values(h):
            pe.wait_ge(mp_done, 12 * (h + 1))
            for t in range(LT):
                i = LT * h + t
                if i >= 2:
                    pe.wait_ge(mh_ev, i - 1)
                else:
                    pe.wait_ge(tr_ev, 2)
                for d in range(2):
                    js = [j for j in range(TT) if j >= LT or (j <= t if d == 0 else j >= t)]
                    for j in js:
                        at = M_OFF[d][j] + t * P - m_range(j, d)[0]
                        mm = pe.matmul(half(6 + i % 2)[:, d * (M_DV + 1):(d + 1) * (M_DV + 1)],
                                       pp[:, h % 2, d, at:at + P], mv[:, j, h, :], start=(j == js[0]), stop=(j == js[-1]))
                mm.then_inc(mo_mm, 1)

        mod_columns(1, 3, PS[2])
        pe.wait_ge(mod_ev, MOD_AT[1, 3])
        m_scores(0)
        for h in range(1, H_M):
            m_scores(h)
            m_values(h - 1)
        m_values(H_M - 1)
        pe.wait_ge(mn_done, 1)
        out_projection(1, lambda c, t: mo[:, t, c * P:(c + 1) * P], hT1, hlo_out1, wsp_out1)
        ln_with_mod(2, ZB[1] + KD, 1, 4, 1, 5)
        ffn(1)
        ln_sums(3)
        pe.wait_ge(ln_rstd, 4)
        for t in range(LT):
            for k in range(KD):
                if t == 0:
                    pe.wait_ge(x_new, 3 * KD + k + 1)
                mm = pe.transpose(PS[t][:, k * P:(k + 1) * P], xT[:, k, t * P:(t + 1) * P], ident)
            mm.then_inc(out_mm, 1)

    @block.scalar
    def _(act):
        steps = 0

        def step(ins):
            nonlocal steps
            steps += 1
            ins.then_inc(act_step, 1)
            act.wait_ge(act_step, steps)

        rows = [(c[0], V_C, 8), (c_ctx, V_CC, 8), (ln_g.rearrange("l s n -> (l s n)"), V_LG, 32),
                (ln_b.rearrange("l s n -> (l s n)"), V_LB, 32), (mla_q_norm[0], V_QN, KQ), (mla_kv_norm[0], V_KVN, KKV),
                (m_conv_w[0].rearrange("w n -> (w n)"), V_CW, 24), (m_conv_b[0], V_CB, 8), (m_norm_g[0], V_NG, 8)]
        act.dma_start(kc[:, :], consts[:, 0:K_BASE]).then_inc(consts_in, 16)
        for src, at, nr in rows:
            act.dma_start(vrow[at:at + nr, :], src.rearrange("(r n) -> r n", n=P)).then_inc(consts_in, 16)
        for l in range(DEPTH):
            act.dma_start(brow[48 * l:48 * l + 48, :], mod_b[l].rearrange("(r n) -> r n", n=P)).then_inc(consts_in, 16)
        act.dma_start(vrow[V_ROWS:P, :], consts[V_ROWS:P, 0:P]).then_inc(consts_in, 16)
        act.dma_start(xin[:, 0:LT, :], x[0].rearrange("(t p) n -> p t n", p=P)).then_inc(x_in, 16)
        act.dma_start(xin[:, LT:TT, :], ctx[0].rearrange("(t p) n -> p t n", p=P)).then_inc(x_in, 16)
        act.wait_ge(vec_ev, 1)
        act.activation(scol[:, :], vcol[:, V_C:V_C + 16], ACT.Silu).then_inc(scol_ok, 1)
        act.wait_ge(xT_mm, KD)
        act.dma_start(cosR[:, :, :], consts[:, K_COSR:K_COSR + 2 * LAT].rearrange("p (a t) -> p a t", a=2)).then_inc(tabs_in, 16)
        act.dma_start(cosM[:, :, :], consts[:, K_COSM:K_COSM + 2 * LAT].rearrange("p (a t) -> p a t", a=2)).then_inc(tabs_in, 16)
        act.dma_start(rel[:, :], consts[:, K_REL:K_REL + REL_W]).then_inc(tabs_in, 16)
        act.dma_start(lgc[:, 0, :], ret_log_decay[0].rearrange("a h -> (a h)").partition_broadcast(P)).then_inc(tabs_in, 16)
        act.dma_start(wuq[:, :, :], mla_w_uq[0].rearrange("(k p) n -> p k n", p=P)).then_inc(wq_in, 16)

        def modulate(l, hT, x_sem, x0):
            act.wait_ge(mod_ev, MOD_AT[l, 1])
            for k in range(KD):
                act.wait_ge(x_sem, x0 + k + 1)
                for a, b, v in ALL_SEGS:
                    ins = act.activation(hT[:, k, a:b], xT[:, k, a:b], ACT.Identity, bias=modc[:, l, 0, k, v:v + 1],
                                         scale=modc[:, l, 1, k, v:v + 1])
                ins.then_inc(hmod, 1)

        def split_high(stage, i, w_hi, width=UNIT):
            n = NB[stage] + i
            act.wait_ge(landed[n % RING], 16 * (n // RING + 1))
            if i >= 2:
                act.wait_ge(unit_done, UB[stage] + i - 1)
            act.activation(w_hi[:, i % 2, :], ring[:, n % RING, :], ACT.Copy).then_inc(hi_made, 1)

        modulate(0, hx[:, 0], xT_ev, 0)
        split_high("in0", 0, wsp_in0[:, 0])
        split_high("in0", 1, wsp_in0[:, 0])

        def strips(h):
            b, lgf, lgb = h % 2, h, H_RET + h
            act.wait_ge(strip_in, 2 * h + 1)
            act.activation(strip[:, b, 0:REL_W], strip[:, b, 0:REL_W], ACT.Exp, scale=lgc[:, 0, lgf:lgf + 1])
            act.activation(strip[:, b, REL_W:], rel[:, 0:S2_W], ACT.Exp, scale=lgc[:, 0, lgf:lgf + 1], bias=lgc[:, 2, lgf:lgf + 1])
            act.activation(stripb, stripb, ACT.Exp, scale=lgc[:, 1, lgb:lgb + 1]).then_inc(strip_exp, 1)
            act.wait_ge(strip_in, 2 * h + 2)
            act.activation(stripb[:, 0:S2_W], rel[:, 0:S2_W], ACT.Exp, scale=lgc[:, 1, lgb:lgb + 1],
                           bias=lgc[:, 3, lgb:lgb + 1]).then_inc(strip_exp, 1)

        def inverse_rms(i, k):
            act.wait_ge(rms_mm, i + 1)
            act.activation(rms[:, i, :], PS[3][:, 0:T], ACT.Ln, scale=1.0 / (k * P), bias=epsc[:, :]).then_inc(rms_ln, 1)
            act.wait_ge(rms_ln, i + 1)
            act.activation(rms[:, i, :], rms[:, i, :], ACT.Exp, scale=-0.5).then_inc(rms_ready, 1)

        act.wait_ge(eps_ok, 1)
        for f in range(NF):
            split_high("in0", f + 2, wsp_in0[:, 0])
            src = PS[f % 3][:, 0:T]
            if f < 5:
                if f == 3:
                    act.wait_ge(rms_mm, 1)
                act.activation(sqb[:, f % 3, :], src, ACT.Square).then_inc(sq_made, 1)
                dst = cqkv[:, f, :]
            elif f == 5:
                src, dst = PS[f % 3][NOPE:DQ, 0:T], krope[NOPE:DQ, :]
            else:
                dst = rq[:, f - 6, :] if f < 10 else rk[:, f - 10, :]
            act.activation(dst, src, ACT.Copy).then_inc(ip_ev, 1)
            if f == 3:
                inverse_rms(0, KQ)
            if f == 5:
                inverse_rms(1, KKV)
        strips(0)
        split_high("in0", NF + 2, wsp_in0[:, 0])
        strips(1)
        for i in range(NF + 3, NF + 6):
            split_high("in0", i, wsp_in0[:, 0])
        for i in range(3):
            act.activation(rv[:, 2 * i:2 * i + 2, :], PS[i][:, :].rearrange("p (t d) -> p t d", t=2), ACT.Copy).then_inc(ip_ev, 1)
        for i in range(NF + 6, N_IN0):
            split_high("in0", i, wsp_in0[:, 0])
        act.wait_ge(unit_done, UB["in0"] + NF + 8)
        for i, b in enumerate((0, 1, 3)):
            act.activation(rg[:, 2 * i:2 * i + 2, :], PS[b][:, :].rearrange("p (t d) -> p t d", t=2), ACT.Silu).then_inc(rg_ready, 1)

        def ret_inverse_std(h):
            act.wait_ge(ret_var, h + 1)
            step(act.activation(rrs[:, :], rmv[:, :, 1], ACT.Ln, bias=epsc[:, :]))
            act.activation(rrs[:, :], rrs[:, :], ACT.Exp, scale=-0.5).then_inc(ret_rstd, 1)

        strips(2)
        ret_inverse_std(0)
        strips(3)
        for h in range(1, H_RET):
            ret_inverse_std(h)

        act.wait_ge(ret_nrm, H_RET)
        for m in range(19):
            act.wait_ge(mp_mm, m + 1)
            pair = PS[m % 3]
            if m < 8:
                ins = act.activation(qh[0:DQ, m, :], pair[0:DQ, 0:T], ACT.Copy)
            elif m < 16:
                ins = act.activation(kh[0:NOPE, m - 8, :], pair[0:NOPE, 0:T], ACT.Copy)
            else:
                i = m - 16
                ins = act.activation(va[:, 2 * i:2 * i + 2, :], pair[:, :].rearrange("p (t d) -> p t d", t=2), ACT.Copy)
            ins.then_inc(mp_ev, 1)

        def att_exponent(it):
            act.wait_ge(att_nmx, it + 1)
            if it >= 2:
                act.wait_ge(att_t, it - 1)
            a = 0 if it % TT < LT else LAT
            act.activation(pa[:, it % 2, a:T], PS[it % 2][:, a:T], ACT.Exp, bias=nmx[:, 0, it:it + 1], scale=A_SCALE,
                           accum_out=den[:, 0, it:it + 1]).then_inc(att_exp, 1)

        def att_copy(it):
            act.wait_ge(att_t, it + 1)
            if it >= 2:
                act.wait_ge(att_o, it - 1)
            act.activation(paT[:, it % 2, 0:LAT], PS[2][:, 0:LAT], ACT.Copy).then_inc(att_tA, 1)

        for i in range(N_ATT + 1):
            if i < N_ATT:
                att_exponent(i)
            if i >= 1 and (i - 1) % TT < LT:
                att_copy(i - 1)

        def ln_square(i, m):
            l = i // 2
            done = ZB[l] + (KD if i % 2 == 0 else 4 * KD) - KD + m + 1
            act.wait_ge(z_ev, done)
            if KD * i + m >= 2:
                act.wait_ge(ln_sum2, KD * i + m - 1)
            act.activation(sq[:, m % 2, 0:NT[l]], xT[:, m, 0:NT[l]], ACT.Square).then_inc(ln_sq, 1)

        def layer_norm(i):
            l, nt = i // 2, NT[i // 2]
            act.wait_ge(ln_mm, 2 * i + 1)
            act.activation(lnm[:, 0:nt], PS[0][:, 0:nt], ACT.Copy, scale=1.0 / D)
            act.activation(s1[:, 0:nt], PS[0][:, 0:nt], ACT.Square, scale=1.0 / D).then_inc(ln_mean, 1)
            act.wait_ge(ln_var, i + 1)
            step(act.activation(lnr[:, 0:nt], s2[:, 0:nt], ACT.Ln))
            act.activation(lnr[:, 0:nt], lnr[:, 0:nt], ACT.Exp, scale=-0.5).then_inc(ln_rstd, 1)
            for k in range(KD):
                act.wait_ge(ln_norm, KD * i + k + 1)
                g, b = V_LG + KD * i + k, V_LB + KD * i + k
                act.activation(xT[:, k, 0:nt], xT[:, k, 0:nt], ACT.Identity, bias=vcol[:, b:b + 1],
                               scale=vcol[:, g:g + 1]).then_inc(x_new, 1)

        def out_projection(l, hT, w_hi):
            nt = NT[l]
            split_high(f"out{l}", 0, w_hi)
            split_high(f"out{l}", 1, w_hi)
            for c in range(KD):
                act.wait_ge(oT_mm, KD * l + c + 1)
                if l == 0:
                    ins = act.activation(hT[:, c, 0:nt], op_pair(c)[:, 0:nt], ACT.Copy)
                else:
                    ins = act.activation(hT[:, c, 0:nt], op_pair(c)[:, 0:nt], ACT.Copy, scale=vcol[:, V_NG + c:V_NG + c + 1])
                ins.then_inc(oT_hi, 1)
            for m in range(KD):
                if m + 2 < KD:
                    split_high(f"out{l}", m + 2, w_hi)
                ln_square(2 * l, m)
            layer_norm(2 * l)

        def ffn(l):
            nt, first = NT[l], NB[f"ffn{l}"]
            act.wait_ge(mod_ev, MOD_AT[l, 4])
            for k in range(KD):
                act.wait_ge(x_new, KD * 2 * l + k + 1)
                for a, b, v in SEGS[l]:
                    ins = act.activation(hhi[:, k, a:b], xT[:, k, a:b], ACT.Identity, bias=modc[:, l, 3, k, v:v + 1],
                                         scale=modc[:, l, 4, k, v:v + 1])
                ins.then_inc(fh_hi, 1)

            def split(u, s, width, n_of):
                act.wait_ge(landed[(first + s) % RING], n_of)
                if not isinstance(u, int) or u - 3 + TILE_CREDIT > 0:
                    act.wait_ge(ffn_tile, u + (TILE_CREDIT - 3))
                act.activation(whi[:, s, 0:width], ring[:, (first + s) % RING, 0:width], ACT.Copy).then_inc(hi_made, 1)

            def split_static(v, width):
                split(FT[l] + v, v % 4, width, 16 * ((first + v) // RING + 1))

            split_static(0, UNIT)
            split_static(1, UNIT)
            V, J = 0, JB[l]
            for third, (j0, nj) in enumerate(THIRDS):
                def silu(it, jj):
                    act.wait_ge(ffn_tile, it * 4 + (FT[l] + V + 2 * jj + 2 + TILE_CREDIT))
                    act.wait_ge(h_done, it * 2 + (J + jj - 1 + H_CREDIT))
                    act.activation(sg[:, jj, 0:nt], PS[2 * jj + 1][:, 0:nt], ACT.Silu).then_inc(silu_done, 1)

                def high(it, jj):
                    act.wait_ge(h_done, it * 2 + (J + jj + 1 + H_CREDIT))
                    j = it * 2 + jj
                    dst = uhi[:, j, 0:nt] if isinstance(it, int) else uhi[:, bass.ds(j, 1), 0:nt].rearrange("p a t -> p (a t)")
                    act.activation(dst, hu[:, jj, 0:nt], ACT.Copy).then_inc(uhi_done, 1)

                with act.Fori(0, nj // 2 - 1) as it:
                    for jj in range(2):
                        for q in range(2):
                            s = 2 * jj + q + 2
                            split(it * 4 + (FT[l] + V + s), s % 4, UNIT, it * 16 + 16 * ((first + V + s) // RING + 1))
                        silu(it, jj)
                        high(it, jj)
                last = nj // 2 - 1
                for jj in range(2):
                    for q in range(2):
                        v = V + 4 * last + 2 * jj + q + 2
                        split_static(v, UNIT if jj == 0 else nj * P)
                    silu(last, jj)
                    high(last, jj)
                V += 2 * nj
                for m in range(KD):
                    if m + 2 < KD:
                        split_static(V + m + 2, nj * P)
                    elif third < 2:
                        split_static(V + m + 2, UNIT)
                    if third == 2:
                        ln_square(2 * l + 1, m)
                V += KD
                J += nj
            layer_norm(2 * l + 1)

        out_projection(0, hx[:, 0], wsp_out0[:, 0])
        ffn(0)

        act.wait_ge(lo_made, SB["in1"])
        act.wait_ge(ln_norm, KD * 2)
        act.dma_start(wgr[:, :, :], m_w_in[0].rearrange("(k p) n -> p k n", p=P)[:, :, C_MG:C_MG + 4 * H_M]).then_inc(gate_in, 16)
        for g in range(4):
            act.dma_start(gb[32 * g:32 * g + H_M, :], m_gate_b[0, g].unsqueeze(1)).then_inc(gate_in, 16)
        act.dma_start(selr[:, :], consts[:, K_SEL:K_SEL + H_M * P]).then_inc(gate_in, 16)
        split_high("in1", 0, whi1)
        split_high("in1", 1, whi1)
        modulate(1, hT1, x_new, KD)
        act.wait_ge(gate_in, 16 * 6)
        act.wait_ge(gate_mm, 1)
        for g, dst in enumerate((li, gt, li, gt)):
            act.activation(dst[0:H_M, g // 2, :], PS[3][32 * g:32 * g + H_M, 0:T], ACT.Identity,
                           bias=gb[32 * g:32 * g + H_M, :]).then_inc(gate_ev, 1)

        def conv_in(f):
            split_high("in1", f + 2, whi1)
            if f < 2:
                act.wait_ge(pad_ok, 4)
            else:
                act.wait_ge(conv_done, f - 1)
            ins = act.activation(cpad[:, f % 2, 1:1 + LAT], PS[f % 3][:, 0:LAT], ACT.Copy)
            if f >= 4:
                ins = act.activation(cpad[:, f % 2, LAT + 3:T + 3], PS[f % 3][:, LAT:T], ACT.Copy)
            ins.then_inc(f_ev, 1)

        def conv_out(f):
            act.wait_ge(conv_done, f + 1)
            bias = vcol[:, V_CB + f:V_CB + f + 1]
            if f < 4:
                act.activation(mq[:, f, :], cacc[:, f % 2, 0:LAT], ACT.Silu, bias=bias).then_inc(silu_ev, 1)
            else:
                act.activation(mk[:, f - 4, 0:LAT], cacc[:, f % 2, 0:LAT], ACT.Silu, bias=bias)
                act.activation(mk[:, f - 4, LAT:T], cacc[:, f % 2, LAT + 2:T + 2], ACT.Silu, bias=bias).then_inc(silu_ev, 1)

        conv_in(0)
        act.wait_ge(ls_in, 1)
        step(act.activation(lf[0:H_M, :, :], gbc[0:H_M, :, :], ACT.Exp))
        act.activation(lf[0:H_M, :, :], lf[0:H_M, :, :], ACT.Ln, bias=onec[0:H_M, :]).then_inc(ls_ln, 1)
        for f in range(1, 8):
            conv_in(f)
            conv_out(f - 1)
        conv_out(7)
        act.wait_ge(floor_in, 1)
        act.activation(gbc[0:H_M, :, 0:LAT], gbc[0:H_M, :, 0:LAT], ACT.Exp, scale=-1.0).then_inc(floor_ok, 1)
        pairs = ((0, 1, 2), (3, 0, 1))
        for g in range(2):
            for i in range(10 + 4 * g, 14 + 4 * g):
                split_high("in1", i, whi1)
            for i, b in enumerate(pairs[g]):
                for q in range(2):
                    ins = act.activation(mv[:, 2 * i + q, 4 * g:4 * g + 4, 0:M_DV],
                                         half(2 * b + q).rearrange("p (h d) -> p h d", h=4), ACT.Copy)
                ins.then_inc(vg_ev, 1)
        for i in range(18, N_IN1):
            split_high("in1", i, whi1)
        act.wait_ge(unit_done, UB["in1"] + N_IN1)
        for t in (2, 3, 0, 1):
            act.activation(mo[:, t, :], PS[t][:, :], ACT.Sigmoid).then_inc(vg_ev, 1)
        act.wait_ge(tr_ev, 1)
        for h in range(H_M):
            act.wait_ge(nm_mm, h + 1)
            for j in range(TT):
                for d in range(2):
                    e = 2 * (TT * h + j) + d
                    if e >= 4:
                        act.wait_ge(mp_done, e - 3)
                    a, b = m_range(j, d)
                    act.activation(ee[:, e % 4, a:b], half(d)[:, a:b], ACT.Exp, bias=acol[:, d, j, h:h + 1]).then_inc(mexp, 1)
        act.wait_ge(mvar, 1)
        step(act.activation(mrs[:, :], mmv[:, :, 1], ACT.Ln, bias=epsc[:, :]))
        act.activation(mrs[:, :], mrs[:, :], ACT.Exp, scale=-0.5).then_inc(mrstd, 1)
        out_projection(1, hT1, wsp_out1[:, 0])
        ffn(1)
        for t in range(LT):
            act.wait_ge(out_mm, t + 1)
            act.activation(orow[:, t, :], PS[t][:, :], ACT.Copy).then_inc(out_ev, 1)

    @block.vector
    def _(dve):
        steps = 0

        def step(ins):
            nonlocal steps
            steps += 1
            ins.then_inc(dve_step, 1)
            dve.wait_ge(dve_step, steps)

        dve.sem_inc(h_done, H_CREDIT)
        dve.memset(onec[:, :], 1.0)
        dve.memset(epsc[:, :], EPS).then_inc(eps_ok, 1)
        dve.wait_ge(vec_T, 1)
        dve.tensor_copy(vcol[:, 0:V_ROWS], half(1)[:, 0:V_ROWS]).then_inc(vec_ev, 1)
        dve.tensor_copy(modb[:, :], half(0)[:, 0:96])
        for k in range(KD):
            dve.wait_ge(xT_mm, k + 1)
            dve.tensor_copy(xT[:, k, :], PS[1 + k % 2][:, 0:T]).then_inc(xT_ev, 1)

        def mod_rows(l, g, pair):
            dve.wait_ge(unit_done, UB[f"mod{l}{g}"] + KD)
            dve.tensor_copy(mrow[:, :], pair[0:2, :]).then_inc(mod_row, 1)

        def mod_columns(l, g, pair):
            dve.wait_ge(mod_T, MOD_AT[l, g])
            src = pair[:, 0:16].rearrange("p (b v) -> p v b", v=2)
            at = 48 * l + KD * g
            for v in range(2):
                dst = modc[:, l, g, :, :].rearrange("p b v -> p v b")[:, v, :]
                if g in (1, 4):
                    ins = dve.scalar_tensor_tensor(dst, src[:, v, :], 1.0, modb[:, at:at + KD], ALU.add, ALU.add)
                else:
                    ins = dve.tensor_tensor(dst, src[:, v, :], modb[:, at:at + KD], ALU.add)
            ins.then_inc(mod_ev, 1)

        mod_rows(0, 0, PS[3])
        mod_columns(0, 0, PS[3])
        mod_rows(0, 1, PS[0])
        mod_columns(0, 1, PS[0])
        def modulate_low(l, hi, lo, raw):
            for k in range(KD):
                dve.wait_ge(hmod, KD * l + k + 1)
                for a, b, v in ALL_SEGS:
                    ins = dve.scalar_tensor_tensor(raw[:, k, a:b], xT[:, k, a:b], modc[:, l, 1, k, v:v + 1],
                                                   hi[:, k, a:b].bitcast(F32), ALU.mult, ALU.subtract)
                step(ins)
                for a, b, v in ALL_SEGS:
                    ins = dve.tensor_scalar(lo[:, k, a:b], raw[:, k, a:b], modc[:, l, 0, k, v:v + 1], None, ALU.add)
                ins.then_inc(hmod_lo, 1)

        modulate_low(0, hx[:, 0], hx[:, 1], hx_raw[:, 1])
        mod_rows(0, 2, PS[3])
        mod_columns(0, 2, PS[3])
        dve.wait_ge(tabs_in, 16 * 4)
        for i, f in ((1, -1.0), (2, float(P)), (3, 640.0)):
            ins = dve.tensor_scalar(lgc[:, i, :], lgc[:, 0, :], f, None, ALU.mult)
        step(ins)
        for c in range(KQ + KKV):
            i = 0 if c < KQ else 1
            dve.wait_ge(rms_ready, i + 1)
            dve.scalar_tensor_tensor(cqkv[:, c, :], cqkv[:, c, :], vcol[:, V_QN + c:V_QN + c + 1], rms[:, i, :],
                                     ALU.mult, ALU.mult).then_inc(cq_norm, 1)

        def rope(r, bank, X, tab, tmp, lo, hi, mm, ev, done):
            dve.wait_ge(mm, r + 1)
            dve.tensor_tensor(tmp[lo:hi, :], bank[lo:hi, :], tab[lo:hi, 1, :], ALU.mult).then_inc(ev, 1)
            step(dve.tensor_tensor(X, X, tab[lo:hi, 0, :], ALU.mult))
            dve.tensor_tensor(X, X, tmp[lo:hi, :], ALU.add).then_inc(done, 1)

        rope(0, half(6), krope[NOPE:DQ, 0:LAT], cosM, rtmp, NOPE, DQ, rope_mm, rope_ev, rope_done)

        def rope_ret(r):
            X = rq[:, r - 1, 0:LAT] if r <= H_RET else rk[:, r - 1 - H_RET, 0:LAT]
            dve.wait_ge(rope_done, r)
            rope(r, half(6 + r % 2), X, cosR, rtmp, 0, P, rope_mm, rope_ev, rope_done)

        for r in range(1, 8):
            rope_ret(r)

        def strips(h):
            a = strip[:, h % 2, 0:REL_W]
            far = float(LAT - P)
            dve.tensor_scalar(a, rel[:, :], -far, 0.0, ALU.add, ALU.max)
            dve.tensor_scalar(stripb, rel[:, :], -far, 0.0, ALU.add, ALU.min).then_inc(strip_in, 1)
            dve.wait_ge(strip_exp, 2 * h + 1)
            dve.scalar_tensor_tensor(a, rel[:, :], far, a, ALU.is_ge, ALU.mult)
            step(dve.scalar_tensor_tensor(stripb, rel[:, :], far, stripb, ALU.is_le, ALU.mult))
            dve.tensor_tensor(a, a, stripb, ALU.add).then_inc(strip_in, 1)
            dve.wait_ge(strip_exp, 2 * h + 2)
            step(dve.tensor_tensor(strip[:, h % 2, REL_W:], strip[:, h % 2, REL_W:], stripb[:, 0:S2_W], ALU.add))

        strips(0)
        strips(1)
        rope_ret(8)
        mod_rows(0, 3, PS[2])

        def ret_weigh(h):
            if h >= 2:
                dve.wait_ge(ret_o, h - 1)
            for i, (j, seg) in enumerate(RET_TILES):
                s = 8 * h + i
                dve.wait_ge(ret_s, s + 1)
                a, b, _ = ALL_SEGS[seg]
                w = b - a
                if seg == 0 and j >= LT:
                    c0 = REL_W + P * (TT - 1 - j)
                else:
                    c0 = (LAT - P) - P * (j - LT * seg)
                dve.scalar_tensor_tensor(pt[:, h % 2, ret_off(j, seg):ret_off(j, seg) + w], half(s % 4)[:, 0:w], R_SCALE,
                                         strip[:, h % 2, c0:c0 + w], ALU.mult, ALU.mult).then_inc(ret_p, 1)

        def ret_norm(h):
            dve.wait_ge(ret_o, h + 1)

            def o(t):
                seg = 0 if t < LT else 1
                return half(4 + 2 * (h % 2) + seg)[:, (t - LT * seg) * P:(t - LT * seg + 1) * P]

            for t in range(TT):
                ins = dve.bn_stats(rst[:, t, :], o(t))
            step(ins)
            for t in range(TT):
                ins = dve.bn_aggr(rmv[:, t, :], rst[:, t, :])
            ins.then_inc(ret_var, 1)
            dve.wait_ge(ret_rstd, h + 1)
            for t in range(TT):
                step(dve.tensor_scalar(rnm[:, t % 2, :], o(t), rmv[:, t, 0:1], rrs[:, t:t + 1], ALU.subtract, ALU.mult))
                dst = rg[:, t, h * P:(h + 1) * P]
                ins = dve.tensor_tensor(dst, dst, rnm[:, t % 2, :], ALU.mult)
            ins.then_inc(ret_nrm, 1)

        dve.wait_ge(rg_ready, 3)
        ret_weigh(0)
        mod_columns(0, 3, PS[2])
        ret_weigh(1)
        strips(2)
        ret_norm(0)
        ret_weigh(2)
        strips(3)
        ret_norm(1)
        ret_weigh(3)
        ret_norm(2)
        ret_norm(3)

        for h in range(H_MLA):
            rope(h, half(6 + h % 2), qh[NOPE:DQ, h, 0:LAT], cosM, mtmp, NOPE, DQ, mrope_mm, mrope_ev, mrope_done)
            dve.wait_ge(mrope_done, h + 1)

        def att_max(it):
            dve.wait_ge(att_s, it + 1)
            a = 0 if it % TT < LT else LAT
            step(dve.tensor_reduce(nmx[:, 1, it:it + 1], PS[it % 2][:, a:T], AX.X, ALU.max))
            dve.tensor_scalar(nmx[:, 0, it:it + 1], nmx[:, 1, it:it + 1], -A_SCALE, None, ALU.mult).then_inc(att_nmx, 1)

        def att_copy(it):
            dve.wait_ge(att_t, it + 1)
            if it >= 2:
                dve.wait_ge(att_o, it - 1)
            dve.tensor_copy(paT[:, it % 2, LAT:T], PS[2][:, LAT:T]).then_inc(att_tB, 1)

        def att_norm(it):
            h, t = divmod(it, TT)
            dve.wait_ge(att_o, it + 1)
            step(dve.reciprocal(den[:, 1, it:it + 1], den[:, 0, it:it + 1]))
            dve.tensor_scalar(att[:, t, h * MLA_V:(h + 1) * MLA_V], half(6 + it % 2)[:, 0:MLA_V], den[:, 1, it:it + 1],
                              None, ALU.mult).then_inc(att_n, 1)

        for i in range(N_ATT + 2):
            if i < N_ATT:
                att_max(i)
            if 1 <= i <= N_ATT:
                att_copy(i - 1)
            if i >= 2:
                att_norm(i - 2)

        mod_rows(1, 0, PS[0])
        mod_columns(1, 0, PS[0])

        def z_update(l, g, m, pair):
            for a, b, v in SEGS[l]:
                ins = dve.scalar_tensor_tensor(xT[:, m, a:b], pair[:, a:b], modc[:, l, g, m, v:v + 1], xT[:, m, a:b],
                                               ALU.mult, ALU.add)
            ins.then_inc(z_ev, 1)

        def ln_sum(i, m, z):
            nt = NT[i // 2]
            dve.wait_ge(z_ev, z)
            if m == 0:
                ins = dve.tensor_copy(s1[:, 0:nt], xT[:, m, 0:nt])
            else:
                ins = dve.tensor_tensor(s1[:, 0:nt], s1[:, 0:nt], xT[:, m, 0:nt], ALU.add)
            if m == KD - 1:
                ins.then_inc(ln_sum1, 1)
            else:
                step(ins)

        def layer_norm(i, mods=()):
            nt = NT[i // 2]
            dve.wait_ge(ln_mm, 2 * i + 2)
            dve.wait_ge(ln_mean, i + 1)
            step(dve.scalar_tensor_tensor(s2[:, 0:nt], PS[1][:, 0:nt], 1.0 / D, s1[:, 0:nt], ALU.mult, ALU.subtract))
            dve.tensor_scalar(s2[:, 0:nt], s2[:, 0:nt], 0.0, EPS, ALU.max, ALU.add).then_inc(ln_var, 1)
            dve.wait_ge(ln_rstd, i + 1)
            for k in range(KD):
                z = xT[:, k, 0:nt]
                step(dve.tensor_tensor(z, z, lnm[:, 0:nt], ALU.subtract))
                dve.tensor_tensor(z, z, lnr[:, 0:nt], ALU.mult).then_inc(ln_norm, 1)
                if mods and k == 2:
                    mod_rows(*mods[0], PS[2])
                if mods and k == 6:
                    mod_columns(*mods[0], PS[2])

        def out_projection(l, h_hi, h_lo):
            nt = NT[l]
            for c in range(KD):
                dve.wait_ge(oT_hi, KD * l + c + 1)
                hi = h_hi[:, c, 0:nt].bitcast(F32)
                if l == 0:
                    ins = dve.tensor_tensor(h_lo[:, c, 0:nt], op_pair(c)[:, 0:nt], hi, ALU.subtract)
                else:
                    ins = dve.scalar_tensor_tensor(h_lo[:, c, 0:nt], op_pair(c)[:, 0:nt], vcol[:, V_NG + c:V_NG + c + 1], hi,
                                                   ALU.mult, ALU.subtract)
                ins.then_inc(oT_ev, 1)
            for m in range(KD):
                dve.wait_ge(unit_done, UB[f"out{l}"] + m + 1)
                dve.wait_ge(xa_done, KD * 2 * l + m + 1)
                z_update(l, 2, m, op_pair(m))
                if m >= 1:
                    ln_sum(2 * l, m - 1, ZB[l] + m)
            ln_sum(2 * l, KD - 1, ZB[l] + KD)
            layer_norm(2 * l, ((l, 4),))

        def ffn(l):
            nt = NT[l]
            for k in range(KD):
                if k == 1:
                    mod_rows(l, 5, PS[3])
                if k == 2:
                    mod_columns(l, 5, PS[3])
                dve.wait_ge(x_new, KD * 2 * l + k + 1)
                for a, b, v in SEGS[l]:
                    ins = dve.tensor_scalar(hu[:, k % 2, a:b], xT[:, k, a:b], modc[:, l, 4, k, v:v + 1],
                                            modc[:, l, 3, k, v:v + 1], ALU.mult, ALU.add)
                step(ins)
                dve.wait_ge(fh_hi, KD * l + k + 1)
                dve.tensor_tensor(hlo[:, k, 0:nt], hu[:, k % 2, 0:nt], hhi[:, k, 0:nt].bitcast(F32), ALU.subtract).then_inc(fh_lo, 1)
            V, J, z0 = 0, JB[l], ZB[l] + KD
            for third, (j0, nj) in enumerate(THIRDS):
                with dve.Fori(0, nj // 2) as it:
                    for jj in range(2):
                        dve.wait_ge(silu_done, it * 2 + (J + jj + 1))
                        dve.wait_ge(uhi_done, it * 2 + (J + jj + 1 - 2) if J or third else it * 2 + jj)
                        dve.tensor_tensor(hu[:, jj, 0:nt], sg[:, jj, 0:nt], PS[2 * jj][:, 0:nt], ALU.mult).then_inc(h_done, 1)
                        dve.wait_ge(uhi_done, it * 2 + (J + jj + 1))
                        j = it * 2 + jj
                        hi = uhi[:, bass.ds(j, 1), 0:nt].rearrange("p a t -> p (a t)")
                        lo = ulo[:, bass.ds(j, 1), 0:nt].rearrange("p a t -> p (a t)")
                        dve.tensor_tensor(lo, hu[:, jj, 0:nt], hi.bitcast(F32), ALU.subtract).then_inc(ulo_done, 1)
                V += 2 * nj
                for m in range(KD):
                    dve.wait_ge(ffn_tile, FT[l] + V + m + 1 + TILE_CREDIT)
                    if third == 0:
                        dve.wait_ge(xa_done, KD * (2 * l + 1) + m + 1)
                    else:
                        dve.wait_ge(z_ev, z0 + KD * (third - 1) + m + 1)
                    z_update(l, 5, m, PS[m % 4])
                    if third == 2 and m >= 1:
                        ln_sum(2 * l + 1, m - 1, z0 + 2 * KD + m)
                V += KD
                J += nj
            ln_sum(2 * l + 1, KD - 1, z0 + 3 * KD)
            if l == 0:
                layer_norm(1, ((1, 1),))
                mod_rows(1, 2, PS[3])
                mod_columns(1, 2, PS[3])
            else:
                layer_norm(3)

        out_projection(0, hx[:, 0], hx[:, 1])
        ffn(0)

        modulate_low(1, hT1, hlo1, hlo1_raw)
        dve.wait_ge(gate_ev, 4)
        z_, g_, b_ = gt[0:H_M, :, :], gbc[0:H_M, :, :], lf[0:H_M, :, :]
        dve.scalar_tensor_tensor(g_, z_, -1.0, z_, ALU.mult, ALU.min).then_inc(ls_in, 1)

        def conv(f):
            w = LAT if f < 4 else T + 2
            dve.wait_ge(f_ev, f + 1)
            if f >= 2:
                dve.wait_ge(silu_ev, f - 1)
            y = cacc[:, f % 2, 0:w]

            def tap(i):
                return vcol[:, V_CW + 8 * i + f:V_CW + 8 * i + f + 1]

            step(dve.tensor_scalar(y, cpad[:, f % 2, 1:1 + w], tap(1), None, ALU.mult))
            step(dve.scalar_tensor_tensor(y, cpad[:, f % 2, 0:w], tap(0), y, ALU.mult, ALU.add))
            dve.scalar_tensor_tensor(y, cpad[:, f % 2, 2:2 + w], tap(2), y, ALU.mult, ALU.add).then_inc(conv_done, 1)

        dve.wait_ge(ls_ln, 1)
        step(dve.scalar_tensor_tensor(b_, z_, 0.0, b_, ALU.min, ALU.subtract))

        def scan(dst, src, d, op, init):
            for a, b in ((LAT, T), (0, LAT)):
                sl = slice(a, b) if d == 0 else slice(b - 1, a - 1 if a else None, -1)
                step(dve.tensor_tensor_scan(dst[0:H_M, d, sl], src[0:H_M, d, sl], src[0:H_M, d, sl], init, op, ALU.bypass))
                last = T - 1 if d == 0 else LAT
                init = dst[0:H_M, d, last:last + 1]

        conv(0)
        for d in range(2):
            scan(gbc, lf, d, ALU.add, 0.0)
        conv(1)
        step(dve.tensor_tensor(li[0:H_M, :, :], li[0:H_M, :, :], g_, ALU.subtract))
        for d in range(2):
            scan(gt, li, d, ALU.max, 0.0)
        conv(2)
        dve.tensor_scalar(negm[0:H_M, :, :], gt[0:H_M, :, 0:LAT], -1.0, None, ALU.mult).then_inc(rows_ok, 1)
        dve.tensor_tensor(gbc[0:H_M, :, 0:LAT], gbc[0:H_M, :, 0:LAT], gt[0:H_M, :, 0:LAT], ALU.add).then_inc(floor_in, 1)
        for f in range(3, 8):
            conv(f)
        mod_rows(1, 3, PS[2])
        dve.wait_ge(tr_mm, 1)
        dve.tensor_copy(acol[:, :, :, :], half(6)[:, 0:2 * TT * H_M].rearrange("p (d t h) -> p d t h", d=2, t=TT)).then_inc(tr_ev, 1)
        dve.tensor_copy(fcol[:, :, :, :], half(6)[:, 2 * TT * H_M:2 * (TT + LT) * H_M].rearrange("p (d t h) -> p d t h", d=2, t=LT)).then_inc(tr_ev, 1)

        def m_weigh(h):
            if h >= 2:
                dve.wait_ge(mo_mm, LT * (h - 1))
            for j in range(TT):
                for d in range(2):
                    s = TT * h + j
                    e = 2 * s + d
                    dve.wait_ge(ms_mm, s + 1)
                    if j < LT:
                        dve.wait_ge(msel, 2 * LT * h + 2 * j + d + 1)
                    else:
                        dve.wait_ge(mexp, e + 1)
                    a, b = m_range(j, d)
                    at = M_OFF[d][j]
                    dve.scalar_tensor_tensor(pp[:, h % 2, d, at:at + b - a], half(2 + s % 4)[:, a:b], M_SCALE,
                                             ee[:, e % 4, a:b], ALU.mult, ALU.mult).then_inc(mp_done, 1)

        mod_columns(1, 3, PS[2])

        def m_divide(h):
            for t in range(LT):
                i = LT * h + t
                dve.wait_ge(mo_mm, i + 1)
                o = half(6 + i % 2)[:, 0:2 * (M_DV + 1)].rearrange("p (d v) -> p d v", d=2)
                dd = dab[:, i % 2, t, :]
                step(dve.tensor_scalar(dd, o[:, :, M_DV], -1.0, None, ALU.mult))
                step(dve.tensor_tensor(dd, dd, o[:, :, M_DV], ALU.max))
                step(dve.tensor_tensor(dd, dd, fcol[:, :, t, h], ALU.max))
                step(dve.reciprocal(dd, dd))
                step(dve.tensor_scalar(hf[:, i % 2, :], o[:, 0, 0:M_DV], dd[:, 0:1], None, ALU.mult))
                dst = hb[:, t, h * M_DV:(h + 1) * M_DV]
                dve.scalar_tensor_tensor(dst, o[:, 1, 0:M_DV], dd[:, 1:2], hf[:, i % 2, :], ALU.mult, ALU.add).then_inc(mh_ev, 1)
            dve.wait_ge(mh_ev, LT * (h + 1))
            for t in range(LT):
                ins = dve.bn_stats(mst[:, h * LT + t, :], hb[:, t, h * M_DV:(h + 1) * M_DV])
            step(ins)
            for t in range(LT):
                ins = dve.bn_aggr(mmv[:, h * LT + t, :], mst[:, h * LT + t, :])
            if h == H_M - 1:
                ins.then_inc(mvar, 1)

        dve.wait_ge(vg_ev, 10)
        m_weigh(0)
        for h in range(1, H_M):
            m_weigh(h)
            m_divide(h - 1)
        m_divide(H_M - 1)
        dve.wait_ge(mrstd, 1)
        for h in range(H_M):
            for t in range(LT):
                i = h * LT + t
                dst = hb[:, t, h * M_DV:(h + 1) * M_DV]
                ins = dve.tensor_scalar(dst, dst, mmv[:, i, 0:1], mrs[:, i:i + 1], ALU.subtract, ALU.mult)
        step(ins)
        for t in range(LT):
            ins = dve.tensor_tensor(mo[:, t, :], mo[:, t, :], hb[:, t, :], ALU.mult)
        ins.then_inc(mn_done, 1)
        out_projection(1, hT1, hlo_out1)
        ffn(1)

    @block.gpsimd
    def _(pool):
        def scale_residual(i, ready, first):
            for k in range(KD):
                scale_chunk(i, k, ready, first)

        def scale_chunk(i, k, ready, first):
            nt = NT[i // 2]
            pool.wait_ge(ready, first + k + 1)
            pool.tensor_scalar(xT[:, k, 0:nt], xT[:, k, 0:nt], ALPHA, None, ALU.mult).then_inc(xa_done, 1)

        def split_low(stage, i, w_hi, w_lo):
            n = NB[stage] + i
            pool.wait_ge(hi_made, SB[stage] + i + 1)
            pool.tensor_tensor(w_lo[:, i % 2, :], ring[:, n % RING, :], w_hi[:, i % 2, :].bitcast(F32),
                               ALU.subtract).then_inc(lo_made, 1)

        def out_projection(l, wsp):
            split_low(f"out{l}", 0, wsp[:, 0], wsp[:, 1])
            split_low(f"out{l}", 1, wsp[:, 0], wsp[:, 1])
            for m in range(KD):
                if m + 2 < KD:
                    split_low(f"out{l}", m + 2, wsp[:, 0], wsp[:, 1])
                ln_sum(2 * l, m)

        def ln_sum(i, m):
            nt = NT[i // 2]
            pool.wait_ge(ln_sq, KD * i + m + 1)
            if m == 0:
                pool.tensor_copy(s2[:, 0:nt], sq[:, 0, 0:nt]).then_inc(ln_sum2, 1)
            else:
                pool.wait_ge(ln_sum2, KD * i + m)
                pool.tensor_tensor(s2[:, 0:nt], s2[:, 0:nt], sq[:, m % 2, 0:nt], ALU.add).then_inc(ln_sum2, 1)

        def ffn(l):
            def low(u, s, width):
                pool.wait_ge(hi_made, u)
                pool.tensor_tensor(wlo[:, s, 0:width], ring[:, (NB[f"ffn{l}"] + s) % RING, 0:width],
                                   whi[:, s, 0:width].bitcast(F32), ALU.subtract).then_inc(lo_made, 1)

            full = sum(2 * nj + KD for _, nj in THIRDS[:2]) + 2 * THIRDS[2][1]
            with pool.Fori(0, full // 4) as it:
                for s in range(4):
                    low(it * 4 + (FB[l] + s + 1), s, UNIT)
            w = THIRDS[2][1] * P
            low(FB[l] + full + 1, 0, w)
            low(FB[l] + full + 2, 1, w)
            for m in range(KD):
                if m + 2 < KD:
                    low(FB[l] + full + m + 3, (m + 2) % 4, w)
                ln_sum(2 * l + 1, m)

        for i in range(N_IN0):
            split_low("in0", i, wsp_in0[:, 0], wsp_in0[:, 1])
            if 2 <= i < 2 + KD:
                scale_chunk(0, i - 2, hmod_lo, 0)
        pool.wait_ge(xa_done, KD)
        pool.wait_ge(rope_done, 1)
        pool.wait_ge(ret_nrm, H_RET)
        for h in range(H_MLA):
            pool.tensor_copy(kh[NOPE:DQ, h, :], krope[NOPE:DQ, :]).then_inc(kr_cp, 1)
        out_projection(0, wsp_out0)
        scale_residual(1, fh_lo, 0)
        ffn(0)
        pool.wait_ge(gate_in, 16 * 6)
        pool.memset(wgf[:, :, :], 0.0).then_inc(pool_step, 1)
        pool.wait_ge(pool_step, 1)
        for g in range(4):
            pool.tensor_copy(wgf[:, :, 32 * g:32 * g + H_M], wgr[:, :, H_M * g:H_M * (g + 1)]).then_inc(gate_w, 1)
        pool.wait_ge(gate_w, 4)
        pool.tensor_copy(wg[:, 0, :, :], wgf[:, :, :]).then_inc(gate_w, 1)
        pool.wait_ge(gate_w, 5)
        pool.tensor_tensor(wg[:, 1, :, :], wgf[:, :, :], wg[:, 0, :, :].bitcast(F32), ALU.subtract).then_inc(gate_w, 1)
        split_low("in1", 0, whi1, wlo1)
        split_low("in1", 1, whi1, wlo1)
        for s in range(2):
            pool.memset(cpad[:, s, 0:1], 0.0)
            pool.memset(cpad[:, s, LAT + 1:LAT + 3], 0.0).then_inc(pad_ok, 1)
            pool.memset(cpad[:, s, T + 3:T + 4], 0.0).then_inc(pad_ok, 1)
        for i in range(2, N_IN1):
            split_low("in1", i, whi1, wlo1)
            if i == 2:
                pool.wait_ge(gate_mm, 1)
                pool.memset(mv[:, :, :, M_DV:M_DV + 1], 1.0).then_inc(ones_ok, 1)
            elif i < 3 + KD:
                scale_chunk(2, i - 3, hmod_lo, KD)
        for h in range(H_M):
            for j in range(LT):
                for d in range(2):
                    e = 2 * (TT * h + j) + d
                    pool.wait_ge(mexp, e + 1)
                    blk = ee[:, e % 4, j * P:(j + 1) * P]
                    sign = 1 if d == 0 else -1
                    pool.affine_select(out=blk, in_=blk, pattern=[[sign, P]], compare_op=ALU.is_ge, fill=0.0, base=0,
                                       channel_multiplier=-sign).then_inc(msel, 1)
        out_projection(1, wsp_out1)
        scale_residual(3, fh_lo, KD)
        ffn(1)

    es.close()


_INS = ['x', 'c', 'ctx', 'c_ctx', 'mod_w', 'mod_b', 'ln_g', 'ln_b', 'ffn_w_in', 'ffn_w_out', 'ab_w_in', 'mla_q_norm',
        'mla_w_uq', 'mla_kv_norm', 'mla_w_ukv', 'ret_log_decay', 'ab_w_out', 'm_w_in', 'm_conv_w', 'm_conv_b',
        'm_gate_b', 'm_norm_g', 'm_w_out']


def kernel(**inputs):
    import concourse.bacc as _bacc
    from concourse.bass_utils import run_bass_kernel_spmd as _run

    nc = _bacc.Bacc("TRN2", target_bir_lowering=False, num_devices=1)
    arrays, args = {}, []
    for name in _INS:
        a = np.ascontiguousarray(inputs[name])
        arrays[f"in_{name}"] = a
        args.append(nc.dram_tensor(f"in_{name}", a.shape, mybir.dt.from_np(a.dtype), kind="ExternalInput").ap())
    k = shape_constants()
    arrays["in_consts"] = k
    args.append(nc.dram_tensor("in_consts", k.shape, F32, kind="ExternalInput").ap())
    args.append(nc.dram_tensor("out", (1, LAT, D), F32, kind="ExternalOutput").ap())
    build(nc, *args)
    r = _run(nc, [arrays], core_ids=[0])
    return r.results[0]["out"]
```

```python
from contextlib import ExitStack

import numpy as np

import concourse.bass as bass
from concourse import mybir

F32 = mybir.dt.float32
F32R = mybir.dt.float32r
ALU = mybir.AluOpType
ACT = mybir.ActivationFunctionType
AX = mybir.AxisListType

P = 128
D = 1024
KD = D // P
LAT, CTX = 512, 256
T = LAT + CTX
TT = T // P
LT = LAT // P
GRID_W = 64
ROPE_BASE = 10000.0
DEPTH = 2
ALPHA = (2 * DEPTH) ** 0.25
EPS = 1e-5

H_MLA, NOPE, ROPE, MLA_V = 8, 64, 32, 64
DQ = NOPE + ROPE
Q_LORA, KV_LORA = 384, 256
KQ, KKV = Q_LORA // P, KV_LORA // P
H_RET, RET_D = 4, 128
H_M, M_DK, M_DV = 8, 64, 128
D_FF = -(-8 * D // (3 * 256)) * 256
FC = D_FF // P
THIRDS = ((0, 8), (8, 8), (16, FC - 16))

RING = 4
UNIT = 1024

C_KR = Q_LORA + KV_LORA
C_RQ = C_KR + ROPE
C_RK = C_RQ + H_RET * RET_D
C_RV = C_RK + H_RET * RET_D
C_RG = C_RV + H_RET * RET_D
C_MK = H_M * M_DK
C_MV = 2 * H_M * M_DK
C_MO = C_MV + H_M * M_DV
C_MG = C_MO + H_M * M_DV

V_C, V_CC, V_LG, V_LB = 0, 8, 16, 48
V_QN, V_KVN, V_CW, V_CB, V_NG = 80, 83, 85, 109, 117
V_ROWS = 125

REL_W = 896
K_ID, K_ONE, K_RR, K_RM = 0, 128, 256, 384
K_BASE = 512
K_COSR, K_SINR = 512, 1024
K_COSM, K_SINM = 1536, 2048
K_REL = 2560
K_SEL = K_REL + REL_W
K_ALL = K_SEL + H_M * P


def shape_constants():
    k = np.zeros((P, K_ALL), np.float32)
    p = np.arange(P)
    k[p, K_ID + p] = 1.0
    k[:, K_ONE:K_ONE + P] = 1.0

    def rotation(base, first, width, half):
        for b in range(first, first + width, 2 * half):
            for c in range(half):
                k[b + half + c, base + b + c] = -1.0
                k[b + c, base + b + half + c] = 1.0

    rotation(K_RR, 0, P, RET_D // 4)
    rotation(K_RM, 0, P, ROPE // 4)
    t = np.arange(LAT)
    pos = np.stack([t // GRID_W, t % GRID_W]).astype(np.float32)

    def table(width, first, cos_at, sin_at):
        da = width // 2
        inv = (np.float32(ROPE_BASE) ** (-np.arange(0, da, 2, dtype=np.float32) / np.float32(da))).astype(np.float32)
        for i in range(width):
            a = pos[i // da] * inv[i % (da // 2)]
            k[first + i, cos_at:cos_at + LAT] = np.cos(a)
            k[first + i, sin_at:sin_at + LAT] = np.sin(a)

    table(RET_D, 0, K_COSR, K_SINR)
    for first in range(0, P, ROPE):
        table(ROPE, first, K_COSM, K_SINM)
    k[:, K_REL:K_REL + REL_W] = np.arange(REL_W)[None, :] - p[:, None]
    for h in range(H_M):
        k[h, K_SEL + h * P:K_SEL + (h + 1) * P] = 1.0
    return k


def build(nc, x, c, ctx, c_ctx, mod_w, mod_b, ln_g, ln_b, ffn_w_in, ffn_w_out, ab_w_in, mla_q_norm, mla_w_uq,
          mla_kv_norm, mla_w_ukv, ret_log_decay, ab_w_out, m_w_in, m_conv_w, m_conv_b, m_gate_b, m_norm_g,
          m_w_out, consts, out):
    es = ExitStack()

    def sb(name, shape, dt=F32, at=None):
        return (at or es).enter_context(nc.sbuf_tensor(name, shape, dt))

    def under(*specs):
        st = ExitStack()
        r = [sb(name, shape, dt, at=st) for name, shape, dt in specs]
        st.close()
        return r if len(r) > 1 else r[0]

    def sem(name):
        return es.enter_context(nc.semaphore(name))

    kc = sb("kc", [P, K_BASE])
    ident, ones = kc[:, K_ID:K_ID + P], kc[:, K_ONE:K_ONE + P]
    rot_ret, rot_mla = kc[:, K_RR:K_RR + P], kc[:, K_RM:K_RM + P]
    xT = sb("xT", [P, KD, T])
    ring = sb("ring", [P, RING, UNIT])
    vcol = sb("vcol", [P, P])
    scol = sb("scol", [P, 16])
    modb = sb("modb", [P, DEPTH * 48])
    modc = sb("modc", [P, DEPTH, 6, KD, 2])
    mrow = sb("mrow", [2, D])
    gain = sb("gain", [P, 3, 2, KD, 2])
    again = sb("again", [P, 64])
    epsc = sb("epsc", [P, 1])
    onec = sb("onec", [P, 1])
    _, whi1 = under(("whi1_pad", [P, 4 * T - UNIT], F32), ("whi1", [P, 2, UNIT], F32R))
    lnbuf = sb("lnbuf", [P, 6, T])
    lnm, lnr, s1, s2 = (lnbuf[:, i, :] for i in range(4))
    sq = lnbuf[:, 4:6, :]

    def phase():
        return ExitStack()

    ph = phase()
    xin = sb("xin", [P, TT, D], at=ph)
    vrow = sb("vrow", [P, P], at=ph)
    brow = sb("brow", [96, P], at=ph)
    ph.close()
    m0 = phase()
    hx = under(("hx", [P, 2, KD, T], F32R))
    hx_raw = under(("hx_raw", [P, 2, KD, T], F32))
    W_KV = H_MLA * (NOPE + MLA_V)
    wukv = sb("wukv", [P, KKV, W_KV], at=m0)
    va = sb("va", [P, TT, H_MLA * MLA_V], at=m0)
    kh, mtmp = under(("kh", [P, H_MLA, T], F32), ("mtmp", [P, LAT], F32))
    PT_W = TT * LAT + 2 * CTX
    pt = sb("pt", [P, 2, PT_W], at=m0)
    assert KKV * W_KV + TT * H_MLA * MLA_V + 2 * PT_W >= 2 * KD * T
    cqkv = sb("cqkv", [P, KQ + KKV, T], at=m0)
    krope = sb("krope", [P, T], at=m0)
    wuq = sb("wuq", [P, KQ, H_MLA * DQ], at=m0)
    wsp_in0 = under(("wsp_in0", [P, 2, 2, UNIT], F32R))
    rg = sb("rg", [P, TT, H_RET * RET_D], at=m0)
    sb("wsp_in0_rest", [P, 4 * UNIT - TT * H_RET * RET_D], at=m0)
    cosM = sb("cosM", [P, 2, LAT], at=m0)
    ph = phase()
    rq = sb("rq", [P, H_RET, T], at=ph)
    rk = sb("rk", [P, H_RET, T], at=ph)
    rv = sb("rv", [P, TT, H_RET * RET_D], at=ph)
    cosR = sb("cosR", [P, 2, LAT], at=ph)
    rel = sb("rel", [P, REL_W], at=ph)
    lnf = lnbuf[:, :, :].rearrange("p a t -> p (a t)")
    sqb, rms = lnbuf[:, 0:3, :], lnbuf[:, 3:5, :]
    S2_W = LAT + P
    strip = lnf[:, 0:2 * (REL_W + S2_W)].rearrange("p (b n) -> p b n", b=2)
    stripb = lnf[:, 2 * (REL_W + S2_W):2 * (REL_W + S2_W) + REL_W]
    lgc = sb("lgc", [P, 4, 2 * H_RET], at=ph)
    rtmp = sb("rtmp", [P, LAT], at=ph)
    rst = sb("rst", [P, H_RET * TT, 6], at=ph)
    rmv = sb("rmv", [P, H_RET * TT, 2], at=ph)
    rrs = sb("rrs", [P, H_RET * TT], at=ph)
    ph.close()
    ph = phase()
    wsp_out0 = under(("wsp_out0", [P, 2, 2, UNIT], F32R))
    qh = sb("qh", [P, H_MLA, T], at=ph)
    att = sb("att", [P, TT, H_MLA * MLA_V], at=ph)
    pa, qrope = lnbuf[:, 0:2, :], lnbuf[:, 4:6, :]
    Q_ROPE, Q_NOPE, KV_NOPE, KV_V = 0, H_MLA * ROPE, 0, H_MLA * NOPE
    QG = P // ROPE
    paT = sb("paT", [P, 2, T], at=ph)
    NI = H_MLA * TT
    nmx = sb("nmx", [P, NI], at=ph)
    den = sb("den", [P, 2, NI], at=ph)
    ph.close()
    m0.close()
    m1 = phase()
    hb = under(("hb", [P, LT, D], F32))
    hT1 = sb("hT1", [P, KD, T], F32R, at=m1)
    mq = sb("mq", [P, H_M // 2, LAT], at=m1)
    mk = sb("mk", [P, H_M // 2, T], at=m1)
    wgr, wgf, wg = under(("wgr", [P, KD, 4 * H_M], F32), ("wgf", [P, KD, P], F32), ("wg", [P, 2, KD, P], F32R))
    mv = sb("mv", [P, TT, H_M, M_DV + 1], at=m1)
    hlo1 = under(("hlo1", [P, KD, T], F32R))
    hlo1_raw = under(("hlo1_raw", [P, KD, T], F32))
    mo = sb("mo", [P, LT, H_M * M_DV], at=m1)
    ee = sb("ee", [P, 4, LAT], at=m1)
    selr = sb("selr", [P, H_M * P], at=m1)
    acol = sb("acol", [P, 2, TT, H_M], at=m1)
    fcol = sb("fcol", [P, 2, LT, H_M], at=m1)
    negm = lnbuf[:, :, :].rearrange("p a t -> p (a t)")[:, 0:2 * LAT].rearrange("p (d t) -> p d t", d=2)
    FW = 2 * LAT + sum(LAT - P * j for j in range(LT))
    ph = phase()
    wlo1 = sb("wlo1", [P, 2, UNIT], F32R, at=ph)
    gb = sb("gb", [P, 1], at=ph)
    cpad = sb("cpad", [P, 2, T + 4], at=ph)
    cacc = sb("cacc", [P, 2, T + 2], at=ph)
    li = sb("li", [P, 2, T], at=ph)
    lf = sb("lf", [P, 2, T], at=ph)
    gt = sb("gt", [P, 2, T], at=ph)
    gbc = sb("gbc", [P, 2, T], at=ph)
    ph.close()
    ph = phase()
    hlo_out1, wsp_out1 = under(("hlo_out1", [P, KD, LAT], F32R), ("wsp_out1", [P, 2, 2, UNIT], F32R))
    pp = sb("pp", [P, 2, 2, FW], at=ph)
    dab = sb("dab", [P, 2, LT, 2], at=ph)
    mst = sb("mst", [P, LT * H_M, 6], at=ph)
    mmv = sb("mmv", [P, LT * H_M, 2], at=ph)
    mrs = sb("mrs", [P, LT * H_M], at=ph)
    hf = sb("hfwd", [P, 2, M_DV], at=ph)
    ph.close()
    m1.close()
    ph = phase()
    hhi = sb("hhi", [P, KD, T], F32R, at=ph)
    hlo_raw = under(("hlo_raw", [P, KD, T], F32))
    hlo = sb("hlo", [P, KD, T], F32R, at=ph)
    uhi = sb("uhi", [P, 8, T], F32R, at=ph)
    ulo = sb("ulo", [P, 8, T], F32R, at=ph)
    whi = sb("whi", [P, RING, UNIT], F32R, at=ph)
    wlo = sb("wlo", [P, RING, UNIT], F32R, at=ph)
    sg = sb("sg", [P, 2, T], at=ph)
    hu = sb("hu", [P, 2, T], at=ph)
    ph.close()
    ph = phase()
    orow = sb("orow", [P, LT, D], at=ph)
    ph.close()

    PS = [es.enter_context(nc.psum_tensor(f"ps{i}", [P, 1024], F32)) for i in range(4)]

    def half(i):
        return PS[i // 2][:, 512 * (i % 2):512 * (i % 2) + 512]


    N_IN0, N_OUT, N_FFN, N_IN1 = 22, KD, sum(2 * nj + KD for _, nj in THIRDS), 24
    STAGES = (("mod00", KD), ("mod01", KD), ("in0", N_IN0), ("mod03", KD), ("mod04", KD), ("mod02", KD), ("mod10", KD),
              ("out0", N_OUT), ("mod11", KD), ("mod05", KD), ("ffn0", N_FFN), ("mod12", KD), ("mod13", KD), ("in1", N_IN1),
              ("mod14", KD), ("out1", N_OUT), ("mod15", KD), ("ffn1", N_FFN))
    NB = {}
    UB = {}
    SB = {}
    freed_by = []
    u = v = 0
    for stage, count in STAGES:
        NB[stage], UB[stage], SB[stage] = len(freed_by), u, v
        for _ in range(count):
            if stage.startswith("mod"):
                freed_by.append((True, u))
            else:
                freed_by.append((False, v))
                v += 1
            if not stage.startswith("ffn"):
                u += 1
    MOD_AT = {}
    for stage, _ in STAGES:
        if stage.startswith("mod"):
            MOD_AT[int(stage[3]), int(stage[4])] = len(MOD_AT) + 1
    FB = (SB["ffn0"], SB["ffn1"])
    FT = (0, N_FFN)
    JB = (0, FC)
    ZB = (0, KD + 3 * KD)
    NT = (T, LAT)
    SEGS = (((0, LAT, 0), (LAT, T, 1)), ((0, LAT, 0),))
    ALL_SEGS = SEGS[0]
    H_CREDIT = 2
    U_CREDIT = 2
    TILE_CREDIT = 2

    def view(slot, k):
        return ring[:, slot, :].rearrange("p (k n) -> p k n", k=k)

    landed = [sem(f"landed{i}") for i in range(RING)]
    consts_in, tabs_in, x_in, wq_in, wkv_in, gate_in = (sem(s) for s in ("consts_in", "tabs_in", "x_in", "wq_in", "wkv_in", "gate_in"))
    unit_done = sem("unit_done")
    vec_T, vec_ev, scol_ok, xT_mm, xT_ev = (sem(s) for s in ("vec_T", "vec_ev", "scol_ok", "xT_mm", "xT_ev"))
    mod_row, mod_T = sem("mod_row"), sem("mod_T")
    mod_ev = sem("mod_ev")
    input_full, input_hi, input_lo, xa_done, gains_ok = (sem(s) for s in ("input_full", "input_hi", "input_lo", "xa_done", "gains_ok"))
    ln_sub, ln_subp = sem("ln_sub"), sem("ln_subp")
    ip_ev, sq_made, rms_mm, rms_ln, rms_ready, cq_norm = (sem(s) for s in ("ip_ev", "sq_made", "rms_mm", "rms_ln", "rms_ready", "cq_norm"))
    rope_mm, rope_ev, rope_done, rg_ready = (sem(s) for s in ("rope_mm", "rope_ev", "rope_done", "rg_ready"))
    strip_in, strip_exp = sem("strip_in"), sem("strip_exp")
    ret_s, ret_p, ret_o, ret_ev, ret_var, ret_rstd = (sem(s) for s in ("ret_s", "ret_p", "ret_o", "ret_ev", "ret_var", "ret_rstd"))
    mp_mm, mp_ev, mrope_mm, mrope_ev, mrope_done, qr_cp, kr_cp = (sem(s) for s in ("mp_mm", "mp_ev", "mrope_mm", "mrope_ev", "mrope_done", "qr_cp", "kr_cp"))
    att_s, att_nmx, att_exp, att_t, att_tA, att_tB, att_o, att_n = (sem(s) for s in ("att_s", "att_nmx", "att_exp", "att_t", "att_tA", "att_tB", "att_o", "att_n"))
    oT_mm, oT_hi, oT_ev, z_ev = sem("oT_mm"), sem("oT_hi"), sem("oT_ev"), sem("z_ev")
    ln_sq, ln_sum1, ln_sum2, ln_mm, ln_mean, ln_var, ln_rstd, ln_norm, x_new = (sem(s) for s in ("ln_sq", "ln_sum1", "ln_sum2", "ln_mm", "ln_mean", "ln_var", "ln_rstd", "ln_norm", "x_new"))
    hi_made, lo_made, ffn_tile, silu_done, h_done, uhi_done, ulo_done = (sem(s) for s in ("hi_made", "lo_made", "ffn_tile", "silu_done", "h_done", "uhi_done", "ulo_done"))
    gate_w, gate_mm, gate_ev, f_ev, conv_done, silu_ev, vg_ev, pad_ok = (sem(s) for s in ("gate_w", "gate_mm", "gate_ev", "f_ev", "conv_done", "silu_ev", "vg_ev", "pad_ok"))
    ls_in, ls_ln, rows_ok, floor_in, floor_ok, tr_mm, tr_ev = (sem(s) for s in ("ls_in", "ls_ln", "rows_ok", "floor_in", "floor_ok", "tr_mm", "tr_ev"))
    nm_mm, ms_mm, mexp, msel, mp_done, mo_mm, mh_ev, mvar, mrstd, mn_done = (sem(s) for s in ("nm_mm", "ms_mm", "mexp", "msel", "mp_done", "mo_mm", "mh_ev", "mvar", "mrstd", "mn_done"))
    eps_ok, ones_ok = sem("eps_ok"), sem("ones_ok")
    out_mm, out_st = sem("out_mm"), sem("out_st")
    out_ev = [sem("out_ev_even"), sem("out_ev_odd")]
    dve_step, act_step, pool_step = sem("dve_step"), sem("act_step"), sem("pool_step")

    F_COLS = [0, P, 2 * P, 3 * P, 4 * P, C_KR] + [C_RQ + P * i for i in range(4)] + [C_RK + P * i for i in range(4)]
    NF = len(F_COLS)
    RET_TILES = [(j, 0) for j in range(TT)] + [(j, 1) for j in range(LT, TT)]

    def ret_off(j, seg):
        return j * LAT if seg == 0 else TT * LAT + (j - LT) * CTX

    def m_range(j, d):
        if j >= LT:
            return 0, LAT
        return (P * j, LAT) if d == 0 else (0, P * (j + 1))

    M_OFF = [[], []]
    for d in range(2):
        at = 0
        for j in range(TT):
            M_OFF[d].append(at)
            at += m_range(j, d)[1] - m_range(j, d)[0]
    assert at == FW
    M_SCALE, R_SCALE, A_SCALE = M_DK ** -0.5, RET_D ** -0.5, DQ ** -0.5
    N_ATT = H_MLA * TT

    MLA = [("q_rope", g) for g in range(H_MLA // QG)] + [(kind, i) for kind in ("q_nope", "k_nope") for i in range(H_MLA // 2)] \
        + [("values", i) for i in range(TT // 2)]

    M_MOD = 5

    def mla_pair(m):
        return PS[(0, 2, 1)[m % 3]]

    def op_pair(i):
        return PS[(i + 1) % 4]

    def lat_items(it):
        return (it // TT) * LT + min(it % TT + 1, LT)

    LAG = 2
    NORM_ENDS = (2, 4, 6, 8)
    SUB_DVE, LEAD = KD - 2, 3

    block = es.enter_context(nc.Block())

    @block.sync
    def _(sp):
        def unit(n, dst, src):
            sp.dma_start(dst, src).then_inc(landed[n % RING], 16)

        def slot_free(n):
            if n >= RING:
                direct, i = freed_by[n - RING]
                sp.wait_ge(unit_done if direct else lo_made, i + 1)

        def mod_units(l, g):
            for k in range(KD):
                n = NB[f"mod{l}{g}"] + k
                slot_free(n)
                unit(n, ring[:, n % RING, :], mod_w[l, k * P:(k + 1) * P, g * D:(g + 1) * D])

        for g in range(2):
            mod_units(0, g)
        w_in = ab_w_in[0].rearrange("(k p) n -> p k n", p=P)
        for f, c0 in enumerate(F_COLS):
            n, w = NB["in0"] + f, P
            if c0 == C_KR:
                c0, w = C_KR - NOPE, DQ
            slot_free(n)
            unit(n, view(n % RING, KD)[:, :, 0:w], w_in[:, :, c0:c0 + w])
            if f == RING:
                sp.wait_ge(xT_mm, KD)
                sp.dma_start(cosR[:, :, :], consts[:, K_COSR:K_COSR + 2 * LAT].rearrange("p (a t) -> p a t", a=2)).then_inc(tabs_in, 16)
                sp.dma_start(cosM[:, :, :], consts[:, K_COSM:K_COSM + 2 * LAT].rearrange("p (a t) -> p a t", a=2)).then_inc(tabs_in, 16)
                sp.dma_start(rel[:, :], consts[:, K_REL:K_REL + REL_W]).then_inc(tabs_in, 16)
                sp.dma_start(lgc[:, 0, :], ret_log_decay[0].rearrange("a h -> (a h)").partition_broadcast(P)).then_inc(tabs_in, 16)
                w_q = mla_w_uq[0].rearrange("(k p) (h d) -> k p h d", p=P, h=H_MLA)
                for k in range(KQ):
                    for c0, a, b in ((Q_ROPE, NOPE, DQ), (Q_NOPE, 0, NOPE)):
                        dst = wuq[:, k, c0:c0 + H_MLA * (b - a)].rearrange("p (h d) -> p h d", h=H_MLA)
                        sp.dma_start(dst, w_q[k, :, :, a:b]).then_inc(wq_in, 16)
        for i in range(8):
            n, c0 = NB["in0"] + NF + i, (C_RV, C_RG)[i // 4]
            slot_free(n)
            unit(n, view(n % RING, 2), w_in[:, 2 * (i % 4):2 * (i % 4) + 2, c0:c0 + 512])
        mod_units(0, 3)
        sp.wait_ge(unit_done, UB["in0"] + N_IN0)
        w_kv = mla_w_ukv[0].rearrange("(k p) (h d) -> k p h d", p=P, h=H_MLA)
        for k in range(KKV):
            for c0, a, b in ((KV_NOPE, 0, NOPE), (KV_V, NOPE, NOPE + MLA_V)):
                dst = wukv[:, k, c0:c0 + H_MLA * (b - a)].rearrange("p (h d) -> p h d", h=H_MLA)
                sp.dma_start(dst, w_kv[k, :, :, a:b]).then_inc(wkv_in, 16)
        mod_units(0, 4)
        mod_units(0, 2)
        mod_units(1, 0)
        w_out = ab_w_out[0].rearrange("(k p) n -> p k n", p=P)
        for m in range(KD):
            n = NB["out0"] + m
            slot_free(n)
            unit(n, view(n % RING, KD), w_out[:, :, m * P:(m + 1) * P])
        mod_units(1, 1)
        mod_units(0, 5)

        def ffn_units(l):
            first = NB[f"ffn{l}"]
            w_up = ffn_w_in[l].rearrange("(k p) n -> p k n", p=P)
            w_dn = ffn_w_out[l].rearrange("(k p) n -> p k n", p=P)

            U = FB[l]
            for third, (j0, nj) in enumerate(THIRDS):
                start = 0
                if third == 0:
                    for s in range(4):
                        slot_free(first + s)
                        c0 = (j0 + s // 2) * P + (s % 2) * D_FF
                        n = (first + s) % RING
                        unit(n, view(n, KD), w_up[:, :, c0:c0 + P])
                    start = 1
                with sp.Fori(start, nj // 2) as it:
                    for s in range(4):
                        sp.wait_ge(lo_made, it * 4 + (U + s - RING + 1))
                        n = (first + s) % RING
                        unit(n, view(n, KD), w_up[:, :, bass.ds(it * (2 * P) + ((j0 + s // 2) * P + (s % 2) * D_FF), P)])
                U += 2 * nj
                with sp.Fori(0, 2) as it:
                    for s in range(4):
                        sp.wait_ge(lo_made, it * 4 + (U + s - RING + 1))
                        n = (first + s) % RING
                        dst = ring[:, n, 0:nj * P].rearrange("p (k n) -> p k n", k=nj)
                        unit(n, dst, w_dn[:, j0:j0 + nj, bass.ds(it * (4 * P) + s * P, P)])
                U += KD

        ffn_units(0)
        mod_units(1, 2)
        mod_units(1, 3)
        w_in = m_w_in[0].rearrange("(k p) n -> p k n", p=P)
        for i in range(N_IN1):
            n = NB["in1"] + i
            slot_free(n)
            if i < 8:
                unit(n, view(n % RING, KD), w_in[:, :, i * P:(i + 1) * P])
            elif i >= 16:
                unit(n, ring[:, n % RING, :], w_in[:, i - 16, C_MO:C_MO + H_M * M_DV])
            else:
                g, q = (i - 8) // 4, (i - 8) % 4
                unit(n, view(n % RING, 2), w_in[:, 2 * q:2 * q + 2, C_MV + g * 512:C_MV + (g + 1) * 512])
        mod_units(1, 4)
        w_out = m_w_out[0].rearrange("(k p) n -> p k n", p=P)
        for m in range(KD):
            n = NB["out1"] + m
            slot_free(n)
            unit(n, view(n % RING, KD), w_out[:, :, m * P:(m + 1) * P])
        mod_units(1, 5)
        ffn_units(1)
        for t in range(LT):
            sp.wait_ge(out_ev[t % 2], t // 2 + 1)
            sp.dma_start(out[0, t * P:(t + 1) * P, :], orow[:, t, :]).then_inc(out_st, 16)
        sp.wait_ge(out_st, 16 * LT)

    @block.tensor
    def _(pe):
        pe.sem_inc(ffn_tile, TILE_CREDIT)

        def loaded(n):
            pe.wait_ge(landed[n % RING], 16 * (n // RING + 1))

        pe.wait_ge(consts_in, 16 * 13)
        pe.transpose(half(0)[:, 0:96], brow[0:96, :], ident[0:96, 0:96])
        pe.transpose(half(1)[:, 0:V_ROWS], vrow[0:V_ROWS, :], ident[0:V_ROWS, 0:V_ROWS]).then_inc(vec_T, 1)
        s_kv = scol[:, :].rearrange("p (v k) -> p k v", v=2)

        def mod_rows(l, g, pair, first=0, end=KD):
            for k in range(first, end):
                n = NB[f"mod{l}{g}"] + k
                loaded(n)
                for b in range(2):
                    mm = pe.matmul(pair[32 * b:32 * b + 2, 512 * b:512 * (b + 1)], s_kv[:, k, :], ring[:, n % RING, 512 * b:512 * (b + 1)],
                                   start=(k == 0), stop=(k == KD - 1))
                mm.then_inc(unit_done, 1)

        def mod_columns(l, g, pair):
            pe.wait_ge(mod_row, MOD_AT[l, g])
            for b in range(KD):
                mm = pe.transpose(pair[:, 2 * b:2 * b + 2], mrow[0:2, b * P:(b + 1) * P], ident[0:2, 0:2])
            mm.then_inc(mod_T, 1)

        pe.wait_ge(scol_ok, 1)
        mod_rows(0, 0, PS[3], 0, 2)
        pe.wait_ge(x_in, 16 * 2)
        for k in range(KD):
            b = 1 + k % 2
            if k >= 2:
                pe.wait_ge(xT_ev, k - 1)
            for t in range(TT):
                mm = pe.transpose(PS[b][:, t * P:(t + 1) * P], xin[:, t, k * P:(k + 1) * P], ident)
            mm.then_inc(xT_mm, 1)
            if k + 2 < KD:
                mod_rows(0, 0, PS[3], k + 2, k + 3)
            else:
                pe.wait_ge(xT_ev, 1)
                mod_rows(0, 1, PS[0], k + 2 - KD, k + 3 - KD)
        mod_rows(0, 1, PS[0], 2, 5)
        mod_columns(0, 0, PS[3])
        mod_rows(0, 1, PS[0], 5, KD)
        mod_columns(0, 1, PS[0])

        def three(dst, hi_lo_pairs, first, last):
            (s_hi, m_hi), (s_lo, m_lo) = hi_lo_pairs
            pe.matmul(dst, s_hi, m_hi, start=first, stop=False)
            pe.matmul(dst, s_hi, m_lo, start=False, stop=False)
            return pe.matmul(dst, s_lo, m_hi, start=False, stop=last)

        def split_unit(stage, i):
            pe.wait_ge(lo_made, SB[stage] + i + 1)

        def project(dst, w_hi, w_lo, h_hi, h_lo, first, last, segs):
            for w, h, st, sp_ in ((w_hi, h_hi, first, False), (w_hi, h_lo, False, False), (w_lo, h_hi, False, last)):
                for a, b, _ in segs:
                    mm = pe.matmul(dst[:, a:b], w, h[:, a:b], start=st, stop=sp_)
            return mm

        def rotate(r, bank, mat, src, lo, hi, done, evac):
            if r >= 2:
                pe.wait_ge(evac, r - 1)
            pe.matmul(bank[lo:hi, :], mat[lo:hi, lo:hi], src, start=True, stop=True).then_inc(done, 1)

        def rms_sums(first, count):
            for c in range(first, first + count):
                for a, b, _ in ALL_SEGS:
                    mm = pe.matmul(PS[3][:, a:b], ones, sqb[:, c % 3, a:b], start=(c == first), stop=(c == first + count - 1))
            mm.then_inc(rms_mm, 1)

        def rot_source(f):
            if f == 5:
                return krope[NOPE:DQ, 0:LAT]
            return rq[:, f - 6, 0:LAT] if f < 10 else rk[:, f - 10, 0:LAT]

        def feature_chunk(f, ks):
            hi = DQ if f == 5 else P
            split_unit("in0", f)
            for k in ks:
                if f < 2:
                    pe.wait_ge(input_lo, k + 1)
                w_hi, w_lo = (wsp_in0[:, a, f % 2, k * P:k * P + hi] for a in range(2))
                mm = project(PS[f % 3][0:hi, :], w_hi, w_lo, hx[:, 0, k, :], hx[:, 1, k, :], k == 0, k == KD - 1, ALL_SEGS)
            if k == KD - 1:
                mm.then_inc(unit_done, 1)

        for f in range(NF):
            if f >= 3:
                pe.wait_ge(ip_ev, f - 2)
            if f == 0:
                for k in range(KD + LAG):
                    if k < KD:
                        feature_chunk(0, (k,))
                    if k >= LAG:
                        feature_chunk(1, (k - LAG,))
            elif f >= 2:
                feature_chunk(f, range(KD))
            if f == 3:
                pe.wait_ge(mod_ev, MOD_AT[0, 0])
                pe.wait_ge(sq_made, 3)
                rms_sums(0, KQ)
            if f == 5:
                pe.wait_ge(sq_made, 5)
                pe.wait_ge(rms_ln, 1)
                rms_sums(KQ, KKV)
            if f == 6:
                pe.wait_ge(rms_ln, 2)
                pe.wait_ge(ip_ev, 6)
                pe.wait_ge(tabs_in, 16 * 4)
                rotate(0, half(6), rot_mla, rot_source(5), NOPE, DQ, rope_mm, rope_ev)
            if f >= 7:
                pe.wait_ge(ip_ev, f)
                rotate(f - 6, half(6 + (f - 6) % 2), rot_ret, rot_source(f - 1), 0, P, rope_mm, rope_ev)

        def token_major(stage, i0, banks, wsp, h_hi, h_lo, ready):
            for q in range(4):
                i = i0 + q
                split_unit(stage, i)
                for k in (2 * q, 2 * q + 1):
                    w_hi, w_lo = (wsp[a][:, i % 2, 512 * (k % 2):512 * (k % 2) + 512] for a in range(2))
                    for t, b in banks:
                        if k == 0:
                            ready(b)
                        cols = slice(t * P, (t + 1) * P)
                        mm = three(half(b), ((h_hi[:, k, cols], w_hi), (h_lo[:, k, cols], w_lo)), k == 0, k == KD - 1)
                mm.then_inc(unit_done, 1)

        in0_parts = ((wsp_in0[:, 0], wsp_in0[:, 1]), hx[:, 0], hx[:, 1])
        token_major("in0", NF, [(0, 0), (1, 1), (4, 4), (5, 5), (2, 2), (3, 3)], *in0_parts,
                    lambda b: pe.wait_ge(ip_ev, NF if b in (2, 3) else NF - 1))
        rotate(8, half(6), rot_ret, rot_source(13), 0, P, rope_mm, rope_ev)

        def rg_ready_for(b):
            if b < 4:
                pe.wait_ge(ip_ev, NF + 1 + b // 2)
            else:
                pe.wait_ge(rope_ev, 9)

        token_major("in0", NF + 4, [(0, 0), (1, 1), (2, 2), (3, 3), (4, 6), (5, 7)], *in0_parts, rg_ready_for)

        def ret_scores(h):
            pe.wait_ge(rope_done, 6 + h)
            for i, (j, seg) in enumerate(RET_TILES):
                s = 8 * h + i
                if s >= 4:
                    pe.wait_ge(ret_p, s - 3)
                else:
                    pe.wait_ge(rg_ready, 2)
                a, b, _ = ALL_SEGS[seg]
                pe.matmul(half(s % 4)[:, 0:b - a], rk[:, h, j * P:(j + 1) * P], rq[:, h, a:b],
                          start=True, stop=True).then_inc(ret_s, 1)

        def ret_values(h):
            pe.wait_ge(ret_p, 8 * h + 8)
            if h >= 2:
                pe.wait_ge(ret_ev, h - 1)
            else:
                pe.wait_ge(rg_ready, 3)
                pe.wait_ge(mod_ev, MOD_AT[0, 3])
            for t in range(TT):
                seg = 0 if t < LT else 1
                bank = half(4 + 2 * (h % 2) + seg)
                js = [j for j, s in RET_TILES if s == seg]
                tq = (t - LT * seg) * P
                for j in js:
                    mm = pe.matmul(bank[:, tq:tq + P], pt[:, h % 2, ret_off(j, seg) + tq:ret_off(j, seg) + tq + P],
                                   rv[:, j, h * P:(h + 1) * P], start=(j == js[0]), stop=(j == js[-1]))
            mm.then_inc(ret_o, 1)

        pe.wait_ge(ip_ev, NF + 3)
        mod_rows(0, 3, PS[2])
        ret_scores(0)
        mod_columns(0, 3, PS[2])
        for h in range(1, H_RET):
            ret_scores(h)
            ret_values(h - 1)
        pe.wait_ge(ret_p, 8 * H_RET)
        mod_rows(0, 4, PS[1], 0, 4)
        ret_values(H_RET - 1)
        mod_rows(0, 4, PS[1], 4, KD)

        pe.wait_ge(ret_p, 8 * H_RET)
        pe.wait_ge(ret_ev, 3)
        pe.wait_ge(wq_in, 16 * 2 * KQ)
        pe.wait_ge(cq_norm, 5)
        for m, (kind, i) in enumerate(MLA):
            pair = mla_pair(m)
            if m == 1:
                mod_columns(0, 4, PS[1])
            if m == 2:
                pe.wait_ge(mod_ev, MOD_AT[0, 4])
            if m >= 3:
                pe.wait_ge(mp_ev, m - 2)
            if (kind, i) == ("k_nope", 0):
                pe.wait_ge(wkv_in, 16 * 2 * KKV)
            if kind == "values":
                for j in range(2):
                    t = 2 * i + j
                    for k in range(KKV):
                        mm = pe.matmul(pair[:, 512 * j:512 * j + 512], cqkv[:, KQ + k, t * P:(t + 1) * P], wukv[:, k, KV_V:],
                                       start=(k == 0), stop=(k == KKV - 1))
            else:
                nk, k0 = (KKV, KQ) if kind == "k_nope" else (KQ, 0)
                for k in range(nk):
                    w, c0 = {"q_rope": (wuq, Q_ROPE), "q_nope": (wuq, Q_NOPE), "k_nope": (wukv, KV_NOPE)}[kind]
                    w = w[:, k, c0 + i * P:c0 + (i + 1) * P]
                    for a, b, _ in ALL_SEGS:
                        mm = pe.matmul(pair[:, a:b], w, cqkv[:, k0 + k, a:b], start=(k == 0), stop=(k == nk - 1))
            mm.then_inc(mp_mm, 1)
            if 1 <= m <= 2:
                r = m - 1
                pe.wait_ge(mp_ev, r + 1)
                if r == 0:
                    pe.wait_ge(ret_ev, 4)
                rotate(r, half(6 + r), rot_mla, qrope[:, r, 0:LAT], 0, P, mrope_mm, mrope_ev)
            if M_MOD <= m < M_MOD + 4:
                if m == M_MOD:
                    pe.wait_ge(mrope_ev, 2)
                mod_rows(0, 2, PS[3], 2 * (m - M_MOD), 2 * (m - M_MOD) + 2)
            if m == len(MLA) - 1:
                mod_columns(0, 2, PS[3])

        def att_scores(it):
            h, t = divmod(it, TT)
            if it >= 2:
                pe.wait_ge(att_exp, it - 1)
            else:
                pe.wait_ge(mp_ev, len(MLA))
            if t == 0:
                pe.wait_ge(qr_cp, h + 1)
                pe.wait_ge(kr_cp, h + 1)
            for a, b, _ in (ALL_SEGS if t < LT else ALL_SEGS[1:]):
                mm = pe.matmul(PS[it % 2][:, a:b], qh[0:DQ, h, t * P:(t + 1) * P], kh[0:DQ, h, a:b], start=True, stop=True)
            mm.then_inc(att_s, 1)

        def att_transpose(it):
            t = it % TT
            pe.wait_ge(att_exp, it + 1)
            if it >= 1:
                pe.wait_ge(att_tA, lat_items(it - 1))
                pe.wait_ge(att_tB, it)
            for j in range(0 if t < LT else LT, TT):
                mm = pe.transpose(PS[2][:, j * P:(j + 1) * P], pa[:, it % 2, j * P:(j + 1) * P], ident)
            mm.then_inc(att_t, 1)

        def att_values(it):
            h, t = divmod(it, TT)
            pe.wait_ge(att_tA, lat_items(it))
            pe.wait_ge(att_tB, it + 1)
            if it >= 2:
                pe.wait_ge(att_n, it - 1)
            else:
                pe.wait_ge(mod_ev, MOD_AT[0, 2])
            j0 = 0 if t < LT else LT
            for j in range(j0, TT):
                mm = pe.matmul(half(6 + it % 2)[:, 0:MLA_V], paT[:, it % 2, j * P:(j + 1) * P],
                               va[:, j, h * MLA_V:(h + 1) * MLA_V], start=(j == j0), stop=(j == TT - 1))
            mm.then_inc(att_o, 1)

        for i in range(N_ATT + 2):
            if i < N_ATT:
                att_scores(i)
            if i >= 2:
                att_values(i - 2)
            if 1 <= i <= N_ATT:
                att_transpose(i - 1)
            if i >= N_ATT:
                q = (i - N_ATT) * 4
                mod_rows(1, 0, PS[0], q, q + 4)

        def out_projection(l, source, h_hi, h_lo, wsp):
            for c in range(KD):
                if c >= 4:
                    pe.wait_ge(oT_ev, KD * l + c - 3)
                if l == 1 and (c == 0 or c in NORM_ENDS):
                    pe.wait_ge(mn_done, 1 + (NORM_ENDS.index(c) + 1 if c else 0))
                if c == 1:
                    if l == 0:
                        mod_columns(1, 0, PS[0])
                    pe.wait_ge(mod_ev, MOD_AT[1, 4 * l])
                for t in range(NT[l] // P):
                    mm = pe.transpose(op_pair(c)[:, t * P:(t + 1) * P], source(c, t), ident)
                mm.then_inc(oT_mm, 1)
            for m in range(KD):
                if m < 4:
                    pe.wait_ge(oT_ev, KD * l + 5 + m)
                else:
                    pe.wait_ge(z_ev, ZB[l] + m - 3)
                split_unit(f"out{l}", m)
                for k in range(KD):
                    if m == 0:
                        pe.wait_ge(oT_ev, KD * l + k + 1)
                    w_hi, w_lo = (wsp[:, a, m % 2, k * P:(k + 1) * P] for a in range(2))
                    mm = project(op_pair(m), w_hi, w_lo, h_hi[:, k, :], h_lo[:, k, :], k == 0, k == KD - 1, SEGS[l])
                mm.then_inc(unit_done, 1)

        def ln_with_mod(i, z, first, second=None):
            pe.wait_ge(z_ev, z - 1)
            mod_rows(*first, PS[2], 0, 3)
            ln_sums(i)
            mod_rows(*first, PS[2], 3, KD)
            if second:
                pe.wait_ge(z_ev, z)
                mod_rows(*second, PS[3], 0, 3)
            mod_columns(*first, PS[2])
            if second:
                mod_rows(*second, PS[3], 3, KD)
                mod_columns(*second, PS[3])
            pe.wait_ge(mod_ev, MOD_AT[second or first])

        def ln_sums(i):
            l = i // 2
            for q, (src, ready, count) in enumerate(((s1, ln_sum1, i + 1), (s2, ln_sum2, KD * (i + 1)))):
                pe.wait_ge(ready, count)
                for a, b, _ in SEGS[l]:
                    mm = pe.matmul(PS[q][:, a:b], ones, src[:, a:b], start=True, stop=True)
                mm.then_inc(ln_mm, 1)

        def ffn(l):
            U, J = FB[l], JB[l]
            z0 = ZB[l] + KD
            for third, (j0, nj) in enumerate(THIRDS):
                def tile(s, k, hi, lo, last):
                    return project(PS[s], whi[:, s, k * P:(k + 1) * P], wlo[:, s, k * P:(k + 1) * P], hi, lo, k == 0, last, SEGS[l])

                if third == 0:
                    pe.wait_ge(h_done, J - 1 + H_CREDIT)
                    for k in range(KD + 1):
                        if k < KD:
                            pe.wait_ge(input_lo, KD * (2 * l + 1) + k + 1)
                        for s, ks in ((0, k), (1, k - 1)):
                            if 0 <= ks < KD:
                                if ks == 0:
                                    pe.wait_ge(lo_made, U + s + 1)
                                mm = tile(s, ks, hhi[:, ks, :], hlo[:, ks, :], ks == KD - 1)
                                if ks == KD - 1:
                                    mm.then_inc(ffn_tile, 1)
                    for s in (2, 3):
                        if s == 2:
                            pe.wait_ge(h_done, J + H_CREDIT)
                        pe.wait_ge(lo_made, U + s + 1)
                        for k in range(KD):
                            mm = tile(s, k, hhi[:, k, :], hlo[:, k, :], k == KD - 1)
                        mm.then_inc(ffn_tile, 1)
                with pe.Fori(0 if third else 1, nj // 2) as it:
                    for s in range(4):
                        if s % 2 == 0:
                            if third:
                                pe.wait_ge(z_ev, z0 + KD * third - 2 + s)
                            pe.wait_ge(h_done, it * 2 + (J + s // 2 - 1 + H_CREDIT))
                        pe.wait_ge(lo_made, it * 4 + (U + s + 1))
                        for k in range(KD):
                            mm = tile(s, k, hhi[:, k, :], hlo[:, k, :], k == KD - 1)
                        mm.then_inc(ffn_tile, 1)
                U += 2 * nj
                with pe.Fori(0, 2) as it:
                    for s in range(4):
                        if s < 2:
                            pe.wait_ge(h_done, J + nj - 1 + s + H_CREDIT)
                        pe.wait_ge(z_ev, it * 4 + (z0 + KD * third + s - 3))
                        pe.wait_ge(lo_made, it * 4 + (U + s + 1))
                        for k in range(nj):
                            if s == 0:
                                pe.wait_ge(ulo_done, J + k + 1)
                            mm = tile(s, k, uhi[:, k, :], ulo[:, k, :], k == nj - 1)
                        mm.then_inc(ffn_tile, 1)
                U += KD
                J += nj

        pe.wait_ge(att_n, N_ATT)
        out_projection(0, lambda c, t: att[:, t, c * P:(c + 1) * P] if c < 4 else rg[:, t, (c - 4) * P:(c - 3) * P],
                       hx[:, 0], hx[:, 1], wsp_out0)
        ln_with_mod(0, KD, (1, 1), (0, 5))
        ffn(0)
        ln_with_mod(1, ZB[1], (1, 2), (1, 3))

        def m_chunk(f, k):
            w_hi, w_lo = (w[:, f % 2, k * P:(k + 1) * P] for w in (whi1, wlo1))
            return project(PS[f % 3], w_hi, w_lo, hT1[:, k, :], hlo1[:, k, :], k == 0, k == KD - 1,
                           ALL_SEGS if f >= 4 else ALL_SEGS[:1])

        pe.wait_ge(gate_w, 6)
        for k in range(KD + 2 * LAG):
            if k < KD:
                pe.wait_ge(input_lo, 2 * KD + k + 1)
                mm = project(PS[3], wg[:, 0, k, :], wg[:, 1, k, :], hT1[:, k, :], hlo1[:, k, :], k == 0, k == KD - 1, ALL_SEGS)
                if k == KD - 1:
                    mm.then_inc(gate_mm, 1)
            for f, kf in ((0, k - LAG), (1, k - 2 * LAG)):
                if 0 <= kf < KD:
                    if kf == 0:
                        split_unit("in1", f)
                    mm = m_chunk(f, kf)
                    if kf == KD - 1:
                        mm.then_inc(unit_done, 1)
        for f in range(2, 8):
            if f >= 3:
                pe.wait_ge(f_ev, f - 2)
            split_unit("in1", f)
            for k in range(KD):
                mm = m_chunk(f, k)
            mm.then_inc(unit_done, 1)
        in1_parts = ((whi1, wlo1), hT1, hlo1)
        token_major("in1", 8, [(t, t) for t in (4, 5, 0, 1, 2, 3)], *in1_parts, lambda b: pe.wait_ge(f_ev, (7, 8, 6)[b // 2]))
        v1 = {3: lambda: pe.wait_ge(gate_ev, 4), 0: lambda: pe.wait_ge(vg_ev, 1), 1: lambda: pe.wait_ge(vg_ev, 2)}
        token_major("in1", 12, [(0, 6), (1, 7), (2, 0), (3, 1), (4, 2), (5, 3)], *in1_parts, lambda b: v1[b // 2]())
        for k in range(KD):
            split_unit("in1", 16 + k)
            for b in (4, 5, 6, 7, 0, 1, 2, 3):
                if k == 0:
                    pe.wait_ge(vg_ev, {2: 3, 3: 4, 0: 5, 1: 6}[b // 2])
                cols, c0 = slice((b // 2) * P, (b // 2 + 1) * P), 512 * (b % 2)
                mm = three(half(b), ((hT1[:, k, cols], whi1[:, k % 2, c0:c0 + 512]), (hlo1[:, k, cols], wlo1[:, k % 2, c0:c0 + 512])),
                           k == 0, k == KD - 1)
            mm.then_inc(unit_done, 1)

        pe.wait_ge(vg_ev, 8)
        pe.wait_ge(rows_ok, 1)
        for d in range(2):
            for t in range(TT):
                at = (d * TT + t) * H_M
                pe.transpose(half(6)[:, at:at + H_M], li[0:H_M, d, t * P:(t + 1) * P], ident[0:H_M, 0:H_M])
        pe.wait_ge(floor_ok, 1)
        for d in range(2):
            for t in range(LT):
                at = (2 * TT + d * LT + t) * H_M
                mm = pe.transpose(half(6)[:, at:at + H_M], gbc[0:H_M, d, t * P:(t + 1) * P], ident[0:H_M, 0:H_M])
        mm.then_inc(tr_mm, 1)

        def m_scores(h):
            if h == 0:
                pe.wait_ge(vg_ev, 10)
                pe.wait_ge(silu_ev, 8)
            else:
                pe.wait_ge(mexp, 12 * h)
            for d in range(2):
                mm = pe.matmul(half(d), selr[0:H_M, h * P:(h + 1) * P], negm[0:H_M, d, :], start=True, stop=True)
            mm.then_inc(nm_mm, 1)
            b = M_DK * (h % 2)
            for j in range(TT):
                s = TT * h + j
                if s >= 4:
                    pe.wait_ge(mp_done, 2 * (s - 3))
                pe.matmul(half(2 + s % 4), mk[b:b + M_DK, h // 2, j * P:(j + 1) * P], mq[b:b + M_DK, h // 2, :],
                          start=True, stop=True).then_inc(ms_mm, 1)

        def m_values(h):
            pe.wait_ge(mp_done, 12 * (h + 1))
            for t in range(LT):
                i = LT * h + t
                if i >= 2:
                    pe.wait_ge(mh_ev, i - 1)
                else:
                    pe.wait_ge(tr_ev, 2)
                for d in range(2):
                    js = [j for j in range(TT) if j >= LT or (j <= t if d == 0 else j >= t)]
                    for j in js:
                        at = M_OFF[d][j] + t * P - m_range(j, d)[0]
                        mm = pe.matmul(half(6 + i % 2)[:, d * (M_DV + 1):(d + 1) * (M_DV + 1)],
                                       pp[:, h % 2, d, at:at + P], mv[:, j, h, :], start=(j == js[0]), stop=(j == js[-1]))
                mm.then_inc(mo_mm, 1)

        m_scores(0)
        for h in range(1, H_M):
            m_scores(h)
            m_values(h - 1)
        pe.wait_ge(mp_done, 2 * TT * H_M)
        mod_rows(1, 4, PS[2], 0, 2)
        m_values(H_M - 1)
        mod_rows(1, 4, PS[2], 2, KD)
        mod_columns(1, 4, PS[2])
        out_projection(1, lambda c, t: mo[:, t, c * P:(c + 1) * P], hT1, hlo_out1, wsp_out1)
        ln_with_mod(2, ZB[1] + KD, (1, 5))
        ffn(1)
        ln_sums(3)
        pe.wait_ge(ln_rstd, 4)
        for k in range(KD):
            pe.wait_ge(x_new, k + 1)
            for t in range(LT):
                mm = pe.transpose(PS[t][:, k * P:(k + 1) * P], xT[:, k, t * P:(t + 1) * P], ident)
                if k == KD - 1:
                    mm.then_inc(out_mm, 1)

    @block.scalar
    def _(act):
        steps = 0

        def step(ins):
            nonlocal steps
            steps += 1
            ins.then_inc(act_step, 1)
            act.wait_ge(act_step, steps)

        rows = [(c[0], V_C, 8), (c_ctx, V_CC, 8), (ln_g.rearrange("l s n -> (l s n)"), V_LG, 32),
                (ln_b.rearrange("l s n -> (l s n)"), V_LB, 32), (mla_q_norm[0], V_QN, KQ), (mla_kv_norm[0], V_KVN, KKV),
                (m_conv_w[0].rearrange("w n -> (w n)"), V_CW, 24), (m_conv_b[0], V_CB, 8), (m_norm_g[0], V_NG, 8)]
        act.dma_start(kc[:, :], consts[:, 0:K_BASE]).then_inc(consts_in, 16)
        for src, at, nr in rows:
            act.dma_start(vrow[at:at + nr, :], src.rearrange("(r n) -> r n", n=P)).then_inc(consts_in, 16)
        for l in range(DEPTH):
            act.dma_start(brow[48 * l:48 * l + 48, :], mod_b[l].rearrange("(r n) -> r n", n=P)).then_inc(consts_in, 16)
        act.dma_start(vrow[V_ROWS:P, :], consts[V_ROWS:P, 0:P]).then_inc(consts_in, 16)
        act.dma_start(xin[:, 0:LT, :], x[0].rearrange("(t p) n -> p t n", p=P)).then_inc(x_in, 16)
        act.dma_start(xin[:, LT:TT, :], ctx[0].rearrange("(t p) n -> p t n", p=P)).then_inc(x_in, 16)
        act.wait_ge(vec_ev, 1)
        act.activation(scol[:, :], vcol[:, V_C:V_C + 16], ACT.Silu).then_inc(scol_ok, 1)
        def split_high(stage, i, w_hi, width=UNIT):
            n = NB[stage] + i
            act.wait_ge(landed[n % RING], 16 * (n // RING + 1))
            if i >= 2:
                act.wait_ge(unit_done, UB[stage] + i - 1)
            act.activation(w_hi[:, i % 2, :], ring[:, n % RING, :], ACT.Copy).then_inc(hi_made, 1)

        def next_input(i, hi, raw, scale, bias, ready, first, split=None):
            segs = ALL_SEGS if i < 3 else SEGS[1]
            split_after = (6, 7) if i in (1, 2) else (0, 1)
            for k in range(KD):
                act.wait_ge(ready, first + k + 1)
                for a, b, v in segs:
                    ins = act.activation(raw[:, k, a:b], xT[:, k, a:b], ACT.Identity, bias=bias(k, v), scale=scale(k, v))
                ins.then_inc(input_full, 1)
                act.wait_ge(input_full, KD * i + k + 1)
                act.activation(hi[:, k, 0:b], raw[:, k, 0:b], ACT.Copy).then_inc(input_hi, 1)
                if split and k in split_after:
                    split(split_after.index(k))

        act.wait_ge(mod_ev, MOD_AT[0, 1])
        next_input(0, hx[:, 0], hx_raw[:, 1], lambda k, v: modc[:, 0, 1, k, v:v + 1], lambda k, v: modc[:, 0, 0, k, v:v + 1],
                   xT_ev, 0,
                   lambda i: split_high("in0", i, wsp_in0[:, 0]))

        def strips(h):
            b, lgf, lgb = h % 2, h, H_RET + h
            act.wait_ge(strip_in, 2 * h + 1)
            act.activation(strip[:, b, 0:REL_W], strip[:, b, 0:REL_W], ACT.Exp, scale=lgc[:, 0, lgf:lgf + 1])
            act.activation(strip[:, b, REL_W:], rel[:, 0:S2_W], ACT.Exp, scale=lgc[:, 0, lgf:lgf + 1], bias=lgc[:, 2, lgf:lgf + 1])
            act.activation(stripb, stripb, ACT.Exp, scale=lgc[:, 1, lgb:lgb + 1]).then_inc(strip_exp, 1)
            act.wait_ge(strip_in, 2 * h + 2)
            act.activation(stripb[:, 0:S2_W], rel[:, 0:S2_W], ACT.Exp, scale=lgc[:, 1, lgb:lgb + 1],
                           bias=lgc[:, 3, lgb:lgb + 1]).then_inc(strip_exp, 1)

        def inverse_rms(i, k):
            act.wait_ge(rms_mm, i + 1)
            act.activation(rms[:, i, :], PS[3][:, 0:T], ACT.Ln, scale=1.0 / (k * P), bias=epsc[:, :]).then_inc(rms_ln, 1)
            act.wait_ge(rms_ln, i + 1)
            act.activation(rms[:, i, :], rms[:, i, :], ACT.Exp, scale=-0.5).then_inc(rms_ready, 1)

        act.wait_ge(eps_ok, 1)
        for f in range(NF):
            split_high("in0", f + 2, wsp_in0[:, 0])
            src = PS[f % 3][:, 0:T]
            if f < 5:
                if f == 3:
                    act.wait_ge(rms_mm, 1)
                act.activation(sqb[:, f % 3, :], src, ACT.Square).then_inc(sq_made, 1)
                dst = cqkv[:, f, :]
            elif f == 5:
                src, dst = PS[f % 3][NOPE:DQ, 0:T], krope[NOPE:DQ, :]
            else:
                dst = rq[:, f - 6, :] if f < 10 else rk[:, f - 10, :]
            act.activation(dst, src, ACT.Copy).then_inc(ip_ev, 1)
            if f == 3:
                inverse_rms(0, KQ)
            if f == 5:
                inverse_rms(1, KKV)
        strips(0)
        split_high("in0", NF + 2, wsp_in0[:, 0])
        strips(1)
        for i in range(NF + 3, NF + 6):
            split_high("in0", i, wsp_in0[:, 0])
        for i in range(3):
            act.activation(rv[:, 2 * i:2 * i + 2, :], PS[i][:, :].rearrange("p (t d) -> p t d", t=2), ACT.Copy).then_inc(ip_ev, 1)
        for i in range(NF + 6, N_IN0):
            split_high("in0", i, wsp_in0[:, 0])
        act.wait_ge(unit_done, UB["in0"] + NF + 8)
        for i, b in enumerate((0, 1, 3)):
            act.activation(rg[:, 2 * i:2 * i + 2, :], PS[b][:, :].rearrange("p (t d) -> p t d", t=2), ACT.Silu).then_inc(rg_ready, 1)

        def ret_copy(h):
            act.wait_ge(ret_o, h + 1)
            for seg, (a, b) in enumerate(((0, LT), (LT, TT))):
                ins = act.activation(rv[:, a:b, h * RET_D:(h + 1) * RET_D],
                                     half(4 + 2 * (h % 2) + seg)[:, 0:(b - a) * P].rearrange("p (t d) -> p t d", d=P), ACT.Copy)
            ins.then_inc(ret_ev, 1)

        strips(2)
        ret_copy(0)
        strips(3)
        ret_copy(1)
        ret_copy(2)
        ret_copy(3)

        for m, (kind, i) in enumerate(MLA):
            if m == 3:
                act.wait_ge(ret_var, 1)
                step(act.activation(rrs[:, :], rmv[:, :, 1], ACT.Ln, bias=epsc[:, :]))
                act.activation(rrs[:, :], rrs[:, :], ACT.Exp, scale=-0.5).then_inc(ret_rstd, 1)
            act.wait_ge(mp_mm, m + 1)
            pair = mla_pair(m)
            if kind == "q_rope":
                ins = act.activation(qrope[:, i, :], pair[:, 0:T], ACT.Copy, scale=A_SCALE)
            elif kind == "values":
                ins = act.activation(va[:, 2 * i:2 * i + 2, :], pair[:, :].rearrange("p (t d) -> p t d", t=2), ACT.Copy)
            else:
                dst, scale = (qh, A_SCALE) if kind == "q_nope" else (kh, 1.0)
                for j in range(2):
                    ins = act.activation(dst[0:NOPE, 2 * i + j, :], pair[NOPE * j:NOPE * (j + 1), 0:T], ACT.Copy, scale=scale)
            ins.then_inc(mp_ev, 1)

        def att_exponent(it):
            act.wait_ge(att_nmx, it + 1)
            if it >= 2:
                act.wait_ge(att_t, it - 1)
            a = 0 if it % TT < LT else LAT
            act.activation(pa[:, it % 2, a:T], PS[it % 2][:, a:T], ACT.Exp, bias=nmx[:, it:it + 1],
                           accum_out=den[:, 0, it:it + 1]).then_inc(att_exp, 1)

        def att_copy(it):
            act.wait_ge(att_t, it + 1)
            if it >= 2:
                act.wait_ge(att_o, it - 1)
            act.activation(paT[:, it % 2, 0:LAT], PS[2][:, 0:LAT], ACT.Copy).then_inc(att_tA, 1)

        for i in range(N_ATT + 1):
            if i < N_ATT:
                att_exponent(i)
            if i >= 1 and (i - 1) % TT < LT:
                att_copy(i - 1)

        def ln_square(i, m):
            l = i // 2
            done = ZB[l] + (KD if i % 2 == 0 else 4 * KD) - KD + m + 1
            act.wait_ge(z_ev, done)
            if KD * i + m >= 2:
                act.wait_ge(ln_sum2, KD * i + m - 1)
            act.activation(sq[:, m % 2, 0:NT[l]], xT[:, m, 0:NT[l]], ACT.Square).then_inc(ln_sq, 1)

        def layer_norm(i):
            l, nt = i // 2, NT[i // 2]
            act.activation(lnr[:, 0:1], epsc[:, :], ACT.Ln)
            act.wait_ge(ln_mm, 2 * i + 1)
            act.activation(lnm[:, 0:nt], PS[0][:, 0:nt], ACT.Copy, scale=1.0 / D)
            act.activation(s1[:, 0:nt], PS[0][:, 0:nt], ACT.Square, scale=1.0 / D).then_inc(ln_mean, 1)
            act.wait_ge(ln_var, i + 1)
            step(act.activation(lnr[:, 0:nt], s2[:, 0:nt], ACT.Ln))
            act.activation(lnr[:, 0:nt], lnr[:, 0:nt], ACT.Exp, scale=-0.5).then_inc(ln_rstd, 1)

        def from_norm(i, hi, raw, split):
            act.wait_ge(gains_ok, i + 1)
            next_input(i + 1, hi, raw, lambda k, v: gain[:, i, 0, k, v:v + 1], lambda k, v: gain[:, i, 1, k, v:v + 1],
                       ln_norm, KD * i, split)

        def out_projection(l, hT, w_hi):
            nt = NT[l]
            split_high(f"out{l}", 0, w_hi)
            split_high(f"out{l}", 1, w_hi)
            for c in range(KD):
                act.wait_ge(oT_mm, KD * l + c + 1)
                if l == 0:
                    ins = act.activation(hT[:, c, 0:nt], op_pair(c)[:, 0:nt], ACT.Copy)
                else:
                    ins = act.activation(hT[:, c, 0:nt], op_pair(c)[:, 0:nt], ACT.Copy, scale=vcol[:, V_NG + c:V_NG + c + 1])
                ins.then_inc(oT_hi, 1)
            for m in range(KD):
                if m + 2 < KD:
                    split_high(f"out{l}", m + 2, w_hi)
                ln_square(2 * l, m)
            layer_norm(2 * l)

        def ffn(l):
            nt, first = NT[l], NB[f"ffn{l}"]

            def split(u, s, width, n_of):
                act.wait_ge(landed[(first + s) % RING], n_of)
                if not isinstance(u, int) or u - 3 + TILE_CREDIT > 0:
                    act.wait_ge(ffn_tile, u + (TILE_CREDIT - 3))
                act.activation(whi[:, s, 0:width], ring[:, (first + s) % RING, 0:width], ACT.Copy).then_inc(hi_made, 1)

            def split_static(v, width):
                split(FT[l] + v, v % 4, width, 16 * ((first + v) // RING + 1))

            from_norm(2 * l, hhi, hlo_raw, lambda v: split_static(v, UNIT))
            V, J = 0, JB[l]
            for third, (j0, nj) in enumerate(THIRDS):
                def silu(it, jj):
                    act.wait_ge(ffn_tile, it * 4 + (FT[l] + V + 2 * jj + 2 + TILE_CREDIT))
                    act.wait_ge(h_done, it * 2 + (J + jj - 1 + H_CREDIT))
                    act.activation(sg[:, jj, 0:nt], PS[2 * jj + 1][:, 0:nt], ACT.Silu).then_inc(silu_done, 1)

                def high(it, jj):
                    act.wait_ge(h_done, it * 2 + (J + jj + 1 + H_CREDIT))
                    j = it * 2 + jj
                    dst = uhi[:, j, 0:nt] if isinstance(it, int) else uhi[:, bass.ds(j, 1), 0:nt].rearrange("p a t -> p (a t)")
                    act.activation(dst, hu[:, jj, 0:nt], ACT.Copy).then_inc(uhi_done, 1)

                with act.Fori(0, nj // 2 - 1) as it:
                    for jj in range(2):
                        for q in range(2):
                            s = 2 * jj + q + 2
                            split(it * 4 + (FT[l] + V + s), s % 4, UNIT, it * 16 + 16 * ((first + V + s) // RING + 1))
                        silu(it, jj)
                        high(it, jj)
                last = nj // 2 - 1
                for jj in range(2):
                    for q in range(2):
                        v = V + 4 * last + 2 * jj + q + 2
                        split_static(v, UNIT if jj == 0 else nj * P)
                    silu(last, jj)
                    high(last, jj)
                V += 2 * nj
                for m in range(KD):
                    if m + 2 < KD:
                        split_static(V + m + 2, nj * P)
                    elif third < 2:
                        split_static(V + m + 2, UNIT)
                    if third == 2:
                        ln_square(2 * l + 1, m)
                V += KD
                J += nj
            layer_norm(2 * l + 1)

        out_projection(0, hx[:, 0], wsp_out0[:, 0])
        ffn(0)

        act.wait_ge(lo_made, SB["in1"])
        act.dma_start(wgr[:, :, :], m_w_in[0].rearrange("(k p) n -> p k n", p=P)[:, :, C_MG:C_MG + 4 * H_M]).then_inc(gate_in, 16)
        for g in range(4):
            act.dma_start(gb[32 * g:32 * g + H_M, :], m_gate_b[0, g].unsqueeze(1)).then_inc(gate_in, 16)
        act.dma_start(selr[:, :], consts[:, K_SEL:K_SEL + H_M * P]).then_inc(gate_in, 16)
        from_norm(1, hT1, hlo1_raw, lambda i: split_high("in1", i, whi1))
        act.wait_ge(gate_in, 16 * 6)
        split_high("in1", 2, whi1)
        act.wait_ge(gate_mm, 1)
        for g, dst in enumerate((li, gt, li, gt)):
            act.activation(dst[0:H_M, g // 2, :], PS[3][32 * g:32 * g + H_M, 0:T], ACT.Identity,
                           bias=gb[32 * g:32 * g + H_M, :]).then_inc(gate_ev, 1)

        def conv_in(f):
            if f >= 2:
                split_high("in1", f + 2, whi1)
            act.wait_ge(unit_done, UB["in1"] + f + 1)
            if f < 2:
                act.wait_ge(pad_ok, 4)
            else:
                act.wait_ge(conv_done, f - 1)
            ins = act.activation(cpad[:, f % 2, 1:1 + LAT], PS[f % 3][:, 0:LAT], ACT.Copy)
            if f >= 4:
                ins = act.activation(cpad[:, f % 2, LAT + 3:T + 3], PS[f % 3][:, LAT:T], ACT.Copy)
            ins.then_inc(f_ev, 1)

        def conv_out(f):
            act.wait_ge(conv_done, f + 1)
            bias = vcol[:, V_CB + f:V_CB + f + 1]
            if f < 4:
                act.activation(mq[:, f, :], cacc[:, f % 2, 0:LAT], ACT.Silu, bias=bias).then_inc(silu_ev, 1)
            else:
                act.activation(mk[:, f - 4, 0:LAT], cacc[:, f % 2, 0:LAT], ACT.Silu, bias=bias)
                act.activation(mk[:, f - 4, LAT:T], cacc[:, f % 2, LAT + 2:T + 2], ACT.Silu, bias=bias).then_inc(silu_ev, 1)

        conv_in(0)
        split_high("in1", 3, whi1)
        act.wait_ge(ls_in, 1)
        step(act.activation(lf[0:H_M, :, :], gbc[0:H_M, :, :], ACT.Exp))
        act.activation(lf[0:H_M, :, :], lf[0:H_M, :, :], ACT.Ln, bias=onec[0:H_M, :]).then_inc(ls_ln, 1)
        for f in range(1, 8):
            conv_in(f)
            if f >= 2:
                conv_out(f - 2)
        conv_out(6)
        conv_out(7)
        act.wait_ge(floor_in, 1)
        act.activation(gbc[0:H_M, :, 0:LAT], gbc[0:H_M, :, 0:LAT], ACT.Exp, scale=-1.0).then_inc(floor_ok, 1)
        pairs = ((0, 1, 2), (3, 0, 1))
        for g in range(2):
            for i in range(10 + 4 * g, 14 + 4 * g):
                split_high("in1", i, whi1)
            for i, b in enumerate(pairs[g]):
                for q in range(2):
                    ins = act.activation(mv[:, 2 * i + q, 4 * g:4 * g + 4, 0:M_DV],
                                         half(2 * b + q).rearrange("p (h d) -> p h d", h=4), ACT.Copy)
                ins.then_inc(vg_ev, 1)
        for i in range(18, N_IN1):
            split_high("in1", i, whi1)
        act.wait_ge(unit_done, UB["in1"] + N_IN1)
        for t in (2, 3, 0, 1):
            act.activation(mo[:, t, :], PS[t][:, :], ACT.Sigmoid).then_inc(vg_ev, 1)
        act.wait_ge(tr_ev, 1)

        def m_inverse_std(i):
            act.wait_ge(mvar, i + 1)
            cols = slice(LT * NORM_ENDS[i - 1] if i else 0, LT * NORM_ENDS[i])
            step(act.activation(mrs[:, cols], mmv[:, cols, 1], ACT.Ln, bias=epsc[:, :]))
            act.activation(mrs[:, cols], mrs[:, cols], ACT.Exp, scale=-0.5).then_inc(mrstd, 1)

        for h in range(H_M):
            if h - 1 in NORM_ENDS:
                m_inverse_std(NORM_ENDS.index(h - 1))
            act.wait_ge(nm_mm, h + 1)
            for j in range(TT):
                for d in range(2):
                    e = 2 * (TT * h + j) + d
                    if e >= 4:
                        act.wait_ge(mp_done, e - 3)
                    a, b = m_range(j, d)
                    act.activation(ee[:, e % 4, a:b], half(d)[:, a:b], ACT.Exp, bias=acol[:, d, j, h:h + 1]).then_inc(mexp, 1)
        m_inverse_std(len(NORM_ENDS) - 1)
        out_projection(1, hT1, wsp_out1[:, 0])
        ffn(1)
        for k in range(KD):
            act.wait_ge(ln_norm, KD * 3 + k + 1)
            g, b = V_LG + KD * 3 + k, V_LB + KD * 3 + k
            act.activation(xT[:, k, 0:LAT], xT[:, k, 0:LAT], ACT.Identity, bias=vcol[:, b:b + 1],
                           scale=vcol[:, g:g + 1]).then_inc(x_new, 1)
        for t in (0, 2):
            act.wait_ge(out_mm, t + 1)
            act.activation(orow[:, t, :], PS[t][:, :], ACT.Copy).then_inc(out_ev[t % 2], 1)

    @block.vector
    def _(dve):
        steps = 0

        def step(ins):
            nonlocal steps
            steps += 1
            ins.then_inc(dve_step, 1)
            dve.wait_ge(dve_step, steps)

        dve.sem_inc(h_done, H_CREDIT)
        dve.sem_inc(uhi_done, U_CREDIT)
        dve.memset(onec[:, :], 1.0)
        dve.memset(epsc[:, :], EPS).then_inc(eps_ok, 1)
        dve.wait_ge(vec_T, 1)
        dve.tensor_copy(vcol[:, 0:V_ROWS], half(1)[:, 0:V_ROWS]).then_inc(vec_ev, 1)
        dve.tensor_copy(modb[:, :], half(0)[:, 0:96])
        for k in range(KD):
            dve.wait_ge(xT_mm, k + 1)
            dve.tensor_copy(xT[:, k, :], PS[1 + k % 2][:, 0:T]).then_inc(xT_ev, 1)

        def mod_rows(l, g, pair):
            dve.wait_ge(unit_done, UB[f"mod{l}{g}"] + KD)
            for b in range(2):
                ins = dve.tensor_copy(mrow[:, 512 * b:512 * (b + 1)], pair[32 * b:32 * b + 2, 512 * b:512 * (b + 1)])
            ins.then_inc(mod_row, 1)

        def mod_columns(l, g, pair):
            dve.wait_ge(mod_T, MOD_AT[l, g])
            src = pair[:, 0:16].rearrange("p (b v) -> p v b", v=2)
            at = 48 * l + KD * g
            for v in range(2):
                dst = modc[:, l, g, :, :].rearrange("p b v -> p v b")[:, v, :]
                if g in (1, 4):
                    ins = dve.scalar_tensor_tensor(dst, src[:, v, :], 1.0, modb[:, at:at + KD], ALU.add, ALU.add)
                else:
                    ins = dve.tensor_tensor(dst, src[:, v, :], modb[:, at:at + KD], ALU.add)
            ins.then_inc(mod_ev, 1)

        mod_rows(0, 0, PS[3])
        mod_columns(0, 0, PS[3])
        mod_rows(0, 1, PS[0])
        mod_columns(0, 1, PS[0])
        def low_chunk(i, k, hi, lo, raw):
            n = T if i < 3 else LAT
            dve.wait_ge(input_hi, KD * i + k + 1)
            dve.tensor_tensor(lo[:, k, 0:n], raw[:, k, 0:n], hi[:, k, 0:n].bitcast(F32), ALU.subtract).then_inc(input_lo, 1)

        for k in range(KD):
            low_chunk(0, k, hx[:, 0], hx[:, 1], hx_raw[:, 1])

        def gains(i):
            l, g0 = ((0, 3), (1, 0), (1, 3))[i]
            for v in range(2):
                sc, sh = modc[:, l, g0 + 1, :, v], modc[:, l, g0, :, v]
                dve.tensor_tensor(gain[:, i, 0, :, v], sc, vcol[:, V_LG + KD * i:V_LG + KD * (i + 1)], ALU.mult)
                step(dve.tensor_tensor(gain[:, i, 1, :, v], sc, vcol[:, V_LB + KD * i:V_LB + KD * (i + 1)], ALU.mult))
                ins = dve.tensor_tensor(gain[:, i, 1, :, v], gain[:, i, 1, :, v], sh, ALU.add)
            ins.then_inc(gains_ok, 1)

        dve.tensor_scalar(again[:, :], vcol[:, V_LG:V_LG + 64], ALPHA, None, ALU.mult)
        dve.wait_ge(tabs_in, 16 * 4)
        for i, f in ((1, -1.0), (2, float(P)), (3, 640.0)):
            ins = dve.tensor_scalar(lgc[:, i, :], lgc[:, 0, :], f, None, ALU.mult)
        step(ins)
        for c in range(KQ + KKV):
            i = 0 if c < KQ else 1
            dve.wait_ge(rms_ready, i + 1)
            dve.scalar_tensor_tensor(cqkv[:, c, :], cqkv[:, c, :], vcol[:, V_QN + c:V_QN + c + 1], rms[:, i, :],
                                     ALU.mult, ALU.mult).then_inc(cq_norm, 1)

        def rope(r, bank, X, tab, tmp, lo, hi, mm, ev, done):
            dve.wait_ge(mm, r + 1)
            dve.tensor_tensor(tmp[lo:hi, :], bank[lo:hi, :], tab[lo:hi, 1, :], ALU.mult).then_inc(ev, 1)
            step(dve.tensor_tensor(X, X, tab[lo:hi, 0, :], ALU.mult))
            dve.tensor_tensor(X, X, tmp[lo:hi, :], ALU.add).then_inc(done, 1)

        rope(0, half(6), krope[NOPE:DQ, 0:LAT], cosM, rtmp, NOPE, DQ, rope_mm, rope_ev, rope_done)

        def rope_ret(r):
            X = rq[:, r - 1, 0:LAT] if r <= H_RET else rk[:, r - 1 - H_RET, 0:LAT]
            dve.wait_ge(rope_done, r)
            rope(r, half(6 + r % 2), X, cosR, rtmp, 0, P, rope_mm, rope_ev, rope_done)

        for r in range(1, 8):
            rope_ret(r)

        far = float(LAT - P)

        def strips_args(h):
            a = strip[:, h % 2, 0:REL_W]
            if h >= 2:
                dve.wait_ge(ret_p, 8 * (h - 1))
            dve.tensor_scalar(a, rel[:, :], -far, 0.0, ALU.add, ALU.max)
            dve.tensor_scalar(stripb, rel[:, :], -far, 0.0, ALU.add, ALU.min).then_inc(strip_in, 1)

        def strips_mask(h):
            a = strip[:, h % 2, 0:REL_W]
            dve.wait_ge(strip_exp, 2 * h + 1)
            dve.scalar_tensor_tensor(a, rel[:, :], far, a, ALU.is_ge, ALU.mult)
            step(dve.scalar_tensor_tensor(stripb, rel[:, :], far, stripb, ALU.is_le, ALU.mult))
            dve.tensor_tensor(a, a, stripb, ALU.add).then_inc(strip_in, 1)

        def strips_sum(h):
            dve.wait_ge(strip_exp, 2 * h + 2)
            step(dve.tensor_tensor(strip[:, h % 2, REL_W:], strip[:, h % 2, REL_W:], stripb[:, 0:S2_W], ALU.add))

        for h in range(2):
            strips_args(h)
            strips_mask(h)
            strips_sum(h)
        rope_ret(8)
        mod_rows(0, 3, PS[2])

        def ret_weigh(h):
            if h >= 2:
                dve.wait_ge(ret_o, h - 1)
            for i, (j, seg) in enumerate(RET_TILES):
                s = 8 * h + i
                dve.wait_ge(ret_s, s + 1)
                a, b, _ = ALL_SEGS[seg]
                w = b - a
                if seg == 0 and j >= LT:
                    c0 = REL_W + P * (TT - 1 - j)
                else:
                    c0 = (LAT - P) - P * (j - LT * seg)
                dve.scalar_tensor_tensor(pt[:, h % 2, ret_off(j, seg):ret_off(j, seg) + w], half(s % 4)[:, 0:w], R_SCALE,
                                         strip[:, h % 2, c0:c0 + w], ALU.mult, ALU.mult).then_inc(ret_p, 1)

        dve.wait_ge(rg_ready, 3)
        ret_weigh(0)
        strips_args(2)
        mod_columns(0, 3, PS[2])
        ret_weigh(1)
        strips_mask(2)
        strips_sum(2)
        strips_args(3)
        ret_weigh(2)
        strips_mask(3)
        strips_sum(3)
        ret_weigh(3)
        for h in range(H_RET):
            dve.wait_ge(ret_ev, h + 1)
            for t in range(TT):
                ins = dve.bn_stats(rst[:, h * TT + t, :], rv[:, t, h * RET_D:(h + 1) * RET_D])
            if h == 2:
                mod_rows(0, 4, PS[1])
        step(ins)
        for i in range(H_RET * TT):
            ins = dve.bn_aggr(rmv[:, i, :], rst[:, i, :])
        ins.then_inc(ret_var, 1)
        mod_columns(0, 4, PS[1])
        dve.wait_ge(mod_ev, MOD_AT[0, 4])
        gains(0)

        def ret_norm(first, count):
            items = [(i, rg[:, i % TT, (i // TT) * P:(i // TT + 1) * P], rv[:, i % TT, (i // TT) * P:(i // TT + 1) * P])
                     for i in range(first, first + count)]
            for i, gate, o in items:
                ins = dve.scalar_tensor_tensor(gate, o, rmv[:, i, 0:1], gate, ALU.subtract, ALU.mult)
            step(ins)
            for i, gate, o in items:
                ins = dve.tensor_scalar(gate, gate, rrs[:, i:i + 1], None, ALU.mult)

        for g in range(H_MLA // QG):
            rope(g, half(6 + g), qrope[:, g, 0:LAT], cosM, mtmp, 0, P, mrope_mm, mrope_ev, mrope_done)
            dve.wait_ge(mrope_done, g + 1)
        dve.wait_ge(ret_rstd, 1)
        for h in range(H_MLA):
            at = ROPE * (h % QG)
            dve.tensor_copy(qh[NOPE:DQ, h, :], qrope[at:at + ROPE, h // QG, :]).then_inc(qr_cp, 1)
            ret_norm(3 * h, 3)
        mod_rows(0, 2, PS[3])
        mod_columns(0, 2, PS[3])

        def att_max(it):
            dve.wait_ge(att_s, it + 1)
            a = 0 if it % TT < LT else LAT
            dve.tensor_reduce(nmx[:, it:it + 1], PS[it % 2][:, a:T], AX.X, ALU.max, negate=True).then_inc(att_nmx, 1)

        def att_copy(it):
            dve.wait_ge(att_t, it + 1)
            if it >= 2:
                dve.wait_ge(att_o, it - 1)
            dve.tensor_copy(paT[:, it % 2, LAT:T], PS[2][:, LAT:T]).then_inc(att_tB, 1)

        def att_norm(it):
            h, t = divmod(it, TT)
            dve.wait_ge(att_o, it + 1)
            step(dve.reciprocal(den[:, 1, it:it + 1], den[:, 0, it:it + 1]))
            dve.tensor_scalar(att[:, t, h * MLA_V:(h + 1) * MLA_V], half(6 + it % 2)[:, 0:MLA_V], den[:, 1, it:it + 1],
                              None, ALU.mult).then_inc(att_n, 1)

        for i in range(N_ATT + 2):
            if i < N_ATT:
                att_max(i)
            if 1 <= i <= N_ATT:
                att_copy(i - 1)
            if i >= 2:
                att_norm(i - 2)

        mod_rows(1, 0, PS[0])
        mod_columns(1, 0, PS[0])

        def z_update(l, g, m, pair):
            for a, b, v in SEGS[l]:
                ins = dve.scalar_tensor_tensor(xT[:, m, a:b], pair[:, a:b], modc[:, l, g, m, v:v + 1], xT[:, m, a:b],
                                               ALU.mult, ALU.add)
            ins.then_inc(z_ev, 1)

        def ln_sum(i, m, z):
            nt = NT[i // 2]
            dve.wait_ge(z_ev, z)
            if m == 0:
                ins = dve.tensor_copy(s1[:, 0:nt], xT[:, m, 0:nt])
            else:
                ins = dve.tensor_tensor(s1[:, 0:nt], s1[:, 0:nt], xT[:, m, 0:nt], ALU.add)
            if m == KD - 1:
                ins.then_inc(ln_sum1, 1)
            else:
                step(ins)

        def layer_norm(i, parts=None, mod=None, mod2=None):
            nt = NT[i // 2]
            dve.wait_ge(ln_mm, 2 * i + 2)
            dve.wait_ge(ln_mean, i + 1)
            step(dve.scalar_tensor_tensor(s2[:, 0:nt], PS[1][:, 0:nt], 1.0 / D, s1[:, 0:nt], ALU.mult, ALU.subtract))
            dve.tensor_scalar(s2[:, 0:nt], s2[:, 0:nt], 0.0, EPS, ALU.max, ALU.add).then_inc(ln_var, 1)

            def centre(k):
                dve.tensor_tensor(xT[:, k, 0:nt], xT[:, k, 0:nt], lnm[:, 0:nt], ALU.subtract).then_inc(ln_sub, 1)

            for k in range(LEAD):
                centre(k)
            dve.wait_ge(ln_rstd, i + 1)
            for k in range(KD):
                if k < SUB_DVE:
                    dve.wait_ge(ln_sub, SUB_DVE * i + k + 1)
                else:
                    dve.wait_ge(ln_subp, (KD - SUB_DVE) * i + k - SUB_DVE + 1)
                dve.tensor_tensor(xT[:, k, 0:nt], xT[:, k, 0:nt], lnr[:, 0:nt], ALU.mult).then_inc(ln_norm, 1)
                if k + LEAD < SUB_DVE:
                    centre(k + LEAD)
                if parts and k >= 2:
                    low_chunk(i + 1, k - 2, *parts)
                if mod and k == 2:
                    mod_rows(*mod, PS[2])
                if mod and k == 6:
                    mod_columns(*mod, PS[2])
            if parts:
                if mod2:
                    mod_rows(*mod2, PS[3])
                low_chunk(i + 1, KD - 2, *parts)
                if mod2:
                    mod_columns(*mod2, PS[3])
                low_chunk(i + 1, KD - 1, *parts)

        def out_projection(l, in_hi, in_lo):
            nt = NT[l]
            for c in range(KD):
                dve.wait_ge(oT_hi, KD * l + c + 1)
                hi = in_hi[:, c, 0:nt].bitcast(F32)
                if l == 0:
                    ins = dve.tensor_tensor(in_lo[:, c, 0:nt], op_pair(c)[:, 0:nt], hi, ALU.subtract)
                else:
                    ins = dve.scalar_tensor_tensor(in_lo[:, c, 0:nt], op_pair(c)[:, 0:nt], vcol[:, V_NG + c:V_NG + c + 1], hi,
                                                   ALU.mult, ALU.subtract)
                ins.then_inc(oT_ev, 1)
            for m in range(KD):
                dve.wait_ge(unit_done, UB[f"out{l}"] + m + 1)
                dve.wait_ge(xa_done, KD * 2 * l + m + 1)
                z_update(l, 2, m, op_pair(m))
                if m >= 1:
                    ln_sum(2 * l, m - 1, ZB[l] + m)
            ln_sum(2 * l, KD - 1, ZB[l] + KD)
            layer_norm(2 * l, (hhi, hlo, hlo_raw), ((1, 1), (1, 5))[l], ((0, 5), None)[l])

        def ffn(l):
            nt = NT[l]
            if l == 0:
                dve.wait_ge(mod_ev, MOD_AT[0, 5])
                gains(1)
            V, J, z0 = 0, JB[l], ZB[l] + KD
            for third, (j0, nj) in enumerate(THIRDS):
                with dve.Fori(0, nj // 2) as it:
                    for jj in range(2):
                        dve.wait_ge(silu_done, it * 2 + (J + jj + 1))
                        dve.wait_ge(uhi_done, it * 2 + (J + jj - 1 + U_CREDIT))
                        dve.tensor_tensor(hu[:, jj, 0:nt], sg[:, jj, 0:nt], PS[2 * jj][:, 0:nt], ALU.mult).then_inc(h_done, 1)
                        dve.wait_ge(uhi_done, it * 2 + (J + jj + 1 + U_CREDIT))
                        j = it * 2 + jj
                        hi = uhi[:, bass.ds(j, 1), 0:nt].rearrange("p a t -> p (a t)")
                        lo = ulo[:, bass.ds(j, 1), 0:nt].rearrange("p a t -> p (a t)")
                        dve.tensor_tensor(lo, hu[:, jj, 0:nt], hi.bitcast(F32), ALU.subtract).then_inc(ulo_done, 1)
                V += 2 * nj
                for m in range(KD):
                    dve.wait_ge(ffn_tile, FT[l] + V + m + 1 + TILE_CREDIT)
                    if third == 0:
                        dve.wait_ge(xa_done, KD * (2 * l + 1) + m + 1)
                    else:
                        dve.wait_ge(z_ev, z0 + KD * (third - 1) + m + 1)
                    z_update(l, 5, m, PS[m % 4])
                    if third == 2 and m >= 1:
                        ln_sum(2 * l + 1, m - 1, z0 + 2 * KD + m)
                V += KD
                J += nj
            ln_sum(2 * l + 1, KD - 1, z0 + 3 * KD)
            if l == 0:
                layer_norm(1, (hT1, hlo1, hlo1_raw), (1, 2), (1, 3))
            else:
                layer_norm(3)

        out_projection(0, hx[:, 0], hx[:, 1])
        ffn(0)

        dve.wait_ge(gate_ev, 4)
        z_, g_, b_ = gt[0:H_M, :, :], gbc[0:H_M, :, :], lf[0:H_M, :, :]
        dve.scalar_tensor_tensor(g_, z_, -1.0, z_, ALU.mult, ALU.min).then_inc(ls_in, 1)

        def conv(f):
            w = LAT if f < 4 else T + 2
            dve.wait_ge(f_ev, f + 1)
            if f >= 2:
                dve.wait_ge(silu_ev, f - 1)
            y = cacc[:, f % 2, 0:w]

            def tap(i):
                return vcol[:, V_CW + 8 * i + f:V_CW + 8 * i + f + 1]

            step(dve.tensor_scalar(y, cpad[:, f % 2, 1:1 + w], tap(1), None, ALU.mult))
            step(dve.scalar_tensor_tensor(y, cpad[:, f % 2, 0:w], tap(0), y, ALU.mult, ALU.add))
            dve.scalar_tensor_tensor(y, cpad[:, f % 2, 2:2 + w], tap(2), y, ALU.mult, ALU.add).then_inc(conv_done, 1)

        dve.wait_ge(ls_ln, 1)
        step(dve.scalar_tensor_tensor(b_, z_, 0.0, b_, ALU.min, ALU.subtract))

        def scan(dst, src, d, op, init):
            for a, b in ((LAT, T), (0, LAT)):
                sl = slice(a, b) if d == 0 else slice(b - 1, a - 1 if a else None, -1)
                step(dve.tensor_tensor_scan(dst[0:H_M, d, sl], src[0:H_M, d, sl], src[0:H_M, d, sl], init, op, ALU.bypass))
                last = T - 1 if d == 0 else LAT
                init = dst[0:H_M, d, last:last + 1]

        conv(0)
        for d in range(2):
            scan(gbc, lf, d, ALU.add, 0.0)
        conv(1)
        step(dve.tensor_tensor(li[0:H_M, :, :], li[0:H_M, :, :], g_, ALU.subtract))
        for d in range(2):
            scan(gt, li, d, ALU.max, 0.0)
        conv(2)
        dve.tensor_scalar(negm[0:H_M, :, :], gt[0:H_M, :, 0:LAT], -1.0, None, ALU.mult).then_inc(rows_ok, 1)
        dve.tensor_tensor(gbc[0:H_M, :, 0:LAT], gbc[0:H_M, :, 0:LAT], gt[0:H_M, :, 0:LAT], ALU.add).then_inc(floor_in, 1)
        for f in range(3, 8):
            conv(f)
        dve.wait_ge(tr_mm, 1)
        dve.tensor_copy(acol[:, :, :, :], half(6)[:, 0:2 * TT * H_M].rearrange("p (d t h) -> p d t h", d=2, t=TT)).then_inc(tr_ev, 1)
        dve.tensor_copy(fcol[:, :, :, :], half(6)[:, 2 * TT * H_M:2 * (TT + LT) * H_M].rearrange("p (d t h) -> p d t h", d=2, t=LT)).then_inc(tr_ev, 1)

        def m_weigh(h):
            if h >= 2:
                dve.wait_ge(mo_mm, LT * (h - 1))
            for j in range(TT):
                for d in range(2):
                    s = TT * h + j
                    e = 2 * s + d
                    dve.wait_ge(ms_mm, s + 1)
                    if j < LT:
                        dve.wait_ge(msel, 2 * LT * h + 2 * j + d + 1)
                    else:
                        dve.wait_ge(mexp, e + 1)
                    a, b = m_range(j, d)
                    at = M_OFF[d][j]
                    dve.scalar_tensor_tensor(pp[:, h % 2, d, at:at + b - a], half(2 + s % 4)[:, a:b], M_SCALE,
                                             ee[:, e % 4, a:b], ALU.mult, ALU.mult).then_inc(mp_done, 1)

        def m_divide(h):
            for t in range(LT):
                i = LT * h + t
                dve.wait_ge(mo_mm, i + 1)
                o = half(6 + i % 2)[:, 0:2 * (M_DV + 1)].rearrange("p (d v) -> p d v", d=2)
                dd = dab[:, i % 2, t, :]
                step(dve.scalar_tensor_tensor(dd, o[:, :, M_DV], -1.0, fcol[:, :, t, h], ALU.mult, ALU.max))
                step(dve.tensor_tensor(dd, dd, o[:, :, M_DV], ALU.max))
                step(dve.reciprocal(dd, dd))
                step(dve.tensor_scalar(hf[:, i % 2, :], o[:, 0, 0:M_DV], dd[:, 0:1], None, ALU.mult))
                dst = hb[:, t, h * M_DV:(h + 1) * M_DV]
                dve.scalar_tensor_tensor(dst, o[:, 1, 0:M_DV], dd[:, 1:2], hf[:, i % 2, :], ALU.mult, ALU.add).then_inc(mh_ev, 1)
            dve.wait_ge(mh_ev, LT * (h + 1))
            for t in range(LT):
                ins = dve.bn_stats(mst[:, h * LT + t, :], hb[:, t, h * M_DV:(h + 1) * M_DV])
            step(ins)
            for t in range(LT):
                ins = dve.bn_aggr(mmv[:, h * LT + t, :], mst[:, h * LT + t, :])
            if h + 1 in NORM_ENDS:
                ins.then_inc(mvar, 1)

        def m_norm(i):
            dve.wait_ge(mrstd, i + 1)
            heads = range(NORM_ENDS[i - 1] if i else 0, NORM_ENDS[i])
            for h in heads:
                for t in range(LT):
                    j = h * LT + t
                    dst = hb[:, t, h * M_DV:(h + 1) * M_DV]
                    ins = dve.tensor_scalar(dst, dst, mmv[:, j, 0:1], mrs[:, j:j + 1], ALU.subtract, ALU.mult)
            step(ins)
            cols = slice(heads[0] * M_DV, NORM_ENDS[i] * M_DV)
            dve.tensor_tensor(mo[:, :, cols], mo[:, :, cols], hb[:, :, cols], ALU.mult).then_inc(mn_done, 1)

        dve.wait_ge(vg_ev, 10)
        m_weigh(0)
        for h in range(1, H_M):
            m_weigh(h)
            m_divide(h - 1)
            if h - 1 in NORM_ENDS:
                m_norm(NORM_ENDS.index(h - 1))
        m_divide(H_M - 1)
        m_norm(len(NORM_ENDS) - 1)
        mod_rows(1, 4, PS[2])
        mod_columns(1, 4, PS[2])
        dve.wait_ge(mod_ev, MOD_AT[1, 4])
        gains(2)
        out_projection(1, hT1, hlo_out1)
        ffn(1)
        for t in (1, 3):
            dve.wait_ge(out_mm, t + 1)
            dve.tensor_copy(orow[:, t, :], PS[t][:, :]).then_inc(out_ev[t % 2], 1)

    @block.gpsimd
    def _(pool):
        def scale_chunk(k):
            pool.wait_ge(input_full, k + 1)
            pool.tensor_scalar(xT[:, k, 0:T], xT[:, k, 0:T], ALPHA, None, ALU.mult).then_inc(xa_done, 1)

        def residual_chunk(i, k):
            nt = NT[(i + 1) // 2]
            pool.wait_ge(input_full, KD * (i + 1) + k + 1)
            pool.tensor_scalar(xT[:, k, 0:nt], xT[:, k, 0:nt], again[:, KD * i + k:KD * i + k + 1],
                               again[:, 32 + KD * i + k:32 + KD * i + k + 1], ALU.mult, ALU.add).then_inc(xa_done, 1)

        def layer_norm(i):
            nt = NT[i // 2]
            pool.wait_ge(ln_mean, i + 1)
            for k in range(SUB_DVE, KD):
                pool.tensor_tensor(xT[:, k, 0:nt], xT[:, k, 0:nt], lnm[:, 0:nt], ALU.subtract).then_inc(ln_subp, 1)

        def split_low(stage, i, w_hi, w_lo):
            n = NB[stage] + i
            pool.wait_ge(hi_made, SB[stage] + i + 1)
            pool.tensor_tensor(w_lo[:, i % 2, :], ring[:, n % RING, :], w_hi[:, i % 2, :].bitcast(F32),
                               ALU.subtract).then_inc(lo_made, 1)

        def out_projection(l, wsp):
            split_low(f"out{l}", 0, wsp[:, 0], wsp[:, 1])
            split_low(f"out{l}", 1, wsp[:, 0], wsp[:, 1])
            for m in range(KD):
                if m + 2 < KD:
                    split_low(f"out{l}", m + 2, wsp[:, 0], wsp[:, 1])
                ln_sum(2 * l, m)
            layer_norm(2 * l)

        def ln_sum(i, m):
            nt = NT[i // 2]
            pool.wait_ge(ln_sq, KD * i + m + 1)
            if m == 0:
                pool.tensor_copy(s2[:, 0:nt], sq[:, 0, 0:nt]).then_inc(ln_sum2, 1)
            else:
                pool.wait_ge(ln_sum2, KD * i + m)
                pool.tensor_tensor(s2[:, 0:nt], s2[:, 0:nt], sq[:, m % 2, 0:nt], ALU.add).then_inc(ln_sum2, 1)

        def ffn(l):
            def low(u, s, width):
                pool.wait_ge(hi_made, u)
                pool.tensor_tensor(wlo[:, s, 0:width], ring[:, (NB[f"ffn{l}"] + s) % RING, 0:width],
                                   whi[:, s, 0:width].bitcast(F32), ALU.subtract).then_inc(lo_made, 1)

            full = sum(2 * nj + KD for _, nj in THIRDS[:2]) + 2 * THIRDS[2][1]
            for v in range(KD):
                low(FB[l] + v + 1, v % 4, UNIT)
                residual_chunk(2 * l, v)
            with pool.Fori(KD // 4, full // 4) as it:
                for s in range(4):
                    low(it * 4 + (FB[l] + s + 1), s, UNIT)
            w = THIRDS[2][1] * P
            low(FB[l] + full + 1, 0, w)
            low(FB[l] + full + 2, 1, w)
            for m in range(KD):
                if m + 2 < KD:
                    low(FB[l] + full + m + 3, (m + 2) % 4, w)
                ln_sum(2 * l + 1, m)
            layer_norm(2 * l + 1)

        for i in range(N_IN0):
            split_low("in0", i, wsp_in0[:, 0], wsp_in0[:, 1])
            if 2 <= i < 2 + KD:
                scale_chunk(i - 2)
        pool.wait_ge(xa_done, KD)
        pool.wait_ge(rope_done, 1)
        pool.wait_ge(ret_o, H_RET)
        for h in range(H_MLA):
            pool.tensor_copy(kh[NOPE:DQ, h, :], krope[NOPE:DQ, :]).then_inc(kr_cp, 1)
        out_projection(0, wsp_out0)
        ffn(0)
        pool.wait_ge(gate_in, 16 * 6)
        pool.memset(wgf[:, :, :], 0.0).then_inc(pool_step, 1)
        pool.wait_ge(pool_step, 1)
        for g in range(4):
            pool.tensor_copy(wgf[:, :, 32 * g:32 * g + H_M], wgr[:, :, H_M * g:H_M * (g + 1)]).then_inc(gate_w, 1)
        pool.wait_ge(gate_w, 4)
        pool.tensor_copy(wg[:, 0, :, :], wgf[:, :, :]).then_inc(gate_w, 1)
        pool.wait_ge(gate_w, 5)
        pool.tensor_tensor(wg[:, 1, :, :], wgf[:, :, :], wg[:, 0, :, :].bitcast(F32), ALU.subtract).then_inc(gate_w, 1)
        split_low("in1", 0, whi1, wlo1)
        split_low("in1", 1, whi1, wlo1)
        for s in range(2):
            pool.memset(cpad[:, s, 0:1], 0.0)
            pool.memset(cpad[:, s, LAT + 1:LAT + 3], 0.0).then_inc(pad_ok, 1)
            pool.memset(cpad[:, s, T + 3:T + 4], 0.0).then_inc(pad_ok, 1)
        for i in range(2, N_IN1):
            split_low("in1", i, whi1, wlo1)
            if i == 3:
                pool.wait_ge(gate_mm, 1)
                pool.memset(mv[:, :, :, M_DV:M_DV + 1], 1.0).then_inc(ones_ok, 1)
            elif 4 <= i < 4 + KD:
                residual_chunk(1, i - 4)
        for h in range(H_M):
            for j in range(LT):
                for d in range(2):
                    e = 2 * (TT * h + j) + d
                    pool.wait_ge(mexp, e + 1)
                    blk = ee[:, e % 4, j * P:(j + 1) * P]
                    sign = 1 if d == 0 else -1
                    pool.affine_select(out=blk, in_=blk, pattern=[[sign, P]], compare_op=ALU.is_ge, fill=0.0, base=0,
                                       channel_multiplier=-sign).then_inc(msel, 1)
        out_projection(1, wsp_out1)
        ffn(1)

    es.close()


_INS = ['x', 'c', 'ctx', 'c_ctx', 'mod_w', 'mod_b', 'ln_g', 'ln_b', 'ffn_w_in', 'ffn_w_out', 'ab_w_in', 'mla_q_norm',
        'mla_w_uq', 'mla_kv_norm', 'mla_w_ukv', 'ret_log_decay', 'ab_w_out', 'm_w_in', 'm_conv_w', 'm_conv_b',
        'm_gate_b', 'm_norm_g', 'm_w_out']


def kernel(**inputs):
    import concourse.bacc as _bacc
    from concourse.bass_utils import run_bass_kernel_spmd as _run

    nc = _bacc.Bacc("TRN2", target_bir_lowering=False, num_devices=1)
    arrays, args = {}, []
    for name in _INS:
        a = np.ascontiguousarray(inputs[name])
        arrays[f"in_{name}"] = a
        args.append(nc.dram_tensor(f"in_{name}", a.shape, mybir.dt.from_np(a.dtype), kind="ExternalInput").ap())
    k = shape_constants()
    arrays["in_consts"] = k
    args.append(nc.dram_tensor("in_consts", k.shape, F32, kind="ExternalInput").ap())
    args.append(nc.dram_tensor("out", (1, LAT, D), F32, kind="ExternalOutput").ap())
    build(nc, *args)
    r = _run(nc, [arrays], core_ids=[0])
    return r.results[0]["out"]
```
